# Optimizing a Trainium2 kernel written in Bass

```python
import math
import jax
import jax.numpy as jnp
from jax import lax
import numpy as np
import jax, jax.numpy as jnp

D_MODEL = 1024
BATCH = 1
SEQ = 512
DEPTH = 2

GRID_W = 64
CTX_LEN = 256
HEAD_DIM = 64
MIX_WIDTH = D_MODEL
GROUP_WIDTH = MIX_WIDTH // 2
N_Q_HEADS = GROUP_WIDTH // HEAD_DIM
N_KV_HEADS = N_Q_HEADS // 4
KV_WIDTH = N_KV_HEADS * HEAD_DIM
HYENA_WIDTH = GROUP_WIDTH
HYENA_ORDER = 2
HYENA_SHORT_CONV = 3
HYENA_EMB = 33
HYENA_HIDDEN = 64
HYENA_DECAY_TARGET = 1e-2
HYENA_SHORT_DECAY_PCT = 0.3
HYENA_LONG_DECAY_PCT = 1.5
Q_BLOCK = 128
WINDOW = 128
NA_ROWS = 8
NA_COLS = 16
ROPE_THETA = 10000.0
EPS = 1e-6
NEG_INF = -1e30
N_EVEN = (DEPTH + 1) // 2
N_ODD = DEPTH // 2
EVEN_SPLITS = (GROUP_WIDTH, KV_WIDTH, KV_WIDTH, (HYENA_ORDER + 1) * HYENA_WIDTH, GROUP_WIDTH, HYENA_WIDTH)
ODD_SPLITS = (GROUP_WIDTH, KV_WIDTH, KV_WIDTH, GROUP_WIDTH, GROUP_WIDTH, GROUP_WIDTH, GROUP_WIDTH, GROUP_WIDTH)
IN_WIDTH = sum(EVEN_SPLITS)


def rms_norm(x, g):
    xf = x.astype(jnp.float32)
    y = xf * lax.rsqrt(jnp.mean(xf * xf, axis=-1, keepdims=True) + EPS)
    return (y * g.astype(jnp.float32)).astype(x.dtype)

def adaln(cond, w, b):
    m = jnp.matmul(jax.nn.silu(cond), w) + b
    return jnp.split(m, 3, axis=-1)

def modulated_norm(x, g, shift, scale):
    return rms_norm(x, g) * (1 + scale) + shift

def split_cols(p, sizes):
    idx = [int(v) for v in np.cumsum(sizes)[:-1]]
    return jnp.split(p, idx, axis=-1)

def heads(t, n):
    return t.reshape(t.shape[0], t.shape[1], n, HEAD_DIM)

def axial_rope_tables(n_tokens):
    t = jnp.arange(n_tokens, dtype=jnp.int32)
    row = (t // GRID_W).astype(jnp.float32)
    col = (t % GRID_W).astype(jnp.float32)
    n_pairs = HEAD_DIM // 4
    inv = ROPE_THETA ** (-jnp.arange(n_pairs, dtype=jnp.float32) / n_pairs)
    ang = jnp.concatenate([row[:, None] * inv, col[:, None] * inv], axis=-1)
    return jnp.cos(ang), jnp.sin(ang)

def apply_rope(x, cos, sin):
    b, n, h, dh = x.shape
    xf = x.astype(jnp.float32).reshape(b, n, h, dh // 2, 2)
    x0, x1 = xf[..., 0], xf[..., 1]
    cs, sn = cos[None, :, None, :], sin[None, :, None, :]
    out = jnp.stack([x0 * cs - x1 * sn, x0 * sn + x1 * cs], axis=-1)
    return out.reshape(b, n, h, dh).astype(x.dtype)

def context_attention(q_ctx, k_ctx, v_ctx, sink_logit=None):
    b, n, h, dh = q_ctx.shape
    kv = k_ctx.shape[2]
    g = h // kv
    qg = q_ctx.reshape(b, n, kv, g, dh)
    sc = jnp.einsum('bqkgd,bckd->bkgqc', qg, k_ctx).astype(jnp.float32) * dh ** -0.5
    if sink_logit is not None:
        sink = jnp.broadcast_to(sink_logit.astype(jnp.float32).reshape(1, kv, g, 1, 1), sc.shape[:-1] + (1,))
        p = jax.nn.softmax(jnp.concatenate([sc, sink], axis=-1), axis=-1)[..., :-1]
    else:
        p = jax.nn.softmax(sc, axis=-1)
    o = jnp.einsum('bkgqc,bckd->bqkgd', p.astype(v_ctx.dtype), v_ctx)
    return o.reshape(b, n, h * dh)

def global_gqa(q, k, v, k_ctx, v_ctx):
    b, s, h, dh = q.shape
    kv = k.shape[2]
    g = h // kv
    nb = s // Q_BLOCK
    k_all = jnp.concatenate([k_ctx, k], axis=1)
    v_all = jnp.concatenate([v_ctx, v], axis=1)
    scale = dh ** -0.5
    qb = q.reshape(b, nb, Q_BLOCK, kv, g, dh).swapaxes(0, 1)

    def one_block(q_blk):
        sc = jnp.einsum('bqkgd,bnkd->bkgqn', q_blk, k_all).astype(jnp.float32) * scale
        p = jax.nn.softmax(sc, axis=-1).astype(v_all.dtype)
        return jnp.einsum('bkgqn,bnkd->bqkgd', p, v_all)

    o = lax.map(one_block, qb)
    return o.swapaxes(0, 1).reshape(b, s, h * dh)

def windowed_gqa(q, k, v, k_ctx, v_ctx, sink_logit):
    b, s, h, dh = q.shape
    kv = k.shape[2]
    g = h // kv
    nb = s // Q_BLOCK
    side = WINDOW // Q_BLOCK
    span = (2 * side + 1) * Q_BLOCK
    n_ctx = k_ctx.shape[1]
    pad = ((0, 0), (side * Q_BLOCK, side * Q_BLOCK), (0, 0), (0, 0))
    kp = jnp.pad(k, pad).reshape(b, nb + 2 * side, Q_BLOCK, kv, dh)
    vp = jnp.pad(v, pad).reshape(b, nb + 2 * side, Q_BLOCK, kv, dh)
    kb = jnp.concatenate([kp[:, j:j + nb] for j in range(2 * side + 1)], axis=2)
    vb = jnp.concatenate([vp[:, j:j + nb] for j in range(2 * side + 1)], axis=2)
    qb = q.reshape(b, nb, Q_BLOCK, kv, g, dh)
    a = jnp.arange(Q_BLOCK)[:, None]
    j = jnp.arange(span)[None, :]
    band = jnp.abs(j - side * Q_BLOCK - a) <= WINDOW
    kpos = jnp.arange(nb)[:, None] * Q_BLOCK - side * Q_BLOCK + jnp.arange(span)[None, :]
    valid = band[None] & ((kpos >= 0) & (kpos < s))[:, None, :]
    sink = sink_logit.astype(jnp.float32).reshape(kv, g, 1, 1)
    scale = dh ** -0.5

    def one_block(args):
        q_blk, k_blk, v_blk, m = args
        s_loc = jnp.einsum('bqkgd,bjkd->bkgqj', q_blk, k_blk).astype(jnp.float32) * scale
        s_loc = jnp.where(m, s_loc, NEG_INF)
        s_ctx = jnp.einsum('bqkgd,bckd->bkgqc', q_blk, k_ctx).astype(jnp.float32) * scale
        s_sink = jnp.broadcast_to(sink, s_loc.shape[:-1] + (1,))
        p = jax.nn.softmax(jnp.concatenate([s_loc, s_ctx, s_sink], axis=-1), axis=-1)
        p_loc = p[..., :span].astype(v.dtype)
        p_ctx = p[..., span:span + n_ctx].astype(v.dtype)
        return (jnp.einsum('bkgqj,bjkd->bqkgd', p_loc, v_blk)
                + jnp.einsum('bkgqc,bckd->bqkgd', p_ctx, v_ctx))

    xs = (qb.swapaxes(0, 1), kb.swapaxes(0, 1), vb.swapaxes(0, 1), valid)
    o = lax.map(one_block, xs)
    return o.swapaxes(0, 1).reshape(b, s, h * dh)

def neighbourhood_attention(q, k, v, k_ctx, v_ctx, rpb):
    b, s, h, dh = q.shape
    rows = s // GRID_W
    kr = min(NA_ROWS, rows)
    kw = min(NA_COLS, GRID_W)
    nk = kr * kw
    t = jnp.arange(s, dtype=jnp.int32)
    r = t // GRID_W
    col = t % GRID_W
    r0 = jnp.clip(r - kr // 2, 0, rows - kr)
    c0 = jnp.clip(col - kw // 2, 0, GRID_W - kw)
    key_r = r0[:, None, None] + jnp.arange(kr, dtype=jnp.int32)[None, :, None]
    key_c = c0[:, None, None] + jnp.arange(kw, dtype=jnp.int32)[None, None, :]
    key_idx = (key_r * GRID_W + key_c).reshape(s, nk)
    rel_idx = ((key_r - r[:, None, None] + NA_ROWS - 1) * (2 * NA_COLS - 1)
               + (key_c - col[:, None, None] + NA_COLS - 1)).reshape(s, nk)
    nb = s // Q_BLOCK
    rpb_flat = rpb.reshape(h, -1).astype(jnp.float32)
    scale = dh ** -0.5
    n_ctx = k_ctx.shape[1]

    def one_block(args):
        q_blk, idx, ridx = args
        kg = jnp.take(k, idx.reshape(-1), axis=1).reshape(b, Q_BLOCK, nk, h, dh)
        vg = jnp.take(v, idx.reshape(-1), axis=1).reshape(b, Q_BLOCK, nk, h, dh)
        s_loc = (jnp.einsum('bqhd,bqnhd->bhqn', q_blk, kg).astype(jnp.float32) * scale
                 + jnp.take(rpb_flat, ridx, axis=1)[None])
        s_ctx = jnp.einsum('bqhd,bchd->bhqc', q_blk, k_ctx).astype(jnp.float32) * scale
        p = jax.nn.softmax(jnp.concatenate([s_loc, s_ctx], axis=-1), axis=-1)
        p_loc = p[..., :nk].astype(v.dtype)
        p_ctx = p[..., nk:nk + n_ctx].astype(v.dtype)
        return (jnp.einsum('bhqn,bqnhd->bqhd', p_loc, vg)
                + jnp.einsum('bhqc,bchd->bqhd', p_ctx, v_ctx))

    xs = (q.reshape(b, nb, Q_BLOCK, h, dh).swapaxes(0, 1),
          key_idx.reshape(nb, Q_BLOCK, nk), rel_idx.reshape(nb, Q_BLOCK, nk))
    o = lax.map(one_block, xs)
    return o.swapaxes(0, 1).reshape(b, s, h * dh)

def hyena_positional_features(n):
    t = jnp.linspace(0.0, 1.0, n, dtype=jnp.float32)[:, None]
    bands = (HYENA_EMB - 1) // 2
    w = 2.0 * math.pi * jnp.arange(n, dtype=jnp.float32)[:, None] / n
    f = jnp.linspace(1e-4, bands - 1, bands, dtype=jnp.float32)[None, :]
    return jnp.concatenate([t, jnp.cos(f * w), -jnp.sin(f * w)], axis=-1)

def hyena_filters(n, w1, b1, w2, b2, freq, w3):
    f32 = jnp.float32
    z = hyena_positional_features(n)
    fr = freq.astype(f32)
    hdn = jnp.sin(fr * (z @ w1.astype(f32) + b1.astype(f32)))
    hdn = jnp.sin(fr * (hdn @ w2.astype(f32) + b2.astype(f32)))
    filt = hdn @ w3.astype(f32)
    t = jnp.linspace(0.0, 1.0, n, dtype=f32)[:, None]
    deltas = jnp.linspace(math.log(HYENA_DECAY_TARGET) / HYENA_LONG_DECAY_PCT,
                          math.log(HYENA_DECAY_TARGET) / HYENA_SHORT_DECAY_PCT, HYENA_WIDTH, dtype=f32)
    decay = jnp.exp(-t * jnp.abs(deltas))
    return filt.reshape(n, HYENA_ORDER, 2, HYENA_WIDTH) * decay[:, None, None, :]

def bidir_long_conv(z, h_fwd, h_bwd, d_skip):
    n = z.shape[1]
    taps = jnp.concatenate([h_fwd, jnp.zeros_like(h_fwd[:1]), h_bwd[:0:-1]], axis=0)
    taps = taps * lax.rsqrt(jnp.sum(taps * taps, axis=0, keepdims=True) + EPS)
    zf = jnp.fft.rfft(z.astype(jnp.float32), n=2 * n, axis=1)
    tf = jnp.fft.rfft(taps, n=2 * n, axis=0)
    y = jnp.fft.irfft(zf * tf[None], n=2 * n, axis=1)[:, :n]
    return (y + z.astype(jnp.float32) * d_skip.astype(jnp.float32)).astype(z.dtype)

def centred_depthwise_conv(u, w, bias):
    pad = w.shape[0] // 2
    y = lax.conv_general_dilated(u, w[:, None, :].astype(u.dtype), window_strides=(1,),
                                 padding=[(pad, pad)], dimension_numbers=('NWC', 'WIO', 'NWC'),
                                 feature_group_count=u.shape[-1])
    return y + bias

def hyena_branch(u, conv_w, conv_b, w1, b1, w2, b2, freq, w3, d_skip):
    n = u.shape[1]
    filt = hyena_filters(n, w1, b1, w2, b2, freq, w3)
    uc = centred_depthwise_conv(u, conv_w, conv_b)
    parts = jnp.split(uc, HYENA_ORDER + 1, axis=-1)
    z = parts[0]
    for o in range(HYENA_ORDER):
        z = parts[o + 1] * bidir_long_conv(z, filt[:, o, 0], filt[:, o, 1], d_skip[o])
    return z

def even_mixer(p, p_ctx, q_norm, k_norm, conv_w, conv_b, w1, b1, w2, b2, freq, w3, d_skip, cos, sin, need_ctx):
    aq, ak, av, hu, ag, hg = split_cols(p, EVEN_SPLITS)
    caq, cak, cav, chu, cag, chg = split_cols(p_ctx, EVEN_SPLITS)
    q = apply_rope(rms_norm(heads(aq, N_Q_HEADS), q_norm), cos, sin)
    k = apply_rope(rms_norm(heads(ak, N_KV_HEADS), k_norm), cos, sin)
    v = heads(av, N_KV_HEADS)
    k_c = rms_norm(heads(cak, N_KV_HEADS), k_norm)
    v_c = heads(cav, N_KV_HEADS)
    y_a = global_gqa(q, k, v, k_c, v_c)
    y_b = hyena_branch(hu, conv_w, conv_b, w1, b1, w2, b2, freq, w3, d_skip)
    y = jnp.concatenate([y_a * jax.nn.silu(ag), y_b * jax.nn.silu(hg)], axis=-1)
    if not need_ctx:
        return y, None
    q_c = rms_norm(heads(caq, N_Q_HEADS), q_norm)
    y_ca = context_attention(q_c, k_c, v_c)
    y_cb = hyena_branch(chu, conv_w, conv_b, w1, b1, w2, b2, freq, w3, d_skip)
    y_c = jnp.concatenate([y_ca * jax.nn.silu(cag), y_cb * jax.nn.silu(chg)], axis=-1)
    return y, y_c

def odd_mixer(p, p_ctx, wq_norm, wk_norm, sink, nq_norm, nk_norm, rpb, cos, sin, need_ctx):
    wq, wk, wv, nq, nk_, nv, wg, ng = split_cols(p, ODD_SPLITS)
    cwq, cwk, cwv, cnq, cnk, cnv, cwg, cng = split_cols(p_ctx, ODD_SPLITS)
    q_w = apply_rope(rms_norm(heads(wq, N_Q_HEADS), wq_norm), cos, sin)
    k_w = apply_rope(rms_norm(heads(wk, N_KV_HEADS), wk_norm), cos, sin)
    v_w = heads(wv, N_KV_HEADS)
    kc_w = rms_norm(heads(cwk, N_KV_HEADS), wk_norm)
    vc_w = heads(cwv, N_KV_HEADS)
    y_w = windowed_gqa(q_w, k_w, v_w, kc_w, vc_w, sink)
    q_n = rms_norm(heads(nq, N_Q_HEADS), nq_norm)
    k_n = rms_norm(heads(nk_, N_Q_HEADS), nk_norm)
    v_n = heads(nv, N_Q_HEADS)
    kc_n = rms_norm(heads(cnk, N_Q_HEADS), nk_norm)
    vc_n = heads(cnv, N_Q_HEADS)
    y_n = neighbourhood_attention(q_n, k_n, v_n, kc_n, vc_n, rpb)
    y = jnp.concatenate([y_w * jax.nn.silu(wg), y_n * jax.nn.silu(ng)], axis=-1)
    if not need_ctx:
        return y, None
    y_cw = context_attention(rms_norm(heads(cwq, N_Q_HEADS), wq_norm), kc_w, vc_w, sink)
    y_cn = context_attention(rms_norm(heads(cnq, N_Q_HEADS), nq_norm), kc_n, vc_n)
    y_c = jnp.concatenate([y_cw * jax.nn.silu(cwg), y_cn * jax.nn.silu(cng)], axis=-1)
    return y, y_c

def first_inputs(seed: int = 0) -> dict:
    key = jax.random.key(seed)
    keys = iter(jax.random.split(key, 32))

    def nrm(shape, std):
        return std * jax.random.normal(next(keys), shape, jnp.float32)

    n_filter_out = HYENA_ORDER * 2 * HYENA_WIDTH
    n_hy_in = (HYENA_ORDER + 1) * HYENA_WIDTH
    return {
        'x': nrm((BATCH, SEQ, D_MODEL), 1.0),
        'c': nrm((BATCH, D_MODEL), 1.0),
        'ctx': nrm((BATCH, CTX_LEN, D_MODEL), 1.0),
        'c_ctx': nrm((D_MODEL,), 1.0),
        'norm_g': 1.0 + nrm((DEPTH, D_MODEL), 0.1),
        'w_ada': nrm((DEPTH, D_MODEL, 3 * D_MODEL), D_MODEL ** -0.5),
        'b_ada': nrm((DEPTH, 3 * D_MODEL), 0.01),
        'w_in': nrm((DEPTH, D_MODEL, IN_WIDTH), D_MODEL ** -0.5),
        'w_out': nrm((DEPTH, MIX_WIDTH, D_MODEL), MIX_WIDTH ** -0.5),
        'glob_q_norm': 1.0 + nrm((N_EVEN, HEAD_DIM), 0.1),
        'glob_k_norm': 1.0 + nrm((N_EVEN, HEAD_DIM), 0.1),
        'hy_conv_w': nrm((N_EVEN, HYENA_SHORT_CONV, n_hy_in), HYENA_SHORT_CONV ** -0.5),
        'hy_conv_b': nrm((N_EVEN, n_hy_in), 0.01),
        'hy_w1': nrm((N_EVEN, HYENA_EMB, HYENA_HIDDEN), HYENA_EMB ** -0.5),
        'hy_b1': nrm((N_EVEN, HYENA_HIDDEN), 0.01),
        'hy_w2': nrm((N_EVEN, HYENA_HIDDEN, HYENA_HIDDEN), HYENA_HIDDEN ** -0.5),
        'hy_b2': nrm((N_EVEN, HYENA_HIDDEN), 0.01),
        'hy_freq': 1.0 + nrm((N_EVEN, HYENA_HIDDEN), 0.1),
        'hy_w3': nrm((N_EVEN, HYENA_HIDDEN, n_filter_out), HYENA_HIDDEN ** -0.5),
        'hy_skip': nrm((N_EVEN, HYENA_ORDER, HYENA_WIDTH), 0.5),
        'win_q_norm': 1.0 + nrm((N_ODD, HEAD_DIM), 0.1),
        'win_k_norm': 1.0 + nrm((N_ODD, HEAD_DIM), 0.1),
        'win_sink': nrm((N_ODD, N_Q_HEADS), 0.5),
        'nat_q_norm': 1.0 + nrm((N_ODD, HEAD_DIM), 0.1),
        'nat_k_norm': 1.0 + nrm((N_ODD, HEAD_DIM), 0.1),
        'nat_rpb': nrm((N_ODD, N_Q_HEADS, 2 * NA_ROWS - 1, 2 * NA_COLS - 1), 0.1),
    }

def first_block(x, c, ctx, c_ctx, norm_g, w_ada, b_ada, w_in, w_out,
              glob_q_norm, glob_k_norm, hy_conv_w, hy_conv_b, hy_w1, hy_b1, hy_w2, hy_b2,
              hy_freq, hy_w3, hy_skip, win_q_norm, win_k_norm, win_sink,
              nat_q_norm, nat_k_norm, nat_rpb):
    cos, sin = axial_rope_tables(x.shape[1])
    x_ctx = ctx
    for layer in range(DEPTH):
        need_ctx = layer < DEPTH - 1
        shift, scale, gate = adaln(c, w_ada[layer], b_ada[layer])
        c_shift, c_scale, c_gate = adaln(c_ctx, w_ada[layer], b_ada[layer])
        h = modulated_norm(x, norm_g[layer], shift[:, None], scale[:, None])
        h_ctx = modulated_norm(x_ctx, norm_g[layer], c_shift, c_scale)
        p = jnp.matmul(h, w_in[layer])
        p_ctx = jnp.matmul(h_ctx, w_in[layer])
        i = layer // 2
        if layer % 2 == 0:
            y, y_ctx = even_mixer(p, p_ctx, glob_q_norm[i], glob_k_norm[i], hy_conv_w[i], hy_conv_b[i],
                                  hy_w1[i], hy_b1[i], hy_w2[i], hy_b2[i], hy_freq[i], hy_w3[i], hy_skip[i],
                                  cos, sin, need_ctx)
        else:
            y, y_ctx = odd_mixer(p, p_ctx, win_q_norm[i], win_k_norm[i], win_sink[i],
                                 nat_q_norm[i], nat_k_norm[i], nat_rpb[i], cos, sin, need_ctx)
        x = x + gate[:, None] * jnp.matmul(y, w_out[layer])
        if need_ctx:
            x_ctx = x_ctx + c_gate * jnp.matmul(y_ctx, w_out[layer])
    return x


DH = 64
QBLK = 128
NSA_HEADS = 8
NSA_GROUPS = 2
NSA_R = NSA_HEADS // NSA_GROUPS
L_CMP = 32
D_CMP = 16
CMP_HIDDEN = 128
L_SLC = 64
N_SEL = 8
WINDOW_2 = 512
MLA_HEADS = 4
MLA_NOPE = 64
MLA_ROPE = 32
MLA_V = 64
MLA_Q_LORA = 384
MLA_KV_LORA = 128
FOX_HEADS = 4
XA_HEADS = 4
MEM_LEN = 256
D_FF = 4 * D_MODEL
T5_BUCKETS = 32
T5_MAX_DIST = 128
NSA_W = NSA_HEADS * DH
NSA_KV = NSA_GROUPS * DH
MLA_W = MLA_HEADS * MLA_V
FOX_W = FOX_HEADS * DH
XA_W = XA_HEADS * DH
IN_SIZES = (NSA_W, NSA_KV, NSA_KV, NSA_KV, NSA_KV, NSA_KV, NSA_KV, 3 * NSA_HEADS,
            MLA_Q_LORA, MLA_KV_LORA, MLA_ROPE,
            FOX_W, FOX_W, FOX_W, FOX_HEADS)
N_IN = sum(IN_SIZES)
DN_ALPHA = (2 * DEPTH) ** 0.25
DN_BETA = (8 * DEPTH) ** -0.25
LN_EPS = 1e-5
RMS_EPS = 1e-6
NEG = -1e30
FORCE = 1e4


def layer_norm(x, g, b):
    x32 = x.astype(jnp.float32)
    mu = jnp.mean(x32, axis=-1, keepdims=True)
    var = jnp.mean(jnp.square(x32 - mu), axis=-1, keepdims=True)
    return ((x32 - mu) * lax.rsqrt(var + LN_EPS) * g + b).astype(x.dtype)

def rms_norm_2(x, g):
    x32 = x.astype(jnp.float32)
    return (x32 * lax.rsqrt(jnp.mean(jnp.square(x32), axis=-1, keepdims=True) + RMS_EPS) * g).astype(x.dtype)

def rope(x, pos):
    half = x.shape[-1] // 2
    inv = ROPE_THETA ** (-jnp.arange(half, dtype=jnp.float32) / half)
    ang = pos.astype(jnp.float32)[:, None] * inv[None, :]
    cos = jnp.cos(ang)[None, :, None, :].astype(x.dtype)
    sin = jnp.sin(ang)[None, :, None, :].astype(x.dtype)
    x1, x2 = x[..., :half], x[..., half:]
    return jnp.concatenate([x1 * cos - x2 * sin, x1 * sin + x2 * cos], axis=-1)

def t5_bucket(dist):
    n = jnp.maximum(dist, 0)
    max_exact = T5_BUCKETS // 2
    nf = jnp.maximum(n, 1).astype(jnp.float32)
    large = max_exact + (jnp.log(nf / max_exact) / math.log(T5_MAX_DIST / max_exact)
                         * (T5_BUCKETS - max_exact)).astype(jnp.int32)
    large = jnp.minimum(large, T5_BUCKETS - 1)
    return jnp.where(n < max_exact, n, large)

def causal_block_attention(q, k, v, cum_log_f=None):
    B, S, H, dk = q.shape
    dv = v.shape[-1]
    nqb = S // QBLK
    scale = dk ** -0.5
    qb = q.reshape(B, nqb, QBLK, H, dk).transpose(1, 0, 2, 3, 4)
    key_pos = jnp.arange(S)
    decay_k = None if cum_log_f is None else cum_log_f.transpose(0, 2, 1)

    def one_block(args):
        i, q_i = args
        q_pos = i * QBLK + jnp.arange(QBLK)
        s = jnp.einsum('bqhd,bkhd->bhqk', q_i, k).astype(jnp.float32) * scale
        if decay_k is not None:
            decay_q = lax.dynamic_slice_in_dim(decay_k, i * QBLK, QBLK, axis=2)
            s = s + decay_q[..., None] - decay_k[:, :, None, :]
        s = jnp.where(key_pos[None, :] <= q_pos[:, None], s, NEG)
        p = jax.nn.softmax(s, axis=-1).astype(v.dtype)
        return jnp.einsum('bhqk,bkhd->bqhd', p, v)

    out = lax.map(one_block, (jnp.arange(nqb), qb))
    return out.transpose(1, 0, 2, 3, 4).reshape(B, S, H * dv)

def nsa_attention(q, k_cmp, v_cmp, k_slc, v_slc, k_win, v_win, gate_logits,
                  cmp_pe, cmp_w1, cmp_w2, t5_table):
    B, S, _ = q.shape
    G, R = NSA_GROUPS, NSA_R
    nqb = S // QBLK
    n_cmp = (S - L_CMP) // D_CMP + 1
    n_slc = S // L_SLC
    n_sel = min(N_SEL, n_slc)
    scale = DH ** -0.5
    k_cmp, v_cmp, k_slc, v_slc, k_win, v_win = [a.reshape(B, S, G, DH) for a in
                                                  (k_cmp, v_cmp, k_slc, v_slc, k_win, v_win)]

    tok_idx = jnp.arange(n_cmp)[:, None] * D_CMP + jnp.arange(L_CMP)[None, :]

    def compress(kv, pe, w1, w2):
        blocks = kv[:, tok_idx] + pe[None, None, :, None, :]
        flat = blocks.transpose(0, 1, 3, 2, 4).reshape(B, n_cmp, G, L_CMP * DH)
        return jax.nn.gelu(flat @ w1) @ w2

    kc = compress(k_cmp, cmp_pe[0], cmp_w1[0], cmp_w2[0])
    vc = compress(v_cmp, cmp_pe[1], cmp_w1[1], cmp_w2[1])
    cmp_end = jnp.arange(n_cmp) * D_CMP + (L_CMP - 1)

    c_lo = jnp.arange(n_cmp)[:, None] * D_CMP
    s_lo = jnp.arange(n_slc)[None, :] * L_SLC
    overlap = (jnp.maximum(jnp.minimum(c_lo + L_CMP, s_lo + L_SLC) - jnp.maximum(c_lo, s_lo), 0)
               .astype(jnp.float32) / D_CMP)

    ks_blk = k_slc.reshape(B, n_slc, L_SLC, G, DH).transpose(0, 3, 1, 2, 4)
    vs_blk = v_slc.reshape(B, n_slc, L_SLC, G, DH).transpose(0, 3, 1, 2, 4)
    kw_pad = jnp.pad(k_win, ((0, 0), (WINDOW_2, 0), (0, 0), (0, 0)))
    vw_pad = jnp.pad(v_win, ((0, 0), (WINDOW_2, 0), (0, 0), (0, 0)))

    qb = q.reshape(B, nqb, QBLK, G, R, DH).transpose(1, 0, 3, 4, 2, 5)
    gb = jax.nn.sigmoid(gate_logits).reshape(B, nqb, QBLK, G, R, 3).transpose(1, 0, 3, 4, 2, 5)
    bias_tab = t5_table.reshape(T5_BUCKETS, G, R).transpose(1, 2, 0)
    b_idx = jnp.arange(B)[:, None, None, None]
    g_idx = jnp.arange(G)[None, :, None, None]
    g5 = jnp.arange(G)[None, :, None, None, None]
    r5 = jnp.arange(R)[None, None, :, None, None]
    blk_ids = jnp.arange(n_slc)

    def one_block(args):
        i, q_i, g_i = args
        t = i * QBLK + jnp.arange(QBLK)
        dist_c = t[:, None] - cmp_end[None, :]
        valid_c = dist_c >= 0
        s_c = (jnp.einsum('bgrqd,bcgd->bgrqc', q_i, kc).astype(jnp.float32) * scale
               + bias_tab[:, :, t5_bucket(dist_c)])
        p_c = jax.nn.softmax(jnp.where(valid_c, s_c, NEG), axis=-1) * valid_c
        o_c = jnp.einsum('bgrqc,bcgd->bgrqd', p_c.astype(vc.dtype), vc)
        imp = jnp.einsum('bgrqc,cn->bgqn', p_c, overlap)
        cur = t // L_SLC
        forced = ((blk_ids[None, :] == 0) | (blk_ids[None, :] == cur[:, None])
                  | (blk_ids[None, :] == cur[:, None] - 1))
        causal_blk = blk_ids[None, :] * L_SLC <= t[:, None]
        imp = jnp.where(causal_blk, imp + FORCE * forced, NEG)
        _, sel = lax.top_k(imp, n_sel)
        k_sel = ks_blk[b_idx, g_idx, sel].reshape(B, G, QBLK, n_sel * L_SLC, DH)
        v_sel = vs_blk[b_idx, g_idx, sel].reshape(B, G, QBLK, n_sel * L_SLC, DH)
        pos_sel = (sel[..., None] * L_SLC + jnp.arange(L_SLC)).reshape(B, G, QBLK, n_sel * L_SLC)
        dist_s = t[:, None] - pos_sel
        s_s = (jnp.einsum('bgrqd,bgqkd->bgrqk', q_i, k_sel).astype(jnp.float32) * scale
               + bias_tab[g5, r5, t5_bucket(dist_s)[:, :, None]])
        p_s = jax.nn.softmax(jnp.where((dist_s >= 0)[:, :, None], s_s, NEG), axis=-1)
        o_s = jnp.einsum('bgrqk,bgqkd->bgrqd', p_s.astype(v_sel.dtype), v_sel)
        pos_w = i * QBLK - WINDOW_2 + jnp.arange(WINDOW_2 + QBLK)
        dist_w = t[:, None] - pos_w[None, :]
        valid_w = (dist_w >= 0) & (dist_w < WINDOW_2) & (pos_w[None, :] >= 0)
        k_w = lax.dynamic_slice_in_dim(kw_pad, i * QBLK, WINDOW_2 + QBLK, axis=1)
        v_w = lax.dynamic_slice_in_dim(vw_pad, i * QBLK, WINDOW_2 + QBLK, axis=1)
        s_w = (jnp.einsum('bgrqd,bkgd->bgrqk', q_i, k_w).astype(jnp.float32) * scale
               + bias_tab[:, :, t5_bucket(dist_w)])
        p_w = jax.nn.softmax(jnp.where(valid_w, s_w, NEG), axis=-1)
        o_w = jnp.einsum('bgrqk,bkgd->bgrqd', p_w.astype(v_w.dtype), v_w)
        return g_i[..., 0:1] * o_c + g_i[..., 1:2] * o_s + g_i[..., 2:3] * o_w

    out = lax.map(one_block, (jnp.arange(nqb), qb, gb))
    return out.transpose(1, 0, 4, 2, 3, 5).reshape(B, S, NSA_W)

def mla_attention(c_q, c_kv, k_rope, q_norm, w_uq, kv_norm, w_ukv):
    B, S, _ = c_q.shape
    pos = jnp.arange(S)
    q = (rms_norm_2(c_q, q_norm) @ w_uq).reshape(B, S, MLA_HEADS, MLA_NOPE + MLA_ROPE)
    q = jnp.concatenate([q[..., :MLA_NOPE], rope(q[..., MLA_NOPE:], pos)], axis=-1)
    kv = (rms_norm_2(c_kv, kv_norm) @ w_ukv).reshape(B, S, MLA_HEADS, MLA_NOPE + MLA_V)
    k_r = jnp.broadcast_to(rope(k_rope[:, :, None, :], pos), (B, S, MLA_HEADS, MLA_ROPE))
    k = jnp.concatenate([kv[..., :MLA_NOPE], k_r], axis=-1)
    return causal_block_attention(q, k, kv[..., MLA_NOPE:])

def fox_attention(q, k, v, f_logit, b_f):
    B, S, _ = q.shape
    shp = (B, S, FOX_HEADS, DH)
    cum = jnp.cumsum(jax.nn.log_sigmoid((f_logit + b_f).astype(jnp.float32)), axis=1)
    return causal_block_attention(q.reshape(shp), k.reshape(shp), v.reshape(shp), cum_log_f=cum)

def hybrid_mixer(h, w_in, cmp_pe, cmp_w1, cmp_w2, t5_table, q_norm, w_uq, kv_norm, w_ukv,
                 b_f, w_gate, w_br_nsa, w_br_mla, w_br_fox, w_out):
    B, S, _ = h.shape
    split_points = np.cumsum(IN_SIZES)[:-1].tolist()
    (nq, nkc, nvc, nks, nvs, nkw, nvw, ngate,
     cq, ckv, kr, fq, fk, fv, ff) = jnp.split(h @ w_in, split_points, axis=-1)
    o_nsa = nsa_attention(nq, nkc, nvc, nks, nvs, nkw, nvw, ngate, cmp_pe, cmp_w1, cmp_w2, t5_table)
    o_mla = mla_attention(cq, ckv, kr, q_norm, w_uq, kv_norm, w_ukv)
    o_fox = fox_attention(fq, fk, fv, ff, b_f)
    gates = jax.nn.sigmoid(h @ w_gate).reshape(B, S, 3, D_MODEL)
    merged = (gates[:, :, 0] * (o_nsa @ w_br_nsa) + gates[:, :, 1] * (o_mla @ w_br_mla)
              + gates[:, :, 2] * (o_fox @ w_br_fox))
    return merged @ w_out

def memory_cross_attention(x, mem, w_q, w_kv, w_o):
    B, S, _ = x.shape
    M = mem.shape[1]
    q = (x @ w_q).reshape(B, S, XA_HEADS, DH)
    kv = (mem @ w_kv).reshape(B, M, 2, XA_HEADS, DH)
    k, v = kv[:, :, 0], kv[:, :, 1]
    s = jnp.einsum('bqhd,bmhd->bhqm', q, k).astype(jnp.float32) * (DH ** -0.5)
    p = jax.nn.softmax(s, axis=-1).astype(v.dtype)
    o = jnp.einsum('bhqm,bmhd->bqhd', p, v).reshape(B, S, XA_W)
    return o @ w_o

def second_inputs(seed: int = 0) -> dict:
    key = jax.random.key(seed)
    ks = jax.random.split(key, 32)
    L = DEPTH

    def dense(k, shape, fan_in, scale=1.0):
        return jax.random.normal(k, shape, jnp.float32) * (scale * fan_in ** -0.5)

    def normal(k, shape, scale=1.0):
        return jax.random.normal(k, shape, jnp.float32) * scale

    return {
        'x': normal(ks[0], (BATCH, SEQ, D_MODEL)),
        'mem': normal(ks[1], (BATCH, MEM_LEN, D_MODEL)),
        'w_in': dense(ks[2], (L, D_MODEL, N_IN), D_MODEL),
        'cmp_pe': normal(ks[3], (L, 2, L_CMP, DH), 0.1),
        'cmp_w1': dense(ks[4], (L, 2, L_CMP * DH, CMP_HIDDEN), L_CMP * DH),
        'cmp_w2': dense(ks[5], (L, 2, CMP_HIDDEN, DH), CMP_HIDDEN),
        't5_table': normal(ks[6], (T5_BUCKETS, NSA_HEADS), 0.5),
        'mla_q_norm': 1.0 + normal(ks[7], (L, MLA_Q_LORA), 0.02),
        'mla_w_uq': dense(ks[8], (L, MLA_Q_LORA, MLA_HEADS * (MLA_NOPE + MLA_ROPE)), MLA_Q_LORA),
        'mla_kv_norm': 1.0 + normal(ks[9], (L, MLA_KV_LORA), 0.02),
        'mla_w_ukv': dense(ks[10], (L, MLA_KV_LORA, MLA_HEADS * (MLA_NOPE + MLA_V)), MLA_KV_LORA),
        'fox_b_f': jax.random.uniform(ks[11], (L, FOX_HEADS), jnp.float32, 1.0, 6.0),
        'w_gate': dense(ks[12], (L, D_MODEL, 3 * D_MODEL), D_MODEL),
        'w_br_nsa': dense(ks[13], (L, NSA_W, D_MODEL), NSA_W),
        'w_br_mla': dense(ks[14], (L, MLA_W, D_MODEL), MLA_W),
        'w_br_fox': dense(ks[15], (L, FOX_W, D_MODEL), FOX_W),
        'w_mix_out': dense(ks[16], (L, D_MODEL, D_MODEL), D_MODEL, DN_BETA),
        'xa_w_q': dense(ks[17], (L, D_MODEL, XA_W), D_MODEL),
        'xa_w_kv': dense(ks[18], (L, D_MODEL, 2 * XA_W), D_MODEL),
        'xa_w_o': dense(ks[19], (L, XA_W, D_MODEL), XA_W, DN_BETA),
        'mlp_w_up': dense(ks[20], (L, D_MODEL, D_FF), D_MODEL),
        'mlp_w_down': dense(ks[21], (L, D_FF, D_MODEL), D_FF, DN_BETA),
        'ln_g': 1.0 + normal(ks[22], (L, 3, D_MODEL), 0.02),
        'ln_b': normal(ks[23], (L, 3, D_MODEL), 0.02),
    }

def second_block(x, mem, w_in, cmp_pe, cmp_w1, cmp_w2, t5_table, mla_q_norm, mla_w_uq, mla_kv_norm,
              mla_w_ukv, fox_b_f, w_gate, w_br_nsa, w_br_mla, w_br_fox, w_mix_out, xa_w_q, xa_w_kv,
              xa_w_o, mlp_w_up, mlp_w_down, ln_g, ln_b):
    for l in range(DEPTH):
        y = hybrid_mixer(x, w_in[l], cmp_pe[l], cmp_w1[l], cmp_w2[l], t5_table, mla_q_norm[l],
                         mla_w_uq[l], mla_kv_norm[l], mla_w_ukv[l], fox_b_f[l], w_gate[l],
                         w_br_nsa[l], w_br_mla[l], w_br_fox[l], w_mix_out[l])
        x = layer_norm(DN_ALPHA * x + y, ln_g[l, 0], ln_b[l, 0])
        y = memory_cross_attention(x, mem, xa_w_q[l], xa_w_kv[l], xa_w_o[l])
        x = layer_norm(DN_ALPHA * x + y, ln_g[l, 1], ln_b[l, 1])
        y = jnp.square(jax.nn.relu(x @ mlp_w_up[l])) @ mlp_w_down[l]
        x = layer_norm(DN_ALPHA * x + y, ln_g[l, 2], ln_b[l, 2])
    return x


def setup_inputs(seed=0):
    out = dict(first_inputs(seed))
    for name, value in second_inputs(seed + 1).items():
        if name != "x":
            out[name + "_2"] = value
    return out


def reference(
    x, c, ctx, c_ctx, norm_g, w_ada, b_ada, w_in, w_out, glob_q_norm, glob_k_norm, hy_conv_w,
    hy_conv_b, hy_w1, hy_b1, hy_w2, hy_b2, hy_freq, hy_w3, hy_skip, win_q_norm, win_k_norm,
    win_sink, nat_q_norm, nat_k_norm, nat_rpb, mem_2, w_in_2, cmp_pe_2, cmp_w1_2, cmp_w2_2,
    t5_table_2, mla_q_norm_2, mla_w_uq_2, mla_kv_norm_2, mla_w_ukv_2, fox_b_f_2, w_gate_2,
    w_br_nsa_2, w_br_mla_2, w_br_fox_2, w_mix_out_2, xa_w_q_2, xa_w_kv_2, xa_w_o_2, mlp_w_up_2,
    mlp_w_down_2, ln_g_2, ln_b_2,
):
    x = first_block(
        x, c, ctx, c_ctx, norm_g, w_ada, b_ada, w_in, w_out, glob_q_norm, glob_k_norm,
        hy_conv_w, hy_conv_b, hy_w1, hy_b1, hy_w2, hy_b2, hy_freq, hy_w3, hy_skip, win_q_norm,
        win_k_norm, win_sink, nat_q_norm, nat_k_norm, nat_rpb,
    )
    return second_block(
        x, mem_2, w_in_2, cmp_pe_2, cmp_w1_2, cmp_w2_2, t5_table_2, mla_q_norm_2, mla_w_uq_2,
        mla_kv_norm_2, mla_w_ukv_2, fox_b_f_2, w_gate_2, w_br_nsa_2, w_br_mla_2, w_br_fox_2,
        w_mix_out_2, xa_w_q_2, xa_w_kv_2, xa_w_o_2, mlp_w_up_2, mlp_w_down_2, ln_g_2, ln_b_2,
    )


_drawn_inputs = setup_inputs


def setup_inputs(seed=0):
    import zlib

    import numpy as np

    out = dict(_drawn_inputs(seed))
    spreads = {}
    factors = {'glob_q_norm': 8.0,
     'glob_k_norm': 8.0,
     'win_q_norm': 8.0,
     'win_k_norm': 8.0,
     'win_sink': 8.0,
     'nat_q_norm': 8.0,
     'nat_k_norm': 8.0,
     'nat_rpb': 8.0,
     'cmp_pe_2': 8.0,
     'mla_q_norm_2': 8.0,
     'mla_kv_norm_2': 8.0}
    for name, (base, spread) in spreads.items():
        noise = np.random.default_rng([zlib.crc32(name.encode()), seed]).standard_normal(out[name].shape)
        drawn = base * np.exp(spread * noise) if base else spread * noise
        out[name] = jnp.asarray(drawn.astype(out[name].dtype))
    for name, factor in factors.items():
        out[name] = (out[name] * factor).astype(out[name].dtype)
    return out
```

```python
import math

import numpy as np
import concourse.bass as bass
from concourse import mybir
from concourse.alu_op_type import AluOpType as ALU

F32 = mybir.dt.float32
ACT = mybir.ActivationFunctionType
AX = mybir.AxisListType
NEG = -1e30
LOW = -3e38
EPS = 1e-6
LN_EPS = 1e-5
ALPHA = 4 ** 0.25

CONST = 0
RING = 3200
SLOT = 4352
NSLOT = 3
XR = RING + SLOT * NSLOT
BIG = XR + 6144
END = 53100


class Engine:

    def __init__(self, nc, eng, name, serial=True):
        self.e, self.sem, self.n, self.seen, self.serial = eng, nc.alloc_semaphore(name), 0, {}, serial

    def need(self, *toks):
        for t in toks:
            if t is None:
                continue
            if isinstance(t, list):
                self.need(*t)
                continue
            sem, v = t
            if self.seen.get(id(sem), 0) < v:
                self.e.wait_ge(sem, v)
                self.seen[id(sem)] = v

    def begin(self, toks):
        self.need(*toks)
        if self.serial and self.n:
            self.need(self.last())

    def done(self, ins):
        self.n += 1
        ins.then_inc(self.sem, 1)
        return (self.sem, self.n)

    def last(self):
        return (self.sem, self.n)

    def tt(self, out, a, b, op, *after):
        self.begin(after)
        return self.done(self.e.tensor_tensor(out, a, b, op))

    def ts(self, out, a, s1, op0, s2, op1, *after):
        self.begin(after)
        return self.done(self.e.tensor_scalar(out, a, s1, s2, op0, op1))

    def ts1(self, out, a, s1, op0, *after):
        self.begin(after)
        return self.done(self.e.tensor_scalar(out, a, s1, None, op0))

    def stt(self, out, a, s, b, op0, op1, *after):
        self.begin(after)
        return self.done(self.e.scalar_tensor_tensor(out, a, s, b, op0, op1))

    def addmax(self, out, a, b, init, acc, *after):
        self.begin(after)
        return self.done(self.e.tensor_tensor_reduce(out=out, in0=a, in1=b, scale=1.0, scalar=init,
                                                     op0=ALU.add, op1=ALU.max, accum_out=acc))

    def red(self, out, a, op, *after):
        self.begin(after)
        return self.done(self.e.tensor_reduce(out, a, AX.X, op))

    def copy(self, out, a, *after):
        self.begin(after)
        return self.done(self.e.tensor_copy(out, a))

    def zero(self, out, v, *after):
        self.begin(after)
        return self.done(self.e.memset(out, v))

    def recip(self, out, a, *after):
        self.begin(after)
        return self.done(self.e.reciprocal(out, a))

    def act(self, out, a, f, *after, bias=0.0, scale=1.0, acc=None):
        self.begin(after)
        if acc is None:
            return self.done(self.e.activation(out, a, f, bias=bias, scale=scale))
        return self.done(self.e.activation(out, a, f, bias=bias, scale=scale, accum_out=acc))


class Dmas:

    def __init__(self, nc, eng, name, n, owner=None):
        self.sems = [nc.alloc_semaphore(f"{name}{i}") for i in range(n)]
        self.vals = [0] * n
        self.k = 0
        self.w = owner or Engine(nc, eng, name + "w")
        self.eng = eng

    def go(self, out, in_, *after):
        i = self.k % len(self.sems)
        self.k += 1
        self.w.need(*after)
        if self.vals[i]:
            self.w.need((self.sems[i], self.vals[i]))
        self.eng.dma_start(out, in_).then_inc(self.sems[i], 16)
        self.vals[i] += 16
        return (self.sems[i], self.vals[i])


def bcast(ap, at, n):
    dims = [list(d) for d in ap.ap]
    dims.insert(at, [0, n])
    return bass.AP(ap.tensor, ap.offset, dims)


def rows(w, r0, kt, c0, c1):
    return w[r0:r0 + 128 * kt, c0:c1].rearrange("(k p) n -> p k n", p=128)


def program(nc, D, out):
    S = nc.alloc_sbuf_tensor("S", [128, END], F32)
    PS = nc.alloc_psum_tensor("PS", [128, 8, 512], F32)
    PE = Engine(nc, nc.tensor, "s_pe", serial=False)
    V = Engine(nc, nc.vector, "s_dve")
    A = Engine(nc, nc.scalar, "s_act")
    G = Engine(nc, nc.gpsimd, "s_pool")
    WQ = Dmas(nc, nc.sync, "s_w", 8)
    MQ = Dmas(nc, nc.gpsimd, "s_m", 12, owner=G)
    pf = [None] * 8

    def sb(off, *dims):
        n = 1
        for d in dims:
            n *= d
        v = S[:, off:off + n]
        if len(dims) == 2:
            v = v.rearrange("p (a b) -> p a b", a=dims[0])
        if len(dims) == 3:
            v = v.rearrange("p (a b c) -> p a b c", a=dims[0], b=dims[1])
        return v

    def barrier():
        toks = [PE.last(), V.last(), A.last(), G.last()]
        toks = [t for t in toks if t[1]]
        for e in (PE, V, A, G):
            e.need(*toks)
        return toks

    plan = []

    def want(src, *dims):
        n = 1
        for d in dims:
            n *= d
        plan.append((src, dims))

    w_ada, w_in, w_out = D["w_ada"], D["w_in"], D["w_out"]
    E_IN = [(0, 512), (512, 768), (2304, 2816), (768, 1280), (1280, 1792), (1792, 2304), (2816, 3328)]
    for n in range(6):
        want(rows(w_ada[0], 0, 8, n * 512, n * 512 + 512), 8, 512)
    for a, b in E_IN:
        want(rows(w_in[0], 0, 8, a, b), 8, b - a)
    for o in range(2):
        want(D["dftf"].rearrange("(k p) n -> p k n", p=128), 4, 1024)
        want(D["dftg"].rearrange("(k p) n -> p k n", p=128), 8, 512)
    for n in range(2):
        want(rows(w_out[0], 0, 8, n * 512, n * 512 + 512), 8, 512)
    for n in range(6):
        want(rows(w_ada[1], 0, 8, n * 512, n * 512 + 512), 8, 512)
    for a, b in [(0, 512), (512, 768), (2304, 2816), (768, 1280), (1280, 1792), (1792, 2304), (2816, 3328)]:
        want(rows(w_in[1], 0, 8, a, b), 8, b - a)
    for n in range(2):
        want(rows(w_out[1], 0, 8, n * 512, n * 512 + 512), 8, 512)
    S_IN = [(0, 512), (512, 1024), (1024, 1304), (1304, 1848), (1848, 2360), (2360, 2620)]
    for l in range(2):
        w2 = D["w_in_2"][l]
        for a, b in S_IN[:3]:
            want(rows(w2, 0, 8, a, b), 8, b - a)
        for kv in range(2):
            want(("cmpw", l, kv), 32, 128)
        want(rows(w2, 0, 8, 1304, 1848), 8, 544)
        want(rows(D["mla_w_uq_2"][l], 0, 3, 0, 384), 3, 384)
        want(rows(D["mla_w_ukv_2"][l], 0, 1, 0, 512), 1, 512)
        for a, b in S_IN[4:]:
            want(rows(w2, 0, 8, a, b), 8, b - a)
        for br, name, kt in ((0, "w_br_nsa_2", 4), (1, "w_br_mla_2", 2), (2, "w_br_fox_2", 2)):
            want(rows(D[name][l], 0, kt, 0, 1024), kt, 1024)
            for n in range(2):
                c = br * 1024 + n * 512
                want(rows(D["w_gate_2"][l], 0, 8, c, c + 512), 8, 512)
        for n in range(2):
            want(rows(D["w_mix_out_2"][l], 0, 8, n * 512, n * 512 + 512), 8, 512)
        want(rows(D["xa_w_q_2"][l], 0, 8, 0, 256), 8, 256)
        want(rows(D["xa_w_kv_2"][l], 0, 8, 0, 512), 8, 512)
        want(rows(D["xa_w_o_2"][l], 0, 2, 0, 1024), 2, 1024)
        for n in range(8):
            want(rows(D["mlp_w_up_2"][l], 0, 8, n * 512, n * 512 + 512), 8, 512)
        for n in range(2):
            for r in range(4):
                want(rows(D["mlp_w_down_2"][l], r * 1024, 8, n * 512, n * 512 + 512), 8, 512)

    loaded = []
    state = {"next": 0}

    def load_weight(*after):
        i = len(loaded)
        if i >= len(plan):
            return
        src, dims = plan[i]
        v = sb(RING + (i % NSLOT) * SLOT, *dims)
        if isinstance(src, tuple):
            _, l, kv = src
            w = D["cmp_w1_2"][l, kv].rearrange("(l d) n -> d l n", d=64)
            t = [WQ.go(v[0:64], w, *after), WQ.go(v[64:128], w, *after)]
        else:
            t = WQ.go(v, src, *after)
        loaded.append((v, t))

    for _ in range(NSLOT):
        load_weight()

    def weight():
        i = state["next"]
        state["next"] += 1
        return loaded[i]

    def used(tok):
        load_weight(tok)

    def group(dst, pairs, *after):
        PE.need(*after)
        n = len(pairs)
        for i, (l, r) in enumerate(pairs):
            m = nc.tensor.matmul(dst, l, r, start=(i == 0), stop=(i == n - 1))
        return PE.done(m)

    rot = {"b": 0, "e": 0}

    def bank():
        rot["b"] = (rot["b"] + 1) % 8
        return rot["b"]

    def evac(dst, src, tok, *after, scale=None):
        rot["e"] ^= 1
        if rot["e"]:
            if scale is None:
                return V.copy(dst, src, tok, *after)
            return V.ts1(dst, src, scale, ALU.mult, tok, *after)
        return A.act(dst, src, ACT.Copy, tok, *after, scale=1.0 if scale is None else scale)

    def flip(dst_of, src_of, ins, outs, npart=128, m=128, evacuate=evac, after=()):
        toks = []
        for o in outs:
            b = bank()
            PE.need(pf[b], *after)
            for n, i in enumerate(ins):
                x = nc.tensor.transpose(PS[0:m, b, n * npart:(n + 1) * npart], src_of(o, i), ident[0:npart, 0:npart])
            tok = PE.done(x)
            pf[b] = evacuate(dst_of(o), PS[0:m, b, 0:len(ins) * npart], tok)
            toks.append(pf[b])
        return toks

    c_at = {"o": CONST}

    def cst(*dims):
        n = 1
        for d in dims:
            n *= d
        o = c_at["o"]
        c_at["o"] += n
        assert c_at["o"] <= RING
        return sb(o, *dims)

    ident = cst(128)
    t_id = MQ.go(ident, D["ident"])
    ones = cst(128)
    V.zero(ones, 1.0)
    small = cst(512)
    stats = cst(8, 16)
    g2i = cst(2, 256)
    MQ.go(g2i, D["g2i"].rearrange("(k p) n -> p k n", p=128))
    cos1, sin1 = cst(4, 32), cst(4, 32)
    cos2, sin2 = cst(4, 16), cst(4, 16)
    for v, name in ((cos1, "cos1"), (sin1, "sin1"), (cos2, "cos2"), (sin2, "sin2")):
        MQ.go(v, D[name].rearrange("(k p) n -> p k n", p=128))
    aff = cst(8, 2, 2)
    ada = cst(24, 2)
    cT = cst(8, 2)
    ctmp = cst(8, 2)
    bada = cst(24)
    ng = cst(8)
    const_toks = [(s, v) for s, v in zip(MQ.sems, MQ.vals) if v]
    for e in (PE, V, A, G):
        e.need(*const_toks)
    barrier()

    def rsqrt(r, x, t1, *after):
        a = A.act(t1, x, ACT.Ln, *after)
        a = A.act(r, t1, ACT.Exp, a, scale=-0.5)
        V.tt(t1, r, r, ALU.mult, a)
        V.tt(t1, t1, x, ALU.mult)
        V.ts(t1, t1, -0.5, ALU.mult, 1.5, ALU.add)
        return V.tt(r, r, t1, ALU.mult)

    X = sb(XR, 6, 1024)

    def attention(jobs, P, PT, order_evac=evac):
        free_P = [None, None]
        free_PT = [None, None, None]
        cnt = {"u": 0, "t": 0}
        pending = []

        def scores(j, n, q):
            pair = cnt["u"] % 2
            cnt["u"] += 1
            b0 = 2 * pair
            pair_ap = PS[:, b0:b0 + 2, :].rearrange("p a b -> p (a b)")
            PE.need(pf[b0], pf[b0 + 1], *j.get("after", ()))
            for c0, nn, l, r in j["scores"](q):
                m = nc.tensor.matmul(pair_ap[:, c0:c0 + nn], l, r, start=True, stop=True)
            tok = PE.done(m)
            st = stats[:, cnt["u"] % 8, :]
            Pq = (j["P"] if "P" in j else P[n % 2])[q]
            rel, rdy = softmax(j, q, pair_ap, Pq, st, tok, free_P[n % 2])
            pf[b0] = pf[b0 + 1] = rel
            return rdy

        def softmax(j, q, ps, Pq, st, tok, free):
            plain, biased = j["segs"](q)
            m = None
            rel = []
            if plain:
                c0, c1 = plain
                t = V.red(st[:, 0:1], ps[:, c0:c1], ALU.max, tok)
                m = st[:, 0:1]
                if j.get("sink") is not None:
                    t = V.tt(st[:, 0:1], st[:, 0:1], j["sink"], ALU.max)
                rel.append(t)
            if biased:
                c0, c1, bias = biased
                src = ps[:, c0:c1]
                if j.get("pre") is not None:
                    cumq, Bk = j["pre"](q)
                    t = V.stt(Pq[:, c0:c1], src, cumq, Bk, ALU.add, ALU.add, tok, free)
                    rel.append(t)
                    src = Pq[:, c0:c1]
                t = V.addmax(Pq[:, c0:c1], src, bias, LOW if m is None else m, st[:, 1:2], tok, free)
                m = st[:, 1:2]
                rel.append(t)
            tn = V.ts1(st[:, 2:3], m, -1.0, ALU.mult)
            nm = st[:, 2:3]
            k = 0
            if plain:
                c0, c1 = plain
                ta = A.act(Pq[:, c0:c1], ps[:, c0:c1], ACT.Exp, tn, free, bias=nm, acc=st[:, 4 + k:5 + k])
                k += 1
                rel.append(ta)
            if biased:
                c0, c1, _ = biased
                ta = A.act(Pq[:, c0:c1], Pq[:, c0:c1], ACT.Exp, tn, bias=nm, acc=st[:, 4 + k:5 + k])
                k += 1
            if j.get("sink") is not None:
                ta = A.act(st[:, 4 + k:5 + k], j["sink"], ACT.Exp, tn, bias=nm)
                k += 1
            V.need(ta)
            for i in range(1, k):
                V.tt(st[:, 4:5], st[:, 4:5], st[:, 4 + i:5 + i], ALU.add)
            V.recip(st[:, 3:4], st[:, 4:5])
            if j.get("gate") is not None:
                V.tt(st[:, 3:4], st[:, 3:4], j["gate"](q), ALU.mult)
            if j.get("valid") is not None and j["valid"](q) is not None:
                c0, c1, _ = biased
                t = V.stt(Pq[:, c0:c1], Pq[:, c0:c1], st[:, 3:4], j["valid"](q), ALU.mult, ALU.mult)
            else:
                cols = []
                if plain:
                    cols.append(plain)
                if biased:
                    cols.append(biased[:2])
                for c0, c1 in cols:
                    t = V.ts1(Pq[:, c0:c1], Pq[:, c0:c1], st[:, 3:4], ALU.mult)
            return rel, t

        def transposes(j, n, kt, rdy):
            pcol, nk, q0, q1, v = j["keys"][kt]
            b = 4 + cnt["t"] % 2
            pt = PT[cnt["t"] % 3]
            slot = cnt["t"] % 3
            cnt["t"] += 1
            PE.need(pf[b], *[rdy[q] for q in range(q0, q1)])
            Pn = j["P"] if "P" in j else P[n % 2]
            for q in range(q0, q1):
                m = nc.tensor.transpose(PS[0:nk, b, q * 128:q * 128 + 128], Pn[q][:, pcol(q):pcol(q) + nk],
                                        ident[:, :])
            tok = PE.done(m)
            pf[b] = order_evac(pt[0:nk, q0 * 128:q1 * 128], PS[0:nk, b, q0 * 128:q1 * 128], tok, free_PT[slot])
            return (j, kt, pt, slot, pf[b], tok)

        def values(x):
            j, kt, pt, slot, ready, _ = x
            pcol, nk, q0, q1, v = j["keys"][kt]
            ob, half = j["out"]
            last = kt == len(j["keys"]) - 1
            PE.need(ready)
            if kt == 0 and j["first"]:
                PE.need(pf[ob])
            m = nc.tensor.matmul(PS[half * 64:half * 64 + 64, ob, q0 * 128:q1 * 128], v,
                                 pt[0:nk, q0 * 128:q1 * 128], start=(kt == 0 and j["first"]),
                                 stop=(last and j["last"]))
            tok = PE.done(m)
            free_PT[slot] = tok
            if last and j.get("final"):
                pf[ob] = j["final"](tok)

        prev = None
        for n in range(len(jobs) + 1):
            a = []
            if n < len(jobs):
                a = [(jobs[n], n, q) for q in range(jobs[n]["nq"])]
            b = []
            if prev is not None:
                b = [(prev[0], n - 1, kt, prev[1]) for kt in range(len(prev[0]["keys"]))]
            rdy = []
            la, lb = len(a), len(b)
            ia = ib = 0
            while ia < la or ib < lb:
                if ia < la and (ib >= lb or ia * lb <= ib * la):
                    rdy.append(scores(*a[ia]))
                    ia += 1
                else:
                    pending.append(transposes(*b[ib]))
                    ib += 1
                    if ib == lb:
                        free_P[(n - 1) % 2] = PE.last()
                    if len(pending) > 1:
                        values(pending.pop(0))
            prev = (jobs[n], rdy) if n < len(jobs) else None
        while pending:
            values(pending.pop(0))

    def grid(base, n, *dims):
        s = 1
        for d in dims:
            s *= d
        return [sb(base + i * s, *dims) for i in range(n)]

    def P_buffers(base):
        f = grid(base, 8, 768)
        return [f[0:4], f[4:8]]

    def modulation(l):
        cc = MQ.go(cT, D["cT"])
        b1 = MQ.go(bada, D["b_adaT"][l])
        b2 = MQ.go(ng, D["norm_gT"][l])
        t = A.act(ctmp, cT, ACT.Tanh, cc, scale=0.5)
        V.stt(ctmp, ctmp, 1.0, cT, ALU.add, ALU.mult, t, cc)
        tc = V.ts1(ctmp, ctmp, 0.5, ALU.mult)
        b = bank()
        PE.need(pf[b], tc)
        for n in range(6):
            w, tw = weight()
            for s in range(4):
                c = (n * 4 + s) * 2
                t = group(PS[:, b, c:c + 2], [(w[:, k, s * 128:s * 128 + 128], ctmp[:, k, :]) for k in range(8)], tw)
            used(t)
        ps = PS[:, b, 0:48].rearrange("p (a b) -> p a b", a=24)
        pf[b] = V.tt(ada, ps, bcast(bada, 2, 2), ALU.add, t, b1)
        V.ts1(aff[:, :, :, 0], ada[:, 8:16, :], 1.0, ALU.add)
        V.tt(aff[:, :, :, 0], aff[:, :, :, 0], bcast(ng, 2, 2), ALU.mult, b2)
        return V.copy(aff[:, :, :, 1], ada[:, 0:8, :])

    def gates(dst, nv, t_mod):
        for v in range(nv):
            for h in range(2):
                b = bank()
                PE.need(pf[b], t_mod)
                for k in range(4):
                    m = nc.tensor.matmul(PS[:, b, k * 128:k * 128 + 128],
                                         ada[:, 16 + h * 4 + k, v:v + 1].to_broadcast([128, 128]), ident[:, :],
                                         start=True, stop=True)
                pf[b] = t = evac(dst[v][:, h * 512:h * 512 + 512], PS[:, b, :], PE.done(m))
        return t

    def normed(hT, xn, junk, tx, t_mod):
        for t in range(6):
            a = A.act(junk, X[:, t, :], ACT.Square, tx, acc=small[:, t:t + 1])
        V.ts(small[:, 0:6], small[:, 0:6], 1.0 / 1024, ALU.mult, EPS, ALU.add, a)
        rsqrt(small[:, 8:14], small[:, 0:6], small[:, 16:22], V.last())
        tn = []
        for t in range(6):
            tn.append(V.ts1(xn[:, t, :], X[:, t, :], small[:, 8 + t:9 + t], ALU.mult))
        toks = []
        for k in range(8):
            for v, ts_ in ((0, range(4)), (1, range(4, 6))):
                b = bank()
                PE.need(pf[b], tn[-1], t_mod)
                for n, t in enumerate(ts_):
                    m = nc.tensor.transpose(PS[:, b, n * 128:n * 128 + 128], xn[:, t, k * 128:k * 128 + 128],
                                            ident[:, :])
                tok = PE.done(m)
                n = len(ts_) * 128
                rot["e"] ^= 1
                if rot["e"]:
                    pf[b] = V.ts(hT[:, k, v * 512:v * 512 + n], PS[:, b, 0:n], aff[:, k, v, 0:1], ALU.mult,
                                 aff[:, k, v, 1:2], ALU.add, tok)
                else:
                    pf[b] = A.act(hT[:, k, v * 512:v * 512 + n], PS[:, b, 0:n], ACT.Identity, tok, t_mod,
                                  scale=aff[:, k, v, 0:1], bias=aff[:, k, v, 1:2])
                toks.append(pf[b])
        return [V.last(), A.last()]

    def project(w, tw, kt, c0, n, hT, tiles, dst_of, evacuate=evac, *after):
        for t in tiles:
            b = bank()
            tok = group(PS[:, b, 0:n], [(hT[:, k, t * 128:t * 128 + 128], w[:, k, c0:c0 + n]) for k in range(kt)],
                        pf[b], tw, *after)
            pf[b] = evacuate(dst_of(t), PS[:, b, 0:n], tok)
        return tok

    def project_T(w, tw, kt, c0, m, hT, spans, evacuate, *after):
        for t0, n in spans:
            b = bank()
            tok = group(PS[0:m, b, 0:n], [(w[:, k, c0:c0 + m], hT[:, k, t0:t0 + n]) for k in range(kt)],
                        pf[b], tw, *after)
            pf[b] = evacuate(t0, n, PS[0:m, b, 0:n], tok)
        return tok

    def silu2_T(dst, tmp):
        def ev(t0, n, ps, tok):
            a = A.act(tmp[:, 0:n], ps, ACT.Tanh, tok, V.last(), scale=0.5)
            return V.stt(dst[:, t0:t0 + n], tmp[:, 0:n], 1.0, ps, ALU.add, ALU.mult, a)
        return ev

    def head_norm(Q, tiles, nh, g, tg, tmp, qscale_heads, *after):
        ss, rr, t1 = small[:, 0:6 * nh], small[:, 128:128 + 6 * nh], small[:, 256:256 + 6 * nh]
        V.need(*after)
        for t in tiles:
            q = Q(t)
            V.tt(tmp[:, 0:nh * 64], q, q, ALU.mult)
            V.red(ss[:, t * nh:t * nh + nh], tmp[:, 0:nh * 64].rearrange("p (h d) -> p h d", d=64), ALU.add)
        a, b = tiles[0] * nh, (tiles[-1] + 1) * nh
        V.ts(ss[:, a:b], ss[:, a:b], 1.0 / 64, ALU.mult, EPS, ALU.add)
        rsqrt(rr[:, a:b], ss[:, a:b], t1[:, a:b], V.last())
        if qscale_heads:
            r3 = rr[:, a:b].rearrange("p (t h) -> p t h", h=nh)[:, :, 0:qscale_heads]
            V.ts1(r3, r3, 0.125, ALU.mult)
        for t in tiles:
            q = Q(t).rearrange("p (h d) -> p h d", d=64)
            V.tt(q, q, bcast(rr[:, t * nh:t * nh + nh], 2, 64), ALU.mult)
            V.tt(Q(t), Q(t), g, ALU.mult, tg)
        return V.last()

    def rope_pairs(Q, tiles, nh, tmp):
        for t in tiles:
            q = Q(t).rearrange("p (h d two) -> p h d two", d=32, two=2)
            x0, x1 = q[:, :, :, 0], q[:, :, :, 1]
            c, s = bcast(cos1[:, t, :], 1, nh), bcast(sin1[:, t, :], 1, nh)
            u = [tmp[:, i * nh * 32:(i + 1) * nh * 32].rearrange("p (h d) -> p h d", d=32) for i in range(4)]
            V.tt(u[0], x0, c, ALU.mult)
            V.tt(u[1], x1, s, ALU.mult)
            V.tt(u[2], x0, s, ALU.mult)
            V.tt(u[3], x1, c, ALU.mult)
            V.tt(x0, u[0], u[1], ALU.subtract)
            V.tt(x1, u[2], u[3], ALU.add)
        return V.last()

    def swap(dst, src, *after):
        return [MQ.go(dst[0:64], src[64:128], *after), MQ.go(dst[64:128], src[0:64], *after)]

    def out_proj(yT, nt, GB, t_ready, tmp):
        for n in range(2):
            w, tw = weight()
            for t in range(nt):
                b = bank()
                tok = group(PS[:, b, :], [(yT[:, k, t * 128:t * 128 + 128], w[:, k, :]) for k in range(8)],
                            pf[b], tw, *t_ready)
                x = X[:, t, n * 512:n * 512 + 512]
                u = tmp[t % 2]
                pf[b] = V.tt(u, PS[:, b, :], GB[0 if t < 4 else 1][:, n * 512:n * 512 + 512], ALU.mult, tok,
                             G.last() if G.n else None)
                G.tt(x, x, u, ALU.add, pf[b])
            used(tok)

    x_d, ctx_d = D["x"], D["ctx"]

    def load_x(*after):
        return [MQ.go(X[:, 0:4, :], x_d.rearrange("(t p) d -> p t d", p=128), *after),
                MQ.go(X[:, 4:6, :], ctx_d.rearrange("(t p) d -> p t d", p=128), *after)]

    tx = load_x()
    t_mod = modulation(0)
    hT = sb(BIG, 8, 768)
    yT = sb(BIG + 6144, 8, 768)
    QKV = sb(BIG + 12288, 6, 768)
    qT = sb(BIG + 16896, 5, 768)
    kS = sb(BIG + 20736, 768)
    PB = BIG + 21504
    xn = sb(PB, 6, 1024)
    t_h = normed(hT, xn, sb(BIG + 12288, 1024), tx, t_mod)
    barrier()
    g10 = sb(PB, 640)
    tmp10 = sb(PB + 640, 1280)
    tg = MQ.go(g10, bcast(D["g10_0"], 0, 128), *barrier())
    w, tw = weight()
    used(project(w, tw, 8, 0, 512, hT, range(6), lambda t: QKV[:, t, 0:512]))
    w, tw = weight()
    used(project(w, tw, 8, 0, 256, hT, range(6), lambda t: QKV[:, t, 512:768]))
    head_norm(lambda t: QKV[:, t, 0:640], range(6), 10, g10, tg, tmp10, 8, A.last(), V.last())
    t_q = rope_pairs(lambda t: QKV[:, t, 0:640], range(4), 10, tmp10)
    w, tw = weight()
    for j in range(4):
        tok = project_T(w, tw, 8, j * 128, 128, hT, [(0, 512), (512, 256)], silu2_T(yT[:, j, :], tmp10))
    used(tok)
    flip(lambda j: qT[:, j, 0:512], lambda j, t: QKV[:, t, j * 128:j * 128 + 128], range(4), range(5), after=[t_q])
    flip(lambda j: qT[:, j, 512:768], lambda j, t: QKV[:, t, j * 128:j * 128 + 128], range(4, 6), range(5))
    f = barrier()
    t_s = swap(kS, qT[:, 4, :], *f)
    P, PT = P_buffers(PB), grid(PB + 6144, 3, 512)

    def yfinal(pair, c0, n, ob):
        def final(tok):
            return V.stt(yT[:, pair, c0:c0 + n], PS[:, ob, 0:n], 0.5, yT[:, pair, c0:c0 + n], ALU.mult, ALU.mult, tok)
        return final

    jobs = []
    for pair in range(4):
        for half in range(2):
            h = pair * 2 + half
            g = h // 4
            ksrc = qT[:, 4, :] if g == half else kS
            lo = half * 64

            def sc(q, pair=pair, lo=lo, ksrc=ksrc):
                l = qT[lo:lo + 64, pair, q * 128:q * 128 + 128]
                return [(0, 512, l, ksrc[lo:lo + 64, 0:512]), (512, 256, l, ksrc[lo:lo + 64, 512:768])]
            ob = 6 + pair % 2
            jobs.append(dict(nq=4, scores=sc, segs=lambda q: ((0, 768), None), out=(ob, half), first=True,
                             last=True, after=t_s,
                             keys=[(lambda q, c=kt * 128: c, 128, 0, 4, QKV[:, kt, 640 + g * 64:704 + g * 64])
                                   for kt in range(6)],
                             final=yfinal(pair, 0, 512, ob) if half else None))
    for pair in range(4):
        for half in range(2):
            h = pair * 2 + half
            g = h // 4
            ksrc = qT[:, 4, :] if g == half else kS
            lo = half * 64

            def sc(q, pair=pair, lo=lo, ksrc=ksrc):
                l = qT[lo:lo + 64, pair, 512 + q * 128:640 + q * 128]
                return [(512, 256, l, ksrc[lo:lo + 64, 512:768])]
            ob = 6 + pair % 2
            jobs.append(dict(nq=2, scores=sc, segs=lambda q: ((512, 768), None), out=(ob, half), first=True,
                             last=True,
                             keys=[(lambda q, c=kt * 128: c, 128, 0, 2, QKV[:, kt, 640 + g * 64:704 + g * 64])
                                   for kt in (4, 5)],
                             final=yfinal(pair, 512, 256, ob) if half else None))
    attention(jobs, P, PT)
    f = barrier()

    UC = sb(BIG + 12288, 6, 1536)
    uct = grid(BIG + 21504, 2, 768)
    gtmp = sb(BIG + 23040, 512)
    cw = sb(BIG + 23600, 12, 4)
    tcw = MQ.go(cw, D["convT"], *f)
    V.need(tcw)
    A.need(tcw)
    free_u = [None, None]
    for n in range(3):
        w, tw = weight()
        for s in range(4):
            ct = n * 4 + s
            u = uct[ct % 2]
            toks = []
            for t0, nn in ((0, 512), (512, 256)):
                b = bank()
                tok = group(PS[:, b, 0:nn], [(w[:, k, s * 128:s * 128 + 128], hT[:, k, t0:t0 + nn]) for k in range(8)],
                            pf[b], tw)
                a = A.act(u[:, t0:t0 + nn], PS[:, b, 0:nn], ACT.Identity, tok, free_u[ct % 2],
                          scale=cw[:, ct, 1:2], bias=cw[:, ct, 3:4])
                V.stt(u[:, t0 + 1:t0 + nn], PS[:, b, 0:nn - 1], cw[:, ct, 0:1], u[:, t0 + 1:t0 + nn],
                      ALU.mult, ALU.add, a)
                pf[b] = V.stt(u[:, t0:t0 + nn - 1], PS[:, b, 1:nn], cw[:, ct, 2:3], u[:, t0:t0 + nn - 1],
                              ALU.mult, ALU.add)
            if s == 3:
                used(tok)
            for t0, nt in ((0, 4), (4, 2)):
                b = bank()
                PE.need(pf[b], V.last())
                for t in range(nt):
                    m = nc.tensor.transpose(PS[:, b, t * 128:t * 128 + 128], u[:, (t0 + t) * 128:(t0 + t + 1) * 128],
                                            ident[:, :])
                tok = PE.done(m)
                pf[b] = evac(UC[:, t0:t0 + nt, ct * 128:ct * 128 + 128],
                             PS[:, b, 0:nt * 128].rearrange("p (t c) -> p t c", t=nt), tok)
            free_u[ct % 2] = tok
    w, tw = weight()
    for j in range(4):
        tok = project_T(w, tw, 8, j * 128, 128, hT, [(0, 512), (512, 256)], silu2_T(yT[:, 4 + j, :], gtmp))
    used(tok)
    f = barrier()

    TR, TI = sb(BIG, 4, 512), sb(BIG + 2048, 4, 512)
    tr, ti = sb(BIG + 4096, 2, 512), sb(BIG + 5120, 2, 512)
    ZR, ZI = sb(BIG + 21504, 4, 512), sb(BIG + 23552, 4, 512)
    zr, zi = sb(BIG + 25600, 2, 512), sb(BIG + 26624, 2, 512)
    tmpa, tmpb = sb(BIG + 27648, 512), sb(BIG + 28160, 512)
    w3 = sb(XR, 2048)
    h2 = sb(XR + 2048, 768)
    zt = sb(XR + 2816, 768)
    hw = sb(XR + 3584, 192)
    dec = grid(XR + 3776, 2, 512)
    dsk = sb(XR + 4800, 512)
    sc1, sc2 = sb(XR + 5312, 512), sb(BIG + 28672, 512)
    t1 = MQ.go(w3[0:64], D["hy_w3"], *f)
    t2 = MQ.go(zt[0:33], D["hyz"], *f)
    t3 = MQ.go(hw[0:33, 0:64], D["hy_w1"], *f)
    t4 = MQ.go(hw[0:64, 64:128], D["hy_w2"], *f)
    t5 = MQ.go(hw[0:64, 128:131], D["hyb"], *f)
    for e in (PE, V, A):
        e.need(t1, t2, t3, t4, t5)

    def wrapped_sin(dst, src, bcol, tok, n):
        x, k = tmpa[0:64, 0:n], tmpb[0:64, 0:n]
        rel = V.ts(x, src, bcol, ALU.add, hw[0:64, 128:129], ALU.mult, tok)
        V.ts(k, x, 1.0 / (2 * math.pi), ALU.mult, 12582912.0, ALU.add)
        V.ts1(k, k, 12582912.0, ALU.subtract)
        V.stt(x, k, -6.28125, x, ALU.mult, ALU.add)
        V.stt(x, k, -(2 * math.pi - 6.28125), x, ALU.mult, ALU.add)
        V.ts(x, x, 3.1415925, ALU.min, -3.1415925, ALU.max)
        return rel, A.act(dst, x, ACT.Sin, V.last())

    for a0, n in ((0, 512), (512, 256)):
        b = bank()
        tok = group(PS[0:64, b, 0:n], [(hw[0:33, 0:64], zt[0:33, a0:a0 + n])], pf[b])
        pf[b], t = wrapped_sin(h2[0:64, a0:a0 + n], PS[0:64, b, 0:n], hw[0:64, 129:130], tok, n)
        b = bank()
        tok = group(PS[0:64, b, 0:n], [(hw[0:64, 64:128], h2[0:64, a0:a0 + n])], pf[b], t)
        pf[b], t = wrapped_sin(h2[0:64, a0:a0 + n], PS[0:64, b, 0:n], hw[0:64, 130:131], tok, n)
        V.need(t)

    def spectrum(w, tw, o, nt, st, s_, d_, Tr, Ti, scl, a0, decay):
        PE.need(A.last())
        td = []
        for t in range(nt):
            td.append(MQ.go(dec[t % 2], decay[t * 128:t * 128 + 128, :], V.last()))
            for side in range(2):
                b = bank()
                c = (o * 2 + side) * 512
                tok = group(PS[:, b, :], [(h2[0:64, a0 + t * 128:a0 + t * 128 + 128], w3[0:64, c:c + 512])], pf[b],
                            V.last())
                dst = (tmpa, tmpb)[side]
                pf[b] = V.tt(dst, PS[:, b, :], dec[t % 2], ALU.mult, tok, td[t])
            if t == 0:
                V.zero(tmpb[0:1, :], 0.0)
            V.tt(s_[:, t, :], tmpa, tmpb, ALU.add)
            V.tt(d_[:, t, :], tmpa, tmpb, ALU.subtract)
        b = bank()
        PE.need(pf[b])
        for t in range(nt):
            V.tt(tmpa, s_[:, t, :], s_[:, t, :], ALU.mult, PE.last())
            x = V.tt(tmpb, d_[:, t, :], d_[:, t, :], ALU.mult)
            PE.need(x)
            nc.tensor.matmul(PS[:, b, :], ones[:, :], tmpa, start=(t == 0), stop=False)
            PE.done(nc.tensor.matmul(PS[:, b, :], ones[:, :], tmpb, start=False, stop=(t == nt - 1)))
        V.ts(tmpa, PS[:, b, :], 0.5, ALU.mult, EPS, ALU.add, PE.last())
        pf[b] = V.last()
        rsqrt(scl, tmpa, tmpb, V.last())
        if nt == 2:
            V.ts1(scl, scl, 2.0, ALU.mult)
        for k in range(nt):
            for src, dst, half in ((s_, Tr, 0), (d_, Ti, 512)):
                b = bank()
                tok = group(PS[:, b, :], [(w[:, t, half + k * 128 * st:half + (k + 1) * 128 * st:st], src[:, t, :])
                                          for t in range(nt)], pf[b], tw)
                pf[b] = evac(dst[:, k, :], PS[:, b, :], tok)
        b = bank()
        tok = group(PS[0:1, b, :], [(w[:, t, 512:513], s_[:, t, :]) for t in range(nt)], pf[b])
        pf[b] = V.copy(Ti[0:1, 0, :], PS[0:1, b, :], tok, A.last())
        return tok

    def forward(w, tw, nt, st, t0, Zr, Zi):
        for k in range(nt):
            for dst, half in ((Zr, 0), (Zi, 512)):
                b = bank()
                tok = group(PS[:, b, :], [(w[:, t, half + k * 128 * st:half + (k + 1) * 128 * st:st],
                                           UC[:, t0 + t, 0:512]) for t in range(nt)], pf[b], tw, V.last(), G.last())
                pf[b] = evac(dst[:, k, :], PS[:, b, :], tok)
        return tok

    def multiply(nt, Zr, Zi, Tr, Ti):
        V.need(A.last())
        for k in range(nt):
            if k == 0:
                V.tt(small[0:1, 0:512], Zr[0:1, 0, :], Tr[0:1, 0, :], ALU.mult)
                V.tt(sc3[0:1, :], Zi[0:1, 0, :], Ti[0:1, 0, :], ALU.mult)
            V.tt(tmpa, Zr[:, k, :], Tr[:, k, :], ALU.mult)
            g = G.tt(tmpb, Zr[:, k, :], Ti[:, k, :], ALU.mult, V.last())
            V.tt(sc4, Zi[:, k, :], Tr[:, k, :], ALU.mult)
            V.tt(Zi[:, k, :], Zi[:, k, :], Ti[:, k, :], ALU.mult)
            V.tt(Zr[:, k, :], tmpa, Zi[:, k, :], ALU.subtract, g)
            V.tt(Zi[:, k, :], tmpb, sc4, ALU.add)
            if k == 0:
                V.copy(Zr[0:1, 0, :], small[0:1, 0:512])
                V.copy(Zi[0:1, 0, :], sc3[0:1, :])
        return V.last()

    sc3, sc4 = sb(BIG + 29184, 512), sb(BIG + 29696, 512)

    def inverse(lhs, nt, t0, o, Zr, Zi, scl, tw, tz):
        for t in range(nt):
            b = bank()
            pairs = [(lhs(0, k, t), Zr[:, k, :]) for k in range(nt)] + [(lhs(1, k, t), Zi[:, k, :]) for k in range(nt)]
            tok = group(PS[:, b, :], pairs, pf[b], tw, tz)
            z = UC[:, t0 + t, 0:512]
            pf[b] = V.tt(tmpa, PS[:, b, :], scl, ALU.mult, tok)
            V.tt(tmpb, z, dsk, ALU.mult)
            V.tt(tmpa, tmpa, tmpb, ALU.add)
            V.tt(z, tmpa, UC[:, t0 + t, (o + 1) * 512:(o + 2) * 512], ALU.mult)
        return tok

    for o in range(2):
        f = barrier()
        tds = MQ.go(dsk, bcast(D["hy_skip"][o], 0, 128), *f)
        V.need(tds)
        w, tw = weight()
        spectrum(w, tw, o, 4, 1, ZR, ZI, TR, TI, sc1, 0, D["decay1"])
        spectrum(w, tw, o, 2, 2, zr, zi, tr, ti, sc2, 512, D["decay2"])
        barrier()
        forward(w, tw, 4, 1, 0, ZR, ZI)
        used(forward(w, tw, 2, 2, 4, zr, zi))
        tz = multiply(4, ZR, ZI, TR, TI)
        w, tw = weight()
        t = inverse(lambda part, k, t, w=w: w[:, part * 4 + k, t * 128:t * 128 + 128], 4, 0, o, ZR, ZI, sc1, tw, tz)
        tz = multiply(2, zr, zi, tr, ti)

        def lhs2(part, k, t, w=w):
            if part == 0:
                return w[:, k, t * 256:t * 256 + 256:2]
            if k == 0:
                return g2i[:, 0, t * 128:t * 128 + 128]
            return w[:, 4 + k, t * 256:t * 256 + 256:2]
        used(inverse(lhs2, 2, 4, o, zr, zi, sc2, tw, tz))
    f = barrier()
    tx = load_x(*f)
    for j in range(4):
        for c0, nt, t0 in ((0, 4, 0), (512, 2, 4)):
            b = bank()
            PE.need(pf[b])
            for t in range(nt):
                m = nc.tensor.transpose(PS[:, b, t * 128:t * 128 + 128], UC[:, t0 + t, j * 128:j * 128 + 128],
                                        ident[:, :])
            y = yT[:, 4 + j, c0:c0 + nt * 128]
            pf[b] = V.stt(y, PS[:, b, 0:nt * 128], 0.5, y, ALU.mult, ALU.mult, PE.done(m))
    GB = [sb(BIG, 1024), sb(BIG + 1024, 1024)]
    tmp = grid(BIG + 2048, 2, 512)
    gates(GB, 2, None)
    V.need(*tx)
    G.need(*tx)
    out_proj(yT, 6, GB, [V.last(), A.last()], tmp)
    f = barrier()

    t_mod = modulation(1)
    hT = sb(BIG, 8, 768)
    yT = sb(BIG + 6144, 8, 512)
    QKV = sb(BIG + 10240, 6, 768)
    qTw = sb(BIG + 14848, 4, 512)
    kTw = sb(BIG + 16896, 768)
    kS = sb(BIG + 17664, 768)
    PB = BIG + 18432
    g10 = sb(PB, 640)
    tmp10 = sb(PB + 640, 1280)
    normed(hT, sb(PB, 6, 1024), sb(BIG + 10240, 1024), None, t_mod)
    f = barrier()
    tg = MQ.go(g10, bcast(D["g10_1"], 0, 128), *f)
    w, tw = weight()
    used(project(w, tw, 8, 0, 512, hT, range(4), lambda t: QKV[:, t, 0:512]))
    w, tw = weight()
    used(project(w, tw, 8, 0, 256, hT, range(6), lambda t: QKV[:, t, 512:768]))
    f = barrier()
    head_norm(lambda t: QKV[:, t, 0:640], range(4), 10, g10, tg, tmp10, 8)
    head_norm(lambda t: QKV[:, t, 512:640], range(4, 6), 2, g10[:, 512:640], tg, tmp10, 0)
    t_q = rope_pairs(lambda t: QKV[:, t, 0:640], range(4), 10, tmp10)
    w, tw = weight()
    for j in range(4):
        tok = project_T(w, tw, 8, j * 128, 128, hT, [(0, 512)], silu2_T(yT[:, j, :], tmp10))
    used(tok)
    flip(lambda j: qTw[:, j, :] if j < 4 else kTw[:, 0:512], lambda j, t: QKV[:, t, j * 128:j * 128 + 128],
         range(4), range(5), after=[t_q])
    flip(lambda j: kTw[:, 512:768], lambda j, t: QKV[:, t, 512:640], range(4, 6), range(1))
    f = barrier()
    t_s = swap(kS, kTw, *f)
    P, PT = P_buffers(PB), grid(PB + 6144, 3, 512)
    wm = sb(PB + 7680, 384)
    sink = sb(PB + 8064, 8)
    t_s.append(MQ.go(wm, D["wmask"], *f))
    t_s.append(MQ.go(sink, bcast(D["win_sink"], 0, 128), *f))
    V.need(*t_s)
    A.need(*t_s)
    jobs = []
    for pair in range(4):
        for half in range(2):
            h = pair * 2 + half
            g = h // 4
            ksrc = kTw if g == half else kS
            lo = half * 64

            def span(q):
                return max(0, q - 1), min(4, q + 2)

            def sc(q, pair=pair, lo=lo, ksrc=ksrc):
                l = qTw[lo:lo + 64, pair, q * 128:q * 128 + 128]
                a, b = span(q)
                return [(0, (b - a) * 128, l, ksrc[lo:lo + 64, a * 128:b * 128]),
                        (512, 256, l, ksrc[lo:lo + 64, 512:768])]

            def segs(q):
                a, b = span(q)
                m0 = (a - q + 1) * 128
                return (512, 768), (0, (b - a) * 128, wm[:, m0:m0 + (b - a) * 128])
            ob = 6 + pair % 2
            keys = [(lambda q, c=kt * 128: c, 128, 0, 4, QKV[:, kt, 640 + g * 64:704 + g * 64]) for kt in (4, 5)]
            keys += [(lambda q, kt=kt: (kt - max(0, q - 1)) * 128, 128, max(0, kt - 1), min(4, kt + 2),
                      QKV[:, kt, 640 + g * 64:704 + g * 64]) for kt in range(4)]
            jobs.append(dict(nq=4, scores=sc, segs=segs, out=(ob, half), first=True, last=True, after=t_s,
                             sink=sink[:, h:h + 1], keys=keys, final=yfinal(pair, 0, 512, ob) if half else None))
    attention(jobs, P, PT)
    f = barrier()

    QKV = sb(BIG + 10240, 6, 1536)
    qTn = sb(BIG + 19456, 4, 512)
    kTn = sb(BIG + 21504, 4, 768)
    PTB = BIG + 24576
    g16 = sb(PTB, 1024)
    tmp16 = sb(PTB + 1024, 1024)
    tg = MQ.go(g16, bcast(D["g16"], 0, 128), *f)
    w, tw = weight()
    used(project(w, tw, 8, 0, 512, hT, range(4), lambda t: QKV[:, t, 0:512]))
    w, tw = weight()
    used(project(w, tw, 8, 0, 512, hT, range(6), lambda t: QKV[:, t, 512:1024]))
    w, tw = weight()
    used(project(w, tw, 8, 0, 512, hT, range(6), lambda t: QKV[:, t, 1024:1536]))
    w, tw = weight()
    for j in range(4):
        tok = project_T(w, tw, 8, j * 128, 128, hT, [(0, 512)], silu2_T(yT[:, 4 + j, :], sb(PTB + 2048, 512)))
    used(tok)
    f = barrier()
    head_norm(lambda t: QKV[:, t, 0:1024], range(4), 16, g16, tg, tmp16, 8)
    t_q = head_norm(lambda t: QKV[:, t, 512:1024], range(4, 6), 8, g16[:, 512:1024], tg, tmp16, 0)
    flip(lambda j: qTn[:, j, :] if j < 4 else kTn[:, j - 4, 0:512], lambda j, t: QKV[:, t, j * 128:j * 128 + 128],
         range(4), range(8), after=[t_q])
    flip(lambda j: kTn[:, j, 512:768], lambda j, t: QKV[:, t, 512 + j * 128:640 + j * 128], range(4, 6), range(4))
    f = barrier()
    P, PT = P_buffers(BIG), grid(PTB, 3, 512)
    rp = grid(PTB + 1536, 3, 15, 64)
    cm = sb(PTB + 1536 + 2880, 64)
    tcm = MQ.go(cm, D["cmask"], *f)
    V.need(tcm)
    G.need(tcm)
    rtok = {}

    def load_rpb(h):
        t = MQ.go(rp[h % 3], D["rpx"][h], V.last())
        rtok[h] = G.tt(rp[h % 3], rp[h % 3], bcast(cm, 1, 15), ALU.add, t)
    jobs = []
    for pair in range(4):
        for half in range(2):
            h = pair * 2 + half
            lo = half * 64

            def sc(q, pair=pair, lo=lo, h=h):
                if q == 0:
                    if h == 0:
                        load_rpb(0)
                    if h < 7:
                        load_rpb(h + 1)
                l = qTn[lo:lo + 64, pair, q * 128:q * 128 + 128]
                return [(0, 512, l, kTn[lo:lo + 64, pair, 0:512]), (512, 256, l, kTn[lo:lo + 64, pair, 512:768])]

            def segs(q, h=h):
                V.need(rtok[h])
                s = 7 - 2 * q
                return (512, 768), (0, 512, rp[h % 3][:, s:s + 8, :].rearrange("p a b -> p (a b)"))
            ob = 6 + pair % 2
            jobs.append(dict(nq=4, scores=sc, segs=segs, out=(ob, half), first=True, last=True,
                             keys=[(lambda q, c=kt * 128: c, 128, 0, 4, QKV[:, kt, 1024 + h * 64:1088 + h * 64])
                                   for kt in range(6)],
                             final=yfinal(4 + pair, 0, 512, ob) if half else None))
    attention(jobs, P, PT)
    f = barrier()
    GB = [sb(BIG, 1024)]
    tmp = grid(BIG + 2048, 2, 512)
    gates(GB, 1, None)
    out_proj(yT, 4, GB, [V.last(), A.last()], tmp)
    f = barrier()

    xT = sb(BIG, 8, 512)
    T5 = sb(BIG + 4096, 8, 512)
    oT = sb(BIG + 8192, 8, 512)
    B2 = BIG + 12288
    XT = XR + 4096
    maskT = sb(XT, 512)
    tri = sb(XT + 512, 512)
    vmask = sb(XT + 1024, 8)
    t1 = MQ.go(maskT, D["cmask2"], *f)
    t2 = MQ.go(tri, D["tri"], *f)
    t3 = MQ.go(vmask, D["vmask"], *f)

    tab = sb(B2, 8)
    oh = sb(B2 + 8, 640)
    tabb = grid(B2 + 700, 2, 128)
    ut = grid(B2 + 1000, 2, 640)
    V.zero(tab[0:64, :], NEG)
    t4 = MQ.go(tab[0:32, :], D["t5"], V.last())
    t5_ = MQ.go(oh[0:33, :], D["onehot"], *f)
    scr = nc.dram_tensor("t5_rows", [8, 128 * 640], F32)
    tbs = []
    for h in range(8):
        V.copy(tabb[h % 2][0:33, :], tab[0:33, h:h + 1].to_broadcast([33, 128]), t4, PE.last())
        tk = V.last()
        for c0, n in ((0, 512), (512, 128)):
            b = bank()
            tok = group(PS[:, b, 0:n], [(tabb[h % 2][0:33, :], oh[0:33, c0:c0 + n])], pf[b], tk, t5_)
            pf[b] = V.copy(ut[h % 2][:, c0:c0 + n], PS[:, b, 0:n], tok, tbs[-2] if len(tbs) > 1 else None)
        sv = bass.AP(scr, h * 81920, [[640, 128], [1, 640]])
        tw_ = MQ.go(sv, ut[h % 2], V.last())
        tbs.append(tw_)
        tbs[-1] = tw_
        t6 = MQ.go(T5[:, h, :], bass.AP(scr, h * 81920 + 127, [[639, 128], [1, 512]]), tw_)
        V.need(t6)
    for e in (PE, V, A, G):
        e.need(t1, t2, t3)

    def make_xT(nt=4):
        return flip(lambda k: xT[:, k, :], lambda k, t: X[:, t, k * 128:k * 128 + 128], range(4), range(8))

    def layer_norm(l, i, gb, gtok):
        mv = small
        for t in range(4):
            for h in range(2):
                V.begin(())
                V.done(nc.vector.bn_stats(mv[:, t * 12 + h * 6:t * 12 + h * 6 + 6], X[:, t, h * 512:h * 512 + 512]))
            V.begin(())
            V.done(nc.vector.bn_aggr(mv[:, 64 + t * 2:66 + t * 2], mv[:, t * 12:t * 12 + 12]))
        mean = mv[:, 64:72].rearrange("p (t two) -> p t two", two=2)
        V.ts1(mv[:, 80:84], mean[:, :, 1], LN_EPS, ALU.add)
        rsqrt(mv[:, 84:88], mv[:, 80:84], mv[:, 88:92], V.last())
        for t in range(4):
            x = X[:, t, :]
            V.ts(x, x, mv[:, 64 + 2 * t:65 + 2 * t], ALU.subtract, mv[:, 84 + t:85 + t], ALU.mult)
            V.tt(x, x, gb[0], ALU.mult, gtok)
            V.tt(x, x, gb[1], ALU.add)
        return V.last()

    def load_gb(l, i, at, f):
        gb = [sb(at, 1024), sb(at + 1024, 1024)]
        return gb, [MQ.go(gb[0], bcast(D["ln_g_2"][l, i], 0, 128), *f), MQ.go(gb[1], bcast(D["ln_b_2"][l, i], 0, 128), *f)]

    def residual(lhs_of, kt, nchunk, wcols, ready, l, i, gb_at):
        gb, gtok = load_gb(l, i, gb_at, barrier())
        for n in range(nchunk):
            w, tw = weight()
            for c in range(wcols // 512):
                for t in range(4):
                    b = bank()
                    tok = group(PS[:, b, :], [(lhs_of(k, t), w[:, k, c * 512:c * 512 + 512]) for k in range(kt)],
                                pf[b], tw, *ready)
                    o = (n * (wcols // 512) + c) * 512
                    x = X[:, t, o:o + 512]
                    pf[b] = V.stt(x, x, ALPHA, PS[:, b, :], ALU.mult, ALU.add, tok)
            used(tok)
        t = layer_norm(l, i, gb, gtok)
        return t

    def plain_final(dst, ob):
        return lambda tok: evac(dst, PS[:, ob, :], tok)

    for l in range(2):
        barrier()
        make_xT()
        nqT = sb(B2, 4, 512)
        kkT = sb(B2 + 2048, 4, 512)
        kss = sb(B2 + 4096, 2, 512)
        vv = sb(B2 + 5120, 4, 2, 128)
        gt = sb(B2 + 6144, 4, 24)
        cAB = sb(B2 + 6240, 2, 512)
        pe = sb(B2 + 7264, 2, 32)
        w2 = sb(B2 + 7328, 2, 64)
        hid = sb(B2 + 7456, 2, 64)
        gtmp_ = sb(B2 + 7584, 64)
        kc2 = sb(B2 + 7648, 64)
        vc2 = sb(B2 + 7712, 2, 64)
        kcs = sb(B2 + 7840, 64)
        pcb = sb(B2 + 7904, 2, 4, 32)
        PB = B2 + 8192
        f = barrier()
        tpe = MQ.go(pe, D["peT"][l], *f)
        tw2 = MQ.go(w2, D["cmpw2"][l], *f)
        G.zero(vc2, 0.0)
        G.zero(pcb, 0.0)
        w, tw = weight()
        for j in range(4):
            tok = project_T(w, tw, 8, j * 128, 128, xT, [(0, 512)],
                            lambda t0, n, ps, tok, j=j: evac(nqT[:, j, :], ps, tok, scale=0.125),
                            V.last(), A.last())
        used(tok)
        w, tw = weight()
        for j in range(3):
            tok = project_T(w, tw, 8, j * 128, 128, xT, [(0, 512)],
                            lambda t0, n, ps, tok, j=j: evac(kkT[:, j, :], ps, tok))
        used(project(w, tw, 8, 384, 128, xT, range(4), lambda t: vv[:, t, 0, :]))
        w, tw = weight()
        tok = project_T(w, tw, 8, 0, 128, xT, [(0, 512)], lambda t0, n, ps, tok: evac(kkT[:, 3, :], ps, tok))

        def ev_vg(dst, ps, tok):
            V.copy(dst[0], ps[:, 0:128], tok)
            return V.copy(dst[1], ps[:, 128:152])
        used(project(w, tw, 8, 128, 152, xT, range(4), lambda t: (vv[:, t, 1, :], gt[:, t, :]), ev_vg))
        t = A.act(gt, gt, ACT.Tanh, V.last(), scale=0.5)
        V.ts(gt, gt, 0.5, ALU.mult, 0.5, ALU.add, t)
        t_s = swap(kss[:, 0, :], kkT[:, 2, :], V.last(), A.last()) + swap(kss[:, 1, :], kkT[:, 3, :], V.last(), A.last())
        for kv in range(2):
            V.need(tpe, A.last())
            for half in range(2):
                src = kkT[:, kv, :].rearrange("p (n l) -> p n l", l=16)
                V.tt(cAB[:, half, :].rearrange("p (n l) -> p n l", l=16), src,
                     bcast(pe[:, kv, half * 16:half * 16 + 16], 1, 32), ALU.add, PE.last())
            w, tw = weight()
            hx = hid[:, 0, :].rearrange("p (g c) -> p g c", g=2)[:, :, 0:31]
            hy = hid[:, 1, :].rearrange("p (g c) -> p g c", g=2)[:, :, 0:31]
            gx = gtmp_.rearrange("p (g c) -> p g c", g=2)[:, :, 0:31]
            for g in range(2):
                b = bank()
                pairs = []
                lo = g * 64
                for i in range(32):
                    src = cAB[lo:lo + 64, i // 16, :]
                    pairs.append((w[lo:lo + 64, i, :], src[:, i:i + 16 * 30 + 1:16]))
                tok = group(PS[:, b, 0:31], pairs, pf[b], tw, V.last())
                pf[b] = V.copy(hx[:, g, :], PS[:, b, 0:31], tok)
            used(tok)
            V.tt(hy, hx, hx, ALU.mult)
            V.ts(hy, hy, 0.044715, ALU.mult, 1.0, ALU.add)
            V.tt(hy, hy, hx, ALU.mult)
            t = A.act(hy, hy, ACT.Tanh, V.last(), scale=math.sqrt(2.0 / math.pi))
            V.stt(gx, hy, 1.0, hx, ALU.add, ALU.mult, t)
            V.ts1(gx, gx, 0.5, ALU.mult)
            b = bank()
            if kv == 0:
                for g in range(2):
                    tok = group(PS[g * 64:g * 64 + 64, b, 0:31], [(w2[:, 0, :], gtmp_[:, g * 32:g * 32 + 31])],
                                pf[b], V.last(), tw2)
                pf[b] = V.copy(kc2[:, 0:31], PS[:, b, 0:31], tok)
                t_s += swap(kcs[:, 0:31], kc2[:, 0:31], V.last())
            else:
                for g in range(2):
                    tok = group(PS[0:31, b, g * 64:g * 64 + 64], [(gtmp_[:, g * 32:g * 32 + 31], w2[:, 1, :])],
                                pf[b], V.last(), tw2)
                pf[b] = V.copy(vc2[0:31, :, :], PS[0:31, b, 0:128].rearrange("p (g c) -> p g c", g=2), tok, G.last())
        f = barrier()
        P, PT = P_buffers(PB), grid(PB + 6144, 3, 512)
        gview = gt.rearrange("p t (h b) -> p t h b", b=3)
        jobs = []
        for pair in range(4):
            for half in range(2):
                h = pair * 2 + half
                g = h // 4
                lo = half * 64
                ob = 6 + pair % 2

                def gate(br, h=h):
                    return lambda q: gview[:, q, h, br:br + 1]

                for br in (1, 2, 0):
                    if br:
                        ksrc = kkT[:, 1 + br, :] if g == half else kss[:, br - 1, :]

                        def sc(q, pair=pair, lo=lo, ksrc=ksrc):
                            l = nqT[lo:lo + 64, pair, q * 128:q * 128 + 128]
                            return [(0, (q + 1) * 128, l, ksrc[lo:lo + 64, 0:(q + 1) * 128])]

                        def segs(q, h=h):
                            return None, (0, (q + 1) * 128, T5[:, h, 384 - 128 * q:512])
                        keys = [(lambda q, c=kt * 128: c, 128, kt, 4, vv[:, kt, br - 1, g * 64:g * 64 + 64])
                                for kt in range(4)]
                        jobs.append(dict(nq=4, scores=sc, segs=segs, out=(ob, half), first=br == 1, last=False,
                                         after=t_s, gate=gate(br), keys=keys))
                    else:
                        ksrc = kc2 if g == half else kcs

                        def sc(q, pair=pair, lo=lo, ksrc=ksrc):
                            l = nqT[lo:lo + 64, pair, q * 128:q * 128 + 128]
                            n = min(31, 8 * q + 7)
                            return [(0, n, l, ksrc[lo:lo + 64, 0:n])]

                        def segs(q, h=h):
                            n = min(31, 8 * q + 7)
                            c = 415 - 128 * q
                            return None, (0, n, T5[:, h, c:c + 16 * (n - 1) + 1:16])
                        jobs.append(dict(nq=4, scores=sc, segs=segs, out=(ob, half), first=False, last=True,
                                         gate=gate(0), P=[pcb[:, half, q, :] for q in range(4)],
                                         valid=lambda q: vmask[:, 0:7] if q == 0 else None,
                                         keys=[(lambda q: 0, 32, 0, 4, vc2[0:32, g, :])],
                                         final=plain_final(oT[:, pair, :], ob) if half else None))
        attention(jobs, P, PT)
        f = barrier()

        cq = sb(B2, 4, 544)
        km = sb(B2 + 2176, 4, 384)
        vm = sb(B2 + 3712, 4, 256)
        qmT = sb(B2 + 4736, 4, 512)
        kmT = sb(B2 + 6784, 4, 512)
        PB = B2 + 8832
        qm = sb(PB, 4, 384)
        cT_ = sb(PB + 1536, 4, 512)
        gq = sb(PB + 3584, 512)
        tmpm = sb(PB + 4096, 512)
        tg = MQ.go(gq, bcast(D["mlag"][l], 0, 128), *f)
        w, tw = weight()
        for t in range(4):
            for c0, n in ((0, 384), (384, 160)):
                b = bank()
                tok = group(PS[:, b, 0:n], [(xT[:, k, t * 128:t * 128 + 128], w[:, k, c0:c0 + n]) for k in range(8)],
                            pf[b], tw)
                pf[b] = evac(cq[:, t, c0:c0 + n], PS[:, b, 0:n], tok)
        used(tok)
        V.need(A.last())
        for t in range(4):
            V.tt(tmpm[:, 0:512], cq[:, t, 0:512], cq[:, t, 0:512], ALU.mult)
            V.red(small[:, t:t + 1], tmpm[:, 0:384], ALU.add)
            V.red(small[:, 4 + t:5 + t], tmpm[:, 384:512], ALU.add)
        V.ts(small[:, 0:4], small[:, 0:4], 1.0 / 384, ALU.mult, EPS, ALU.add)
        V.ts(small[:, 4:8], small[:, 4:8], 1.0 / 128, ALU.mult, EPS, ALU.add)
        rsqrt(small[:, 8:16], small[:, 0:8], small[:, 16:24], V.last())
        for t in range(4):
            V.stt(cq[:, t, 0:384], cq[:, t, 0:384], small[:, 8 + t:9 + t], gq[:, 0:384], ALU.mult, ALU.mult, tg)
            V.stt(cq[:, t, 384:512], cq[:, t, 384:512], small[:, 12 + t:13 + t], gq[:, 384:512], ALU.mult, ALU.mult)
        flip(lambda k: cT_[:, k, :], lambda k, t: cq[:, t, k * 128:k * 128 + 128], range(4), range(4),
             after=[V.last()])
        w, tw = weight()
        V.need(A.last())
        used(project(w, tw, 3, 0, 384, cT_, range(4), lambda t: qm[:, t, :],
                     lambda d, s, tok: evac(d, s, tok, scale=96 ** -0.5), V.last(), A.last()))
        w, tw = weight()

        def ev_kv(t, ps, tok):
            v4 = ps.rearrange("p (h c) -> p h c", h=4)
            V.copy(km[:, t, :].rearrange("p (h c) -> p h c", h=4)[:, :, 0:64], v4[:, :, 0:64], tok)
            return V.copy(vm[:, t, :].rearrange("p (h c) -> p h c", h=4), v4[:, :, 64:128])
        used(project(w, tw, 1, 0, 512, cT_[:, 3:4, :], range(4), lambda t: t, ev_kv))
        V.need(A.last())
        for t in range(4):
            kr = cq[:, t, 512:544]
            q4 = qm[:, t, :].rearrange("p (h c) -> p h c", h=4)
            k4 = km[:, t, :].rearrange("p (h c) -> p h c", h=4)
            c, s = cos2[:, t, :], sin2[:, t, :]
            c4, s4 = bcast(c, 1, 4), bcast(s, 1, 4)
            u = [tmpm[:, i * 64:(i + 1) * 64].rearrange("p (h d) -> p h d", h=4) for i in range(4)]
            a, b_ = q4[:, :, 64:80], q4[:, :, 80:96]
            V.tt(u[0], a, c4, ALU.mult)
            V.tt(u[1], b_, s4, ALU.mult)
            V.tt(u[2], a, s4, ALU.mult)
            V.tt(u[3], b_, c4, ALU.mult)
            V.tt(a, u[0], u[1], ALU.subtract)
            V.tt(b_, u[2], u[3], ALU.add)
            r = [tmpm[:, 256 + i * 16:272 + i * 16] for i in range(6)]
            V.tt(r[0], kr[:, 0:16], c, ALU.mult)
            V.tt(r[1], kr[:, 16:32], s, ALU.mult)
            V.tt(r[2], kr[:, 0:16], s, ALU.mult)
            V.tt(r[3], kr[:, 16:32], c, ALU.mult)
            V.tt(r[4], r[0], r[1], ALU.subtract)
            V.tt(r[5], r[2], r[3], ALU.add)
            V.copy(k4[:, :, 64:96], bcast(tmpm[:, 320:352], 1, 4))
        flip(lambda h: qmT[0:96, h, :], lambda h, t: qm[:, t, h * 96:h * 96 + 96], range(4), range(4), m=96,
             after=[V.last()])
        flip(lambda h: kmT[0:96, h, :], lambda h, t: km[:, t, h * 96:h * 96 + 96], range(4), range(4), m=96)
        barrier()
        P, PT = P_buffers(PB), None
        PT = grid(XT + 1040, 1, 512) + grid(B2 + 0, 2, 512)
        jobs = []
        for h in range(4):
            half, ob = h % 2, 6 + h // 2

            def sc(q, h=h):
                return [(0, (q + 1) * 128, qmT[0:96, h, q * 128:q * 128 + 128], kmT[0:96, h, 0:(q + 1) * 128])]
            jobs.append(dict(nq=4, scores=sc,
                             segs=lambda q: (None, (0, (q + 1) * 128, maskT[:, 384 - 128 * q:512])),
                             out=(ob, half), first=True, last=True,
                             keys=[(lambda q, c=kt * 128: c, 128, kt, 4, vm[:, kt, h * 64:h * 64 + 64])
                                   for kt in range(4)],
                             final=plain_final(oT[:, 4 + h // 2, :], ob) if half else None))
        attention(jobs, P, PT)
        f = barrier()

        fqT = sb(B2, 4, 512)
        fv = sb(B2 + 2048, 4, 256)
        ff = sb(B2 + 3072, 4, 4)
        lsn = sb(B2 + 3088, 4, 4)
        cum = sb(B2 + 3104, 4, 4)
        ft = sb(B2 + 3120, 16)
        bf = sb(B2 + 3140, 4)
        Bk = sb(B2 + 3200, 4, 512)
        PB = B2 + 5248
        tbf = MQ.go(bf, bcast(D["fox_b_f_2"][l], 0, 128), *f)
        w, tw = weight()
        for j in range(4):
            tok = project_T(w, tw, 8, j * 128, 128, xT, [(0, 512)],
                            lambda t0, n, ps, tok, j=j: evac(fqT[:, j, :], ps, tok, scale=0.125 if j < 2 else None))
        used(tok)
        w, tw = weight()

        def ev_fv(t, ps, tok):
            V.copy(fv[:, t, :], ps[:, 0:256], tok)
            return V.tt(ff[:, t, :], ps[:, 256:260], bf, ALU.add, tbf)
        used(project(w, tw, 8, 0, 260, xT, range(4), lambda t: t, ev_fv))
        fl = ff.rearrange("p a b -> p (a b)")
        ll = lsn.rearrange("p a b -> p (a b)")
        V.stt(ft, fl, -1.0, fl, ALU.mult, ALU.max)
        t = A.act(ft, ft, ACT.Exp, V.last(), scale=-1.0)
        t = A.act(ft, ft, ACT.Ln, bias=ones[:, 0:1])
        V.stt(ll, fl, 0.0, ft, ALU.min, ALU.subtract, t)
        for i in range(4):
            b = bank()
            tok = group(PS[:, b, 0:4], [(tri[:, (i - j) * 128:(i - j) * 128 + 128], lsn[:, j, :])
                                        for j in range(i + 1)], pf[b], V.last())
            pf[b] = V.copy(cum[:, i, :], PS[:, b, 0:4], tok)
        V.ts1(ll, ll, -1.0, ALU.mult, PE.last())
        for h in range(4):
            b = bank()
            PE.need(pf[b], V.last())
            for j in range(4):
                m = nc.tensor.matmul(PS[:, b, 128 * j:512], lsn[:, j, h:h + 1].to_broadcast([128, 128]),
                                     tri[:, 0:512 - 128 * j], start=(j == 0), stop=(j == 3))
            pf[b] = evac(Bk[:, h, :], PS[:, b, :], PE.done(m))
        f = barrier()
        P, PT = P_buffers(PB), grid(PB + 6144, 3, 512)
        jobs = []
        for h in range(4):
            half, ob, lo = h % 2, 6 + h // 2, (h % 2) * 64

            def sc(q, h=h, lo=lo):
                return [(0, (q + 1) * 128, fqT[lo:lo + 64, h // 2, q * 128:q * 128 + 128],
                         fqT[lo:lo + 64, 2 + h // 2, 0:(q + 1) * 128])]
            jobs.append(dict(nq=4, scores=sc,
                             segs=lambda q: (None, (0, (q + 1) * 128, maskT[:, 384 - 128 * q:512])),
                             pre=lambda q, h=h: (cum[:, q, h:h + 1], Bk[:, h, 0:(q + 1) * 128]),
                             out=(ob, half), first=True, last=True,
                             keys=[(lambda q, c=kt * 128: c, 128, kt, 4, fv[:, kt, h * 64:h * 64 + 64])
                                   for kt in range(4)],
                             final=plain_final(oT[:, 6 + h // 2, :], ob) if half else None))
        attention(jobs, P, PT)
        f = barrier()

        mg = sb(B2, 8, 512)
        brv = sb(B2 + 4096, 8, 512)
        gm = grid(B2 + 8192, 2, 512)
        for br, k0, kt in ((0, 0, 4), (1, 4, 2), (2, 6, 2)):
            w, tw = weight()
            for m_ in range(8):
                tok = project_T(w, tw, kt, m_ * 128, 128, oT[:, k0:k0 + kt, :], [(0, 512)],
                                lambda t0, n, ps, tok, m_=m_: evac(brv[:, m_, :], ps, tok, V.last(), G.last()))
            used(tok)
            for n in range(2):
                w, tw = weight()
                for s in range(4):
                    m_ = n * 4 + s
                    gmb = gm[m_ % 2]

                    def ev(t0, nn, ps, tok, m_=m_, gmb=gmb, br=br):
                        a = A.act(gmb, ps, ACT.Tanh, tok, V.last(), G.last(), scale=0.5)
                        V.need(A.last())
                        if br == 0:
                            V.stt(mg[:, m_, :], gmb, 1.0, brv[:, m_, :], ALU.add, ALU.mult, a)
                        else:
                            V.stt(gmb, gmb, 1.0, brv[:, m_, :], ALU.add, ALU.mult, a)
                            G.tt(mg[:, m_, :], mg[:, m_, :], gmb, ALU.add, V.last())
                        return a
                    tok = project_T(w, tw, 8, s * 128, 128, xT, [(0, 512)], ev)
                used(tok)
        V.need(G.last())
        V.ts1(mg, mg, 0.5, ALU.mult)
        residual(lambda k, t: mg[:, k, t * 128:t * 128 + 128], 8, 2, 512, [V.last()], l, 0, B2 + 9300)
        f = barrier()
        make_xT()
        mem = sb(B2, 2, 1024)
        memT = sb(B2 + 2048, 8, 256)
        qa = sb(B2 + 4096, 2, 512)
        ka = sb(B2 + 5120, 2, 256)
        va = sb(B2 + 5632, 2, 256)
        PB = B2 + 6144
        tm = MQ.go(mem, D["mem_2"].rearrange("(t p) d -> p t d", p=128), *f)
        for k in range(8):
            b = bank()
            PE.need(pf[b], tm)
            for t in range(2):
                m = nc.tensor.transpose(PS[:, b, t * 128:t * 128 + 128], mem[:, t, k * 128:k * 128 + 128], ident[:, :])
            pf[b] = evac(memT[:, k, :], PS[:, b, 0:256], PE.done(m))
        w, tw = weight()
        for j in range(2):
            tok = project_T(w, tw, 8, j * 128, 128, xT, [(0, 512)],
                            lambda t0, n, ps, tok, j=j: evac(qa[:, j, :], ps, tok, scale=0.125), V.last(), A.last())
        used(tok)
        w, tw = weight()
        for j in range(2):
            tok = project_T(w, tw, 8, j * 128, 128, memT, [(0, 256)],
                            lambda t0, n, ps, tok, j=j: evac(ka[:, j, :], ps, tok))
        used(project(w, tw, 8, 256, 256, memT, range(2), lambda t: va[:, t, :]))
        barrier()
        P, PT = P_buffers(PB), grid(B2, 3, 512)
        jobs = []
        for h in range(4):
            half, ob, lo = h % 2, 6 + h // 2, (h % 2) * 64

            def sc(q, h=h, lo=lo):
                return [(0, 256, qa[lo:lo + 64, h // 2, q * 128:q * 128 + 128], ka[lo:lo + 64, h // 2, :])]
            jobs.append(dict(nq=4, scores=sc, segs=lambda q: ((0, 256), None), out=(ob, half), first=True,
                             last=True,
                             keys=[(lambda q, c=kt * 128: c, 128, 0, 4, va[:, kt, h * 64:h * 64 + 64])
                                   for kt in range(2)],
                             final=plain_final(oT[:, h // 2, :], ob) if half else None))
        attention(jobs, P, PT)
        barrier()
        residual(lambda k, t: oT[:, k, t * 128:t * 128 + 128], 2, 1, 1024, [V.last()], l, 1, B2)
        f = barrier()
        make_xT()
        hd = sb(BIG + 8192, 32, 512)
        rl = grid(BIG + 8192 + 16384, 2, 512)
        gb, gtok = load_gb(l, 2, BIG + 8192 + 17408, barrier())
        for n in range(8):
            w, tw = weight()
            for s in range(4):
                j = n * 4 + s

                def ev(t0, nn, ps, tok, j=j):
                    a = A.act(rl[j % 2], ps, ACT.Relu, tok, V.last())
                    V.tt(hd[:, j, :], rl[j % 2], rl[j % 2], ALU.mult, a)
                    return a
                tok = project_T(w, tw, 8, s * 128, 128, xT, [(0, 512)], ev)
            used(tok)
        for n in range(2):
            bs = [bank() for _ in range(4)]
            for r in range(4):
                w, tw = weight()
                for t in range(4):
                    b = bs[t]
                    PE.need(tw, V.last(), pf[b] if r == 0 else None)
                    for k in range(8):
                        m = nc.tensor.matmul(PS[:, b, :], hd[:, r * 8 + k, t * 128:t * 128 + 128], w[:, k, :],
                                             start=(r == 0 and k == 0), stop=(r == 3 and k == 7))
                    tok = PE.done(m)
                    if r == 3:
                        x = X[:, t, n * 512:n * 512 + 512]
                        pf[b] = V.stt(x, x, ALPHA, PS[:, b, :], ALU.mult, ALU.add, tok)
                used(tok)
        t = layer_norm(l, 2, gb, gtok)
    t = MQ.go(out.rearrange("(t p) d -> p t d", p=128), X[:, 0:4, :], t)
    barrier()
    for s, v in zip(MQ.sems, MQ.vals):
        G.need((s, v))
    for s, v in zip(WQ.sems, WQ.vals):
        WQ.w.need((s, v))


def constants():
    f = np.float32
    c = {"ident": np.eye(128, dtype=f)}
    t = np.arange(512)
    inv = (f(10000.0) ** (-np.arange(16, dtype=f) / f(16))).astype(f)
    ang = np.concatenate([(t // 64).astype(f)[:, None] * inv, (t % 64).astype(f)[:, None] * inv], -1)
    c["cos1"], c["sin1"] = np.cos(ang).astype(f), np.sin(ang).astype(f)
    ang = t.astype(f)[:, None] * inv[None, :]
    c["cos2"], c["sin2"] = np.cos(ang).astype(f), np.sin(ang).astype(f)
    k = np.arange(512)
    tk = (t[:, None] * k[None, :]) % 1024
    cs, sn = np.cos(2 * np.pi * tk / 1024), np.sin(2 * np.pi * tk / 1024)
    alt = np.where(t % 2 == 0, 1.0, -1.0)
    fi = -sn.copy()
    fi[:, 0] = alt
    c["dftf"] = np.concatenate([cs, fi], 1).astype(f)
    gr = 2 * cs.T / 1024
    gr[0] = 1 / 1024
    gi = -2 * sn.T / 1024
    gi[0] = alt / 1024
    c["dftg"] = np.concatenate([gr, gi], 0).astype(f)
    t2 = np.arange(256)
    tk = (t2[:, None] * t2[None, :]) % 512
    gi2 = -2 * np.sin(2 * np.pi * tk / 512) / 1024
    gi2[0] = np.where(t2 % 2 == 0, 1.0, -1.0) / 1024
    c["g2i"] = gi2.astype(f)
    z = []
    for n in (512, 256):
        tt = np.linspace(0.0, 1.0, n, dtype=f)[:, None]
        w = (2.0 * np.pi * np.arange(n, dtype=f)[:, None] / f(n)).astype(f)
        fb = np.linspace(1e-4, 15, 16, dtype=f)[None, :]
        z.append(np.concatenate([tt, np.cos((fb * w).astype(f)), -np.sin((fb * w).astype(f))], -1).astype(f))
        d = np.linspace(math.log(1e-2) / 1.5, math.log(1e-2) / 0.3, 512, dtype=f)
        c["decay1" if n == 512 else "decay2"] = np.exp(-tt * np.abs(d)).astype(f)
    c["hyz"] = np.ascontiguousarray(np.concatenate(z, 0).T)
    p, j = np.arange(128)[:, None], np.arange(384)[None, :]
    c["wmask"] = np.where(np.abs(j - 128 - p) <= 128, 0.0, NEG).astype(f)
    col, kc = np.arange(128)[:, None] % 64, np.arange(64)[None, :]
    c0 = np.clip(col - 8, 0, 48)
    c["cmask"] = np.where((kc >= c0) & (kc < c0 + 16), 0.0, NEG).astype(f)
    j = np.arange(512)[None, :]
    c["cmask2"] = np.where(p - j + 384 >= 0, 0.0, NEG).astype(f)
    c["tri"] = (p <= j).astype(f)
    cc = np.arange(8)[None, :]
    c["vmask"] = (p - 16 * cc - 31 >= 0).astype(f)
    dist = 511 - np.arange(640)
    n = np.maximum(dist, 0)
    nf = np.maximum(n, 1).astype(f)
    large = 16 + (np.log(nf / f(16)) / f(math.log(128 / 16)) * f(16)).astype(np.int32)
    bucket = np.where(n < 16, n, np.minimum(large, 31))
    oh = np.zeros((33, 640), f)
    for i in range(639):
        oh[bucket[i] if dist[i] >= 0 else 32, i] = 1.0
    c["onehot"] = oh
    return c


def layouts(I):
    f = np.float32
    L = {}
    L["cT"] = np.stack([I["c"][0].reshape(8, 128).T, I["c_ctx"].reshape(8, 128).T], -1)
    L["b_adaT"] = I["b_ada"].reshape(2, 24, 128).transpose(0, 2, 1)
    L["norm_gT"] = I["norm_g"].reshape(2, 8, 128).transpose(0, 2, 1)
    L["g10_0"] = np.concatenate([np.tile(I["glob_q_norm"][0], 8), np.tile(I["glob_k_norm"][0], 2)])
    L["g10_1"] = np.concatenate([np.tile(I["win_q_norm"][0], 8), np.tile(I["win_k_norm"][0], 2)])
    L["g16"] = np.concatenate([np.tile(I["nat_q_norm"][0], 8), np.tile(I["nat_k_norm"][0], 8)])
    L["convT"] = np.concatenate([I["hy_conv_w"][0], I["hy_conv_b"]], 0).reshape(4, 12, 128).transpose(2, 1, 0)
    L["hyb"] = np.stack([I["hy_freq"][0], I["hy_b1"][0], I["hy_b2"][0]], 1)
    rp = np.zeros((8, 15, 127), f)
    rp[:, :, 48:79] = I["nat_rpb"][0]
    at = np.arange(64)[None, :] - np.arange(64)[:, None] + 63
    lo = rp[:, :, at].transpose(0, 2, 1, 3)
    x = np.zeros((8, 128, 15, 64), f)
    x[:, 0:64] = lo
    x[:, 64:128, 1:15] = lo[:, :, 0:14]
    L["rpx"] = x
    pe = I["cmp_pe_2"].transpose(0, 3, 1, 2)
    L["peT"] = np.concatenate([pe, pe], 1)
    L["cmpw2"] = I["cmp_w2_2"].transpose(0, 2, 1, 3)
    L["mlag"] = np.concatenate([I["mla_q_norm_2"], I["mla_kv_norm_2"]], 1)
    L["t5"] = I["t5_table_2"]
    L["x"], L["ctx"], L["mem_2"] = I["x"][0], I["ctx"][0], I["mem_2"][0]
    L["hy_w1"], L["hy_w2"], L["hy_w3"], L["hy_skip"] = I["hy_w1"][0], I["hy_w2"][0], I["hy_w3"][0], I["hy_skip"][0]
    L["win_sink"] = I["win_sink"][0]
    for n in ("w_ada", "w_in", "w_out", "w_in_2", "cmp_w1_2", "mla_w_uq_2", "mla_w_ukv_2", "fox_b_f_2", "w_gate_2",
              "w_br_nsa_2", "w_br_mla_2", "w_br_fox_2", "w_mix_out_2", "xa_w_q_2", "xa_w_kv_2", "xa_w_o_2",
              "mlp_w_up_2", "mlp_w_down_2", "ln_g_2", "ln_b_2"):
        L[n] = I[n]
    return L


def kernel(**inputs):
    import concourse.bacc as bacc
    from concourse.bass_utils import run_bass_kernel_spmd

    I = {k: np.asarray(v) for k, v in inputs.items()}
    nc = bacc.Bacc("TRN2", target_bir_lowering=False, num_devices=1)
    arrays, D = {}, {}
    for name, a in {**layouts(I), **constants()}.items():
        a = np.ascontiguousarray(a)
        arrays["in_" + name] = a
        D[name] = nc.dram_tensor("in_" + name, a.shape, F32, kind="ExternalInput").ap()
    out = nc.dram_tensor("out_x", (512, 1024), F32, kind="ExternalOutput").ap()
    program(nc, D, out)
    r = run_bass_kernel_spmd(nc, [arrays], core_ids=[0])
    return r.results[0]["out_x"].reshape(1, 512, 1024)
```

```python
import math

import numpy as np
import concourse.bass as bass
from concourse import mybir
from concourse.alu_op_type import AluOpType as ALU

F32 = mybir.dt.float32
ACT = mybir.ActivationFunctionType
AX = mybir.AxisListType
NEG = -1e30
LOW = -3e38
EPS = 1e-6
LN_EPS = 1e-5
ALPHA = 4 ** 0.25

CONST = 0
RING = 3200
SLOT = 4352
NSLOT = 3
XR = RING + SLOT * NSLOT
BIG = XR + 6144
END = 53100


class Engine:

    def __init__(self, nc, eng, name, serial=True):
        self.e, self.sem, self.n, self.seen, self.serial = eng, nc.alloc_semaphore(name), 0, {}, serial

    def need(self, *toks):
        for t in toks:
            if t is None:
                continue
            if isinstance(t, list):
                self.need(*t)
                continue
            sem, v = t
            if self.seen.get(id(sem), 0) < v:
                self.e.wait_ge(sem, v)
                self.seen[id(sem)] = v

    def begin(self, toks):
        self.need(*toks)
        if self.serial and self.n:
            self.need(self.last())

    def done(self, ins):
        self.n += 1
        ins.then_inc(self.sem, 1)
        return (self.sem, self.n)

    def last(self):
        return (self.sem, self.n)

    def tt(self, out, a, b, op, *after):
        self.begin(after)
        return self.done(self.e.tensor_tensor(out, a, b, op))

    def ts(self, out, a, s1, op0, s2, op1, *after):
        self.begin(after)
        return self.done(self.e.tensor_scalar(out, a, s1, s2, op0, op1))

    def ts1(self, out, a, s1, op0, *after):
        self.begin(after)
        return self.done(self.e.tensor_scalar(out, a, s1, None, op0))

    def stt(self, out, a, s, b, op0, op1, *after):
        self.begin(after)
        return self.done(self.e.scalar_tensor_tensor(out, a, s, b, op0, op1))

    def addmax(self, out, a, b, init, acc, *after):
        self.begin(after)
        return self.done(self.e.tensor_tensor_reduce(out=out, in0=a, in1=b, scale=1.0, scalar=init,
                                                     op0=ALU.add, op1=ALU.max, accum_out=acc))

    def red(self, out, a, op, *after):
        self.begin(after)
        return self.done(self.e.tensor_reduce(out, a, AX.X, op))

    def copy(self, out, a, *after):
        self.begin(after)
        return self.done(self.e.tensor_copy(out, a))

    def zero(self, out, v, *after):
        self.begin(after)
        return self.done(self.e.memset(out, v))

    def recip(self, out, a, *after):
        self.begin(after)
        return self.done(self.e.reciprocal(out, a))

    def act(self, out, a, f, *after, bias=0.0, scale=1.0, acc=None):
        self.begin(after)
        if acc is None:
            return self.done(self.e.activation(out, a, f, bias=bias, scale=scale))
        return self.done(self.e.activation(out, a, f, bias=bias, scale=scale, accum_out=acc))


class Dmas:

    def __init__(self, nc, eng, name, n, owner=None):
        self.sems = [nc.alloc_semaphore(f"{name}{i}") for i in range(n)]
        self.vals = [0] * n
        self.k = 0
        self.w = owner or Engine(nc, eng, name + "w")
        self.eng = eng

    def go(self, out, in_, *after):
        i = self.k % len(self.sems)
        self.k += 1
        self.w.need(*after)
        if self.vals[i]:
            self.w.need((self.sems[i], self.vals[i]))
        self.eng.dma_start(out, in_).then_inc(self.sems[i], 16)
        self.vals[i] += 16
        return (self.sems[i], self.vals[i])


def bcast(ap, at, n):
    dims = [list(d) for d in ap.ap]
    dims.insert(at, [0, n])
    return bass.AP(ap.tensor, ap.offset, dims)


def rows(w, r0, kt, c0, c1):
    return w[r0:r0 + 128 * kt, c0:c1].rearrange("(k p) n -> p k n", p=128)


def program(nc, D, out):
    S = nc.alloc_sbuf_tensor("S", [128, END], F32)
    PS = nc.alloc_psum_tensor("PS", [128, 8, 512], F32)
    PE = Engine(nc, nc.tensor, "s_pe", serial=False)
    V = Engine(nc, nc.vector, "s_dve")
    A = Engine(nc, nc.scalar, "s_act")
    G = Engine(nc, nc.gpsimd, "s_pool")
    WQ = Dmas(nc, nc.sync, "s_w", 8)
    MQ = Dmas(nc, nc.gpsimd, "s_m", 12, owner=G)
    pf = [None] * 8

    def sb(off, *dims):
        n = 1
        for d in dims:
            n *= d
        v = S[:, off:off + n]
        if len(dims) == 2:
            v = v.rearrange("p (a b) -> p a b", a=dims[0])
        if len(dims) == 3:
            v = v.rearrange("p (a b c) -> p a b c", a=dims[0], b=dims[1])
        return v

    def barrier():
        toks = [PE.last(), V.last(), A.last(), G.last()]
        toks = [t for t in toks if t[1]]
        for e in (PE, V, A, G):
            e.need(*toks)
        return toks

    plan = []

    def want(src, *dims):
        n = 1
        for d in dims:
            n *= d
        plan.append((src, dims))

    w_ada, w_in, w_out = D["w_ada"], D["w_in"], D["w_out"]
    E_IN = [(0, 512), (512, 768), (2304, 2816), (768, 1280), (1280, 1792), (1792, 2304), (2816, 3328)]
    for n in range(6):
        want(rows(w_ada[0], 0, 8, n * 512, n * 512 + 512), 8, 512)
    for a, b in E_IN:
        want(rows(w_in[0], 0, 8, a, b), 8, b - a)
    for o in range(2):
        want(D["dftf"].rearrange("(k p) n -> p k n", p=128), 4, 1024)
        want(D["dftg"].rearrange("(k p) n -> p k n", p=128), 8, 512)
    for n in range(2):
        want(rows(w_out[0], 0, 8, n * 512, n * 512 + 512), 8, 512)
    for n in range(6):
        want(rows(w_ada[1], 0, 8, n * 512, n * 512 + 512), 8, 512)
    for a, b in [(0, 512), (512, 768), (768, 1280), (1280, 1792), (1792, 2304), (2304, 2816), (2816, 3328)]:
        want(rows(w_in[1], 0, 8, a, b), 8, b - a)
    for n in range(2):
        want(rows(w_out[1], 0, 8, n * 512, n * 512 + 512), 8, 512)
    S_IN = [(0, 512), (512, 1024), (1024, 1304), (1304, 1848), (1848, 2360), (2360, 2620)]
    for l in range(2):
        w2 = D["w_in_2"][l]
        for a, b in S_IN[:3]:
            want(rows(w2, 0, 8, a, b), 8, b - a)
        for kv in range(2):
            want(("cmpw", l, kv), 16, 128)
        want(rows(w2, 0, 8, 1304, 1848), 8, 544)
        want(rows(D["mla_w_uq_2"][l], 0, 3, 0, 384), 3, 384)
        want(rows(D["mla_w_ukv_2"][l], 0, 1, 0, 512), 1, 512)
        for a, b in S_IN[4:]:
            want(rows(w2, 0, 8, a, b), 8, b - a)
        for br, name, kt in ((0, "w_br_nsa_2", 4), (1, "w_br_mla_2", 2), (2, "w_br_fox_2", 2)):
            want(rows(D[name][l], 0, kt, 0, 1024), kt, 1024)
            for n in range(2):
                c = br * 1024 + n * 512
                want(rows(D["w_gate_2"][l], 0, 8, c, c + 512), 8, 512)
        for n in range(2):
            want(rows(D["w_mix_out_2"][l], 0, 8, n * 512, n * 512 + 512), 8, 512)
        want(rows(D["xa_w_q_2"][l], 0, 8, 0, 256), 8, 256)
        want(rows(D["xa_w_kv_2"][l], 0, 8, 0, 512), 8, 512)
        want(rows(D["xa_w_o_2"][l], 0, 2, 0, 1024), 2, 1024)
        for n in range(8):
            want(rows(D["mlp_w_up_2"][l], 0, 8, n * 512, n * 512 + 512), 8, 512)
        for r in range(4):
            for n in range(2):
                want(rows(D["mlp_w_down_2"][l], r * 1024, 8, n * 512, n * 512 + 512), 8, 512)

    loaded = []
    state = {"next": 0}

    def load_weight(*after):
        i = len(loaded)
        if i >= len(plan):
            return
        src, dims = plan[i]
        v = sb(RING + (i % NSLOT) * SLOT, *dims)
        if isinstance(src, tuple):
            _, l, kv = src
            w = D["cmp_w1_2"][l, kv].rearrange("(a l d) n -> a d l n", a=2, d=64)
            t = [WQ.go(v[0:64], w[0], *after), WQ.go(v[64:128], w[1], *after)]
        else:
            t = WQ.go(v, src, *after)
        loaded.append((v, t))

    for _ in range(NSLOT):
        load_weight()

    def weight():
        i = state["next"]
        state["next"] += 1
        return loaded[i]

    def used(tok):
        load_weight(tok)

    def group(dst, pairs, *after):
        PE.need(*after)
        n = len(pairs)
        for i, (l, r) in enumerate(pairs):
            m = nc.tensor.matmul(dst, l, r, start=(i == 0), stop=(i == n - 1))
        return PE.done(m)

    rot = {"b": 0, "e": 0}

    def bank():
        rot["b"] = (rot["b"] + 1) % 8
        return rot["b"]

    def evac(dst, src, tok, *after, scale=None):
        rot["e"] ^= 1
        if rot["e"]:
            if scale is None:
                return V.copy(dst, src, tok, *after)
            return V.ts1(dst, src, scale, ALU.mult, tok, *after)
        return A.act(dst, src, ACT.Copy, tok, *after, scale=1.0 if scale is None else scale)

    def flip(dst_of, src_of, ins, outs, npart=128, m=128, evacuate=evac, after=()):
        toks = []
        for o in outs:
            b = bank()
            PE.need(pf[b], *after)
            for n, i in enumerate(ins):
                x = nc.tensor.transpose(PS[0:m, b, n * npart:(n + 1) * npart], src_of(o, i), ident[0:npart, 0:npart])
            tok = PE.done(x)
            pf[b] = evacuate(dst_of(o), PS[0:m, b, 0:len(ins) * npart], tok)
            toks.append(pf[b])
        return toks

    c_at = {"o": CONST}

    def cst(*dims):
        n = 1
        for d in dims:
            n *= d
        o = c_at["o"]
        c_at["o"] += n
        assert c_at["o"] <= RING
        return sb(o, *dims)

    ident = cst(128)
    t_id = MQ.go(ident, D["ident"])
    ones = cst(128)
    V.zero(ones, 1.0)
    small = cst(512)
    stats = cst(8, 16)
    g2i = cst(2, 256)
    MQ.go(g2i, D["g2i"].rearrange("(k p) n -> p k n", p=128))
    cos1, sin1 = cst(4, 32), cst(4, 32)
    cos2, sin2 = cst(4, 16), cst(4, 16)
    for v, name in ((cos1, "cos1"), (sin1, "sin1"), (cos2, "cos2"), (sin2, "sin2")):
        MQ.go(v, D[name].rearrange("(k p) n -> p k n", p=128))
    aff = cst(8, 2, 2)
    ada = cst(24, 2)
    cT = cst(8, 2)
    ctmp = cst(8, 2)
    bada = cst(24)
    ng = cst(8)
    const_toks = [(s, v) for s, v in zip(MQ.sems, MQ.vals) if v]
    for e in (PE, V, A, G):
        e.need(*const_toks)
    barrier()

    def rsqrt(r, x, t1, *after):
        a = A.act(t1, x, ACT.Ln, *after)
        a = A.act(r, t1, ACT.Exp, a, scale=-0.5)
        V.tt(t1, r, r, ALU.mult, a)
        V.tt(t1, t1, x, ALU.mult)
        V.ts(t1, t1, -0.5, ALU.mult, 1.5, ALU.add)
        return V.tt(r, r, t1, ALU.mult)

    X = sb(XR, 6, 1024)

    def attention(jobs, P, PT, wide=True, order_evac=evac):
        free_P = [None, None]
        free_PT = [None, None, None]
        cnt = {"u": 0, "t": 0}
        pending = []
        late = []
        one = wide is False

        def scores(j, n, q):
            cnt["u"] += 1
            if one:
                b0 = cnt["u"] % 4
                bs = [b0]
                pair_ap = PS[:, b0, :]
            else:
                b0 = 2 * (cnt["u"] % 2)
                bs = [b0, b0 + 1]
                pair_ap = PS[:, b0:b0 + 2, :].rearrange("p a b -> p (a b)")
            PE.need([pf[b] for b in bs], *j.get("after", ()))
            for c0, nn, l, r in j["scores"](q):
                m = nc.tensor.matmul(pair_ap[:, c0:c0 + nn], l, r, start=True, stop=True)
            tok = PE.done(m)
            st = stats[:, cnt["u"] % 8, :]
            Pq = (j["P"] if "P" in j else P[n % 2])[q]
            rel, ta, k, biased, plain = softmax(j, q, pair_ap, Pq, st, tok, free_P[n % 2])
            for b in bs:
                pf[b] = rel
            cell = []
            while late:
                late.pop(0)()
            late.append(lambda: cell.append(normalize(j, q, Pq, st, ta, k, plain, biased)))
            return cell

        def softmax(j, q, ps, Pq, st, tok, free):
            plain, biased = j["segs"](q)
            m = None
            rel = []
            if plain:
                c0, c1 = plain
                t = V.red(st[:, 0:1], ps[:, c0:c1], ALU.max, tok)
                m = st[:, 0:1]
                if j.get("sink") is not None:
                    t = V.tt(st[:, 0:1], st[:, 0:1], j["sink"], ALU.max)
                rel.append(t)
            if biased:
                c0, c1, bias = biased
                src = ps[:, c0:c1]
                if j.get("pre") is not None:
                    cumq, Bk = j["pre"](q)
                    t = V.stt(Pq[:, c0:c1], src, cumq, Bk, ALU.add, ALU.add, tok, free)
                    rel.append(t)
                    src = Pq[:, c0:c1]
                t = V.addmax(Pq[:, c0:c1], src, bias, LOW if m is None else m, st[:, 1:2], tok, free)
                m = st[:, 1:2]
                rel.append(t)
            tn = V.ts1(st[:, 2:3], m, -1.0, ALU.mult)
            nm = st[:, 2:3]
            k = 0
            if plain:
                c0, c1 = plain
                ta = A.act(Pq[:, c0:c1], ps[:, c0:c1], ACT.Exp, tn, free, bias=nm, acc=st[:, 4 + k:5 + k])
                k += 1
                rel.append(ta)
            if biased:
                c0, c1, _ = biased
                ta = A.act(Pq[:, c0:c1], Pq[:, c0:c1], ACT.Exp, tn, bias=nm, acc=st[:, 4 + k:5 + k])
                k += 1
            if j.get("sink") is not None:
                ta = A.act(st[:, 4 + k:5 + k], j["sink"], ACT.Exp, tn, bias=nm)
                k += 1
            return rel, ta, k, biased, plain

        def normalize(j, q, Pq, st, ta, k, plain, biased):
            V.need(ta)
            for i in range(1, k):
                V.tt(st[:, 4:5], st[:, 4:5], st[:, 4 + i:5 + i], ALU.add)
            V.recip(st[:, 3:4], st[:, 4:5])
            if j.get("gate") is not None:
                V.tt(st[:, 3:4], st[:, 3:4], j["gate"](q), ALU.mult)
            if j.get("valid") is not None and j["valid"](q) is not None:
                c0, c1, _ = biased
                t = V.stt(Pq[:, c0:c1], Pq[:, c0:c1], st[:, 3:4], j["valid"](q), ALU.mult, ALU.mult)
            else:
                cols = []
                if plain:
                    cols.append(plain)
                if biased:
                    cols.append(biased[:2])
                for c0, c1 in cols:
                    t = V.ts1(Pq[:, c0:c1], Pq[:, c0:c1], st[:, 3:4], ALU.mult)
            return t

        def transposes(j, n, kt, rdy):
            pcol, nk, q0, q1, v = j["keys"][kt]
            b = 4 + cnt["t"] % 2
            pt = PT[cnt["t"] % 3]
            slot = cnt["t"] % 3
            cnt["t"] += 1
            if not all(rdy[q] for q in range(q0, q1)):
                while late:
                    late.pop(0)()
            PE.need(pf[b], *[rdy[q][0] for q in range(q0, q1)])
            Pn = j["P"] if "P" in j else P[n % 2]
            for q in range(q0, q1):
                m = nc.tensor.transpose(PS[0:nk, b, q * 128:q * 128 + 128], Pn[q][:, pcol(q):pcol(q) + nk],
                                        ident[:, :])
            tok = PE.done(m)
            pf[b] = order_evac(pt[0:nk, q0 * 128:q1 * 128], PS[0:nk, b, q0 * 128:q1 * 128], tok, free_PT[slot])
            return (j, kt, pt, slot, pf[b], tok)

        def values(x):
            j, kt, pt, slot, ready, _ = x
            pcol, nk, q0, q1, v = j["keys"][kt]
            ob, half = j["out"]
            last = kt == len(j["keys"]) - 1
            PE.need(ready)
            if kt == 0 and j["first"]:
                PE.need(pf[ob])
            m = nc.tensor.matmul(PS[half * 64:half * 64 + 64, ob, q0 * 128:q1 * 128], v,
                                 pt[0:nk, q0 * 128:q1 * 128], start=(kt == 0 and j["first"]),
                                 stop=(last and j["last"]))
            tok = PE.done(m)
            free_PT[slot] = tok
            if last and j.get("final"):
                pf[ob] = j["final"](tok)

        prev = None
        for n in range(len(jobs) + 1):
            a = []
            if n < len(jobs):
                a = [(jobs[n], n, q) for q in range(jobs[n]["nq"])]
            b = []
            if prev is not None:
                b = [(prev[0], n - 1, kt, prev[1]) for kt in range(len(prev[0]["keys"]))]
            rdy = []
            la, lb = len(a), len(b)
            ia = ib = 0
            while ia < la or ib < lb:
                if ia < la and (ib >= lb or ia * lb <= ib * la):
                    rdy.append(scores(*a[ia]))
                    ia += 1
                else:
                    pending.append(transposes(*b[ib]))
                    ib += 1
                    if ib == lb:
                        free_P[(n - 1) % 2] = PE.last()
                    if len(pending) > 1:
                        values(pending.pop(0))
            prev = (jobs[n], rdy) if n < len(jobs) else None
        while pending:
            values(pending.pop(0))

    def grid(base, n, *dims):
        s = 1
        for d in dims:
            s *= d
        return [sb(base + i * s, *dims) for i in range(n)]

    def P_narrow(base):
        f = grid(base, 8, 512)
        return [f[0:4], f[4:8]]

    def P_buffers(base):
        f = grid(base, 8, 768)
        return [f[0:4], f[4:8]]

    def modulation(l):
        cc = MQ.go(cT, D["cT"])
        b1 = MQ.go(bada, D["b_adaT"][l])
        b2 = MQ.go(ng, D["norm_gT"][l])
        t = A.act(ctmp, cT, ACT.Tanh, cc, scale=0.5)
        V.stt(ctmp, ctmp, 1.0, cT, ALU.add, ALU.mult, t, cc)
        tc = V.ts1(ctmp, ctmp, 0.5, ALU.mult)
        bt = bank()
        row = small[0:2, 0:512]
        tr = None
        for n in range(6):
            w, tw = weight()
            b = bank()
            if b == bt:
                b = bank()
            t = group(PS[0:2, b, :], [(ctmp[:, k, :], w[:, k, :]) for k in range(8)], tw, pf[b], tc)
            used(t)
            pf[b] = V.copy(row, PS[0:2, b, :], t, tr)
            PE.need(pf[b], pf[bt])
            for i in range(4):
                c = (n * 4 + i) * 2
                m = nc.tensor.transpose(PS[:, bt, c:c + 2], row[:, i * 128:i * 128 + 128], ident[0:2, 0:2])
            tr = PE.done(m)
        ps = PS[:, bt, 0:48].rearrange("p (a b) -> p a b", a=24)
        pf[bt] = V.tt(ada, ps, bcast(bada, 2, 2), ALU.add, tr, b1)
        V.ts1(aff[:, :, :, 0], ada[:, 8:16, :], 1.0, ALU.add)
        V.tt(aff[:, :, :, 0], aff[:, :, :, 0], bcast(ng, 2, 2), ALU.mult, b2)
        return V.copy(aff[:, :, :, 1], ada[:, 0:8, :])

    def gates(dst, nv, t_mod):
        for v in range(nv):
            for h in range(2):
                b = bank()
                PE.need(pf[b], t_mod)
                for k in range(4):
                    m = nc.tensor.matmul(PS[:, b, k * 128:k * 128 + 128],
                                         ada[:, 16 + h * 4 + k, v:v + 1].to_broadcast([128, 128]), ident[:, :],
                                         start=True, stop=True)
                pf[b] = t = evac(dst[v][:, h * 512:h * 512 + 512], PS[:, b, :], PE.done(m))
        return t

    def normed(hT, xn, junk, tx, t_mod):
        for t in range(6):
            a = A.act(junk, X[:, t, :], ACT.Square, tx, t_mod, acc=small[:, t:t + 1])
        V.ts(small[:, 0:6], small[:, 0:6], 1.0 / 1024, ALU.mult, EPS, ALU.add, a)
        rsqrt(small[:, 8:14], small[:, 0:6], small[:, 16:22], V.last())
        tn = []
        for t in range(6):
            tn.append(V.ts1(xn[:, t, :], X[:, t, :], small[:, 8 + t:9 + t], ALU.mult))
        toks = []
        for k in range(8):
            for v, ts_ in ((0, range(4)), (1, range(4, 6))):
                b = bank()
                PE.need(pf[b], tn[-1], t_mod)
                for n, t in enumerate(ts_):
                    m = nc.tensor.transpose(PS[:, b, n * 128:n * 128 + 128], xn[:, t, k * 128:k * 128 + 128],
                                            ident[:, :])
                tok = PE.done(m)
                n = len(ts_) * 128
                rot["e"] ^= 1
                if rot["e"]:
                    pf[b] = V.ts(hT[:, k, v * 512:v * 512 + n], PS[:, b, 0:n], aff[:, k, v, 0:1], ALU.mult,
                                 aff[:, k, v, 1:2], ALU.add, tok)
                else:
                    pf[b] = A.act(hT[:, k, v * 512:v * 512 + n], PS[:, b, 0:n], ACT.Identity, tok, t_mod,
                                  scale=aff[:, k, v, 0:1], bias=aff[:, k, v, 1:2])
                toks.append(pf[b])
        return [V.last(), A.last()]

    def project(w, tw, kt, c0, n, hT, tiles, dst_of, evacuate=evac, *after):
        for t in tiles:
            b = bank()
            tok = group(PS[:, b, 0:n], [(hT[:, k, t * 128:t * 128 + 128], w[:, k, c0:c0 + n]) for k in range(kt)],
                        pf[b], tw, *after)
            pf[b] = evacuate(dst_of(t), PS[:, b, 0:n], tok)
        return tok

    def project_T(w, tw, kt, c0, m, hT, spans, evacuate, *after):
        for t0, n in spans:
            b = bank()
            tok = group(PS[0:m, b, 0:n], [(w[:, k, c0:c0 + m], hT[:, k, t0:t0 + n]) for k in range(kt)],
                        pf[b], tw, *after)
            pf[b] = evacuate(t0, n, PS[0:m, b, 0:n], tok)
        return tok

    def silu2_T(dst, tmp):
        def ev(t0, n, ps, tok):
            a = A.act(tmp[:, 0:n], ps, ACT.Tanh, tok, V.last(), scale=0.5)
            return V.stt(dst[:, t0:t0 + n], tmp[:, 0:n], 1.0, ps, ALU.add, ALU.mult, a)
        return ev

    def head_norm(Q, tiles, nh, g, tg, tmp, qscale_heads, *after):
        ss, rr, t1 = small[:, 0:6 * nh], small[:, 128:128 + 6 * nh], small[:, 256:256 + 6 * nh]
        V.need(*after)
        for t in tiles:
            q = Q(t)
            V.tt(tmp[:, 0:nh * 64], q, q, ALU.mult)
            V.red(ss[:, t * nh:t * nh + nh], tmp[:, 0:nh * 64].rearrange("p (h d) -> p h d", d=64), ALU.add)
        a, b = tiles[0] * nh, (tiles[-1] + 1) * nh
        V.ts(ss[:, a:b], ss[:, a:b], 1.0 / 64, ALU.mult, EPS, ALU.add)
        rsqrt(rr[:, a:b], ss[:, a:b], t1[:, a:b], V.last())
        if qscale_heads:
            r3 = rr[:, a:b].rearrange("p (t h) -> p t h", h=nh)[:, :, 0:qscale_heads]
            V.ts1(r3, r3, 0.125, ALU.mult)
        for t in tiles:
            q = Q(t).rearrange("p (h d) -> p h d", d=64)
            V.tt(q, q, bcast(rr[:, t * nh:t * nh + nh], 2, 64), ALU.mult)
            V.tt(Q(t), Q(t), g, ALU.mult, tg)
        return V.last()

    def rope_pairs(Q, tiles, nh, tmp):
        for t in tiles:
            q = Q(t).rearrange("p (h d two) -> p h d two", d=32, two=2)
            x0, x1 = q[:, :, :, 0], q[:, :, :, 1]
            c, s = bcast(cos1[:, t, :], 1, nh), bcast(sin1[:, t, :], 1, nh)
            u = [tmp[:, i * nh * 32:(i + 1) * nh * 32].rearrange("p (h d) -> p h d", d=32) for i in range(4)]
            V.tt(u[0], x0, c, ALU.mult)
            V.tt(u[1], x1, s, ALU.mult)
            V.tt(u[2], x0, s, ALU.mult)
            V.tt(u[3], x1, c, ALU.mult)
            V.tt(x0, u[0], u[1], ALU.subtract)
            V.tt(x1, u[2], u[3], ALU.add)
        return V.last()

    def swap(dst, src, *after):
        return [MQ.go(dst[0:64], src[64:128], *after), MQ.go(dst[64:128], src[0:64], *after)]

    def out_proj(yT, nt, GB, t_ready, tmp):
        for n in range(2):
            w, tw = weight()
            for t in range(nt):
                b = bank()
                tok = group(PS[:, b, :], [(yT[:, k, t * 128:t * 128 + 128], w[:, k, :]) for k in range(8)],
                            pf[b], tw, *t_ready)
                x = X[:, t, n * 512:n * 512 + 512]
                u = tmp[t % 2]
                pf[b] = V.tt(u, PS[:, b, :], GB[0 if t < 4 else 1][:, n * 512:n * 512 + 512], ALU.mult, tok,
                             G.last() if G.n else None)
                G.tt(x, x, u, ALU.add, pf[b])
            used(tok)

    x_d, ctx_d = D["x"], D["ctx"]

    def load_x(*after):
        return [MQ.go(X[:, 0:4, :], x_d.rearrange("(t p) d -> p t d", p=128), *after),
                MQ.go(X[:, 4:6, :], ctx_d.rearrange("(t p) d -> p t d", p=128), *after)]

    def head_transposes(QK, qT, ntile, blocks, after):
        for j in blocks:
            for c0, t0, nt in ((0, 0, ntile), (512, 4, 2)):
                if nt:
                    b = bank()
                    PE.need(pf[b], *after)
                    for t in range(nt):
                        m = nc.tensor.transpose(PS[:, b, t * 128:t * 128 + 128],
                                                QK[:, t0 + t, j * 128:j * 128 + 128], ident[:, :])
                    pf[b] = evac(qT(j)[:, c0:c0 + nt * 128], PS[:, b, 0:nt * 128], PE.done(m))

    tx = load_x()
    t_mod = modulation(0)
    hT = sb(BIG, 8, 768)
    yT = sb(BIG + 6144, 8, 768)
    UC = sb(BIG + 12288, 6, 1536)
    QK = sb(BIG + 21504, 6, 640)
    VV = sb(BIG + 25344, 6, 128)
    g10 = sb(BIG + 26112, 640)
    tmp10 = sb(BIG + 26752, 1280)
    uct = grid(BIG + 28032, 2, 768)
    gtmp = sb(BIG + 29568, 512)
    cw = sb(BIG + 30080, 12, 4)
    tg = MQ.go(g10, bcast(D["g10_0"], 0, 128))
    tcw = MQ.go(cw, D["convT"])
    normed(hT, sb(BIG + 12288, 6, 1024), sb(BIG + 6144, 1024), tx, t_mod)
    barrier()
    w, tw = weight()
    used(project(w, tw, 8, 0, 512, hT, range(6), lambda t: QK[:, t, 0:512]))
    w, tw = weight()

    def ev_kv0(t, ps, tok):
        V.copy(QK[:, t, 512:640], ps[:, 0:128], tok)
        return V.copy(VV[:, t, :], ps[:, 128:256])
    used(project(w, tw, 8, 0, 256, hT, range(6), lambda t: t, ev_kv0))
    head_norm(lambda t: QK[:, t, :], range(6), 10, g10, tg, tmp10, 8, A.last(), V.last())
    t_q = rope_pairs(lambda t: QK[:, t, :], range(4), 10, tmp10)
    w, tw = weight()
    for j in range(4):
        tok = project_T(w, tw, 8, j * 128, 128, hT, [(0, 512), (512, 256)], silu2_T(yT[:, j, :], gtmp))
    used(tok)

    V.need(tcw)
    A.need(tcw)
    free_u = [None, None]

    def to_tokens(ct, u, after):
        for t0, nt in ((0, 4), (4, 2)):
            b = bank()
            PE.need(pf[b], after)
            for t in range(nt):
                m = nc.tensor.transpose(PS[:, b, t * 128:t * 128 + 128], u[:, (t0 + t) * 128:(t0 + t + 1) * 128],
                                        ident[:, :])
            tok = PE.done(m)
            pf[b] = evac(UC[:, t0:t0 + nt, ct * 128:ct * 128 + 128],
                         PS[:, b, 0:nt * 128].rearrange("p (t c) -> p t c", t=nt), tok)
        free_u[ct % 2] = tok
    conv_prev = None
    for n in range(3):
        w, tw = weight()
        for s in range(4):
            ct = n * 4 + s
            u = uct[ct % 2]
            for t0, nn in ((0, 512), (512, 256)):
                b = bank()
                tok = group(PS[:, b, 0:nn], [(w[:, k, s * 128:s * 128 + 128], hT[:, k, t0:t0 + nn]) for k in range(8)],
                            pf[b], tw)
                a = A.act(u[:, t0:t0 + nn], PS[:, b, 0:nn], ACT.Identity, tok, free_u[ct % 2],
                          scale=cw[:, ct, 1:2], bias=cw[:, ct, 3:4])
                V.stt(u[:, t0 + 1:t0 + nn], PS[:, b, 0:nn - 1], cw[:, ct, 0:1], u[:, t0 + 1:t0 + nn],
                      ALU.mult, ALU.add, a)
                pf[b] = V.stt(u[:, t0:t0 + nn - 1], PS[:, b, 1:nn], cw[:, ct, 2:3], u[:, t0:t0 + nn - 1],
                              ALU.mult, ALU.add)
            if s == 3:
                used(tok)
            if conv_prev:
                to_tokens(*conv_prev)
            conv_prev = (ct, u, V.last())
    w, tw = weight()
    for j in range(4):
        tok = project_T(w, tw, 8, j * 128, 128, hT, [(0, 512), (512, 256)], silu2_T(yT[:, 4 + j, :], gtmp))
        if j == 0:
            to_tokens(*conv_prev)
    used(tok)
    f = barrier()
    qT = sb(BIG, 5, 768)
    kS = sb(BIG + 3840, 768)
    head_transposes(QK, lambda j: qT[:, j, :], 4, (4, 0, 1, 2, 3), [])
    t_s = swap(kS, qT[:, 4, :], V.last(), A.last())
    P, PT = P_buffers(XR), grid(BIG + 28032, 3, 512)

    def yfinal(pair, c0, n, ob):
        def final(tok):
            return V.stt(yT[:, pair, c0:c0 + n], PS[:, ob, 0:n], 0.5, yT[:, pair, c0:c0 + n], ALU.mult, ALU.mult, tok)
        return final

    jobs = []
    for nq, q00, kts in ((4, 0, range(6)), (2, 4, (4, 5))):
        for pair in range(4):
            for half in range(2):
                h = pair * 2 + half
                g = h // 4
                ksrc = qT[:, 4, :] if g == half else kS
                lo = half * 64

                def sc(q, pair=pair, lo=lo, ksrc=ksrc, nq=nq, q00=q00):
                    l = qT[lo:lo + 64, pair, (q00 + q) * 128:(q00 + q) * 128 + 128]
                    a = [(0, 512, l, ksrc[lo:lo + 64, 0:512])] if nq == 4 else []
                    return a + [(512, 256, l, ksrc[lo:lo + 64, 512:768])]
                ob = 6 + pair % 2
                jobs.append(dict(nq=nq, scores=sc, segs=lambda q, nq=nq: ((0 if nq == 4 else 512, 768), None),
                                 out=(ob, half), first=True, last=True, after=[V.last(), A.last()] + (
                                     t_s if g != half else []),
                                 keys=[(lambda q, c=kt * 128: c, 128, 0, nq, VV[:, kt, g * 64:g * 64 + 64])
                                       for kt in kts],
                                 final=yfinal(pair, q00 * 128, nq * 128, ob) if half else None))
    attention(jobs, P, PT)
    f = barrier()

    TR, TI = sb(BIG, 4, 512), sb(BIG + 2048, 4, 512)
    tr, ti = sb(BIG + 4096, 2, 512), sb(BIG + 5120, 2, 512)
    ZR, ZI = sb(BIG + 21504, 4, 512), sb(BIG + 23552, 4, 512)
    zr, zi = sb(BIG + 25600, 2, 512), sb(BIG + 26624, 2, 512)
    tmpa, tmpb = sb(BIG + 27648, 512), sb(BIG + 28160, 512)
    w3 = sb(XR, 2048)
    h2 = sb(XR + 2048, 768)
    zt = sb(XR + 2816, 768)
    hw = sb(XR + 3584, 192)
    dec = grid(XR + 3776, 2, 512)
    dsk = sb(XR + 4800, 512)
    sc1, sc2 = sb(XR + 5312, 512), sb(BIG + 28672, 512)
    t1 = MQ.go(w3[0:64], D["hy_w3"], *f)
    t2 = MQ.go(zt[0:33], D["hyz"], *f)
    t3 = MQ.go(hw[0:33, 0:64], D["hy_w1"], *f)
    t4 = MQ.go(hw[0:64, 64:128], D["hy_w2"], *f)
    t5 = MQ.go(hw[0:64, 128:131], D["hyb"], *f)
    for e in (PE, V, A):
        e.need(t1, t2, t3, t4, t5)

    def wrapped_sin(dst, src, bcol, tok, n):
        x, k = tmpa[0:64, 0:n], tmpb[0:64, 0:n]
        rel = V.ts(x, src, bcol, ALU.add, hw[0:64, 128:129], ALU.mult, tok)
        V.ts(k, x, 1.0 / (2 * math.pi), ALU.mult, 12582912.0, ALU.add)
        V.ts1(k, k, 12582912.0, ALU.subtract)
        V.stt(x, k, -6.28125, x, ALU.mult, ALU.add)
        V.stt(x, k, -(2 * math.pi - 6.28125), x, ALU.mult, ALU.add)
        V.ts(x, x, 3.1415925, ALU.min, -3.1415925, ALU.max)
        return rel, A.act(dst, x, ACT.Sin, V.last())

    for a0, n in ((0, 512), (512, 256)):
        b = bank()
        tok = group(PS[0:64, b, 0:n], [(hw[0:33, 0:64], zt[0:33, a0:a0 + n])], pf[b])
        pf[b], t = wrapped_sin(h2[0:64, a0:a0 + n], PS[0:64, b, 0:n], hw[0:64, 129:130], tok, n)
        b = bank()
        tok = group(PS[0:64, b, 0:n], [(hw[0:64, 64:128], h2[0:64, a0:a0 + n])], pf[b], t)
        pf[b], t = wrapped_sin(h2[0:64, a0:a0 + n], PS[0:64, b, 0:n], hw[0:64, 130:131], tok, n)
        V.need(t)

    def spectrum(w, tw, o, nt, st, s_, d_, Tr, Ti, scl, a0, decay):
        PE.need(A.last())
        td = [MQ.go(dec[t], decay[t * 128:t * 128 + 128, :], V.last()) for t in range(2)]
        for t in range(nt):
            pair = []
            for side in range(2):
                b = bank()
                c = (o * 2 + side) * 512
                tok = group(PS[:, b, :], [(h2[0:64, a0 + t * 128:a0 + t * 128 + 128], w3[0:64, c:c + 512])], pf[b])
                pair.append((b, tok))
            for side in range(2):
                b, tok = pair[side]
                pf[b] = V.tt((tmpa, tmpb)[side], PS[:, b, :], dec[t % 2], ALU.mult, tok, td[t])
            if t + 2 < nt:
                td.append(MQ.go(dec[t % 2], decay[(t + 2) * 128:(t + 3) * 128, :], V.last()))
            if t == 0:
                V.zero(tmpb[0:1, :], 0.0)
            V.tt(s_[:, t, :], tmpa, tmpb, ALU.add)
            V.tt(d_[:, t, :], tmpa, tmpb, ALU.subtract)
        sq = []
        PE.need(V.last())
        bn = bank()
        sums = []
        for k in range(nt):
            for src, dst, half in ((s_, Tr, 0), (d_, Ti, 512)):
                b = bank()
                if b == bn:
                    b = bank()
                tok = group(PS[:, b, :], [(w[:, t, half + k * 128 * st:half + (k + 1) * 128 * st:st], src[:, t, :])
                                          for t in range(nt)], pf[b], tw)
                pf[b] = A.act(dst[:, k, :], PS[:, b, :], ACT.Copy, tok)
            u = (tmpa, tmpb)[k % 2]
            V.tt(u, s_[:, k, :], s_[:, k, :], ALU.mult, sums[k - 2] if k > 1 else None)
            V.tt(sc4, d_[:, k, :], d_[:, k, :], ALU.mult)
            x = V.tt(u, u, sc4, ALU.add)
            PE.need(x, pf[bn] if k == 0 else None)
            sums.append(PE.done(nc.tensor.matmul(PS[:, bn, :], ones[:, :], u, start=(k == 0), stop=(k == nt - 1))))
        b = bank()
        if b == bn:
            b = bank()
        tok = group(PS[0:1, b, :], [(w[:, t, 512:513], s_[:, t, :]) for t in range(nt)], pf[b])
        V.ts(tmpa, PS[:, bn, :], 0.5, ALU.mult, EPS, ALU.add, sums[-1])
        pf[bn] = V.last()
        rsqrt(scl, tmpa, tmpb, V.last())
        if nt == 2:
            V.ts1(scl, scl, 2.0, ALU.mult)
        pf[b] = V.copy(Ti[0:1, 0, :], PS[0:1, b, :], tok, A.last())
        return tok

    sc3, sc4 = sb(BIG + 29184, 512), sb(BIG + 29696, 512)

    def forward(w, tw, nt, st, t0, Zr, Zi, Tr, Ti):
        toks = []
        V.need(A.last())
        PE.need(V.last(), G.last())
        for k in range(nt):
            ev = []
            for dst, half in ((Zr, 0), (Zi, 512)):
                b = bank()
                tok = group(PS[:, b, :], [(w[:, t, half + k * 128 * st:half + (k + 1) * 128 * st:st],
                                           UC[:, t0 + t, 0:512]) for t in range(nt)], pf[b], tw)
                pf[b] = A.act(dst[:, k, :], PS[:, b, :], ACT.Copy, tok)
                ev.append(pf[b])
            if k == 0:
                V.tt(small[0:1, 0:512], Zr[0:1, 0, :], Tr[0:1, 0, :], ALU.mult, *ev)
                V.tt(sc3[0:1, :], Zi[0:1, 0, :], Ti[0:1, 0, :], ALU.mult)
            g = G.tt(tmpb, Zr[:, k, :], Ti[:, k, :], ALU.mult, V.last(), *ev)
            V.tt(tmpa, Zr[:, k, :], Tr[:, k, :], ALU.mult, *ev)
            V.tt(sc4, Zi[:, k, :], Tr[:, k, :], ALU.mult)
            V.tt(Zi[:, k, :], Zi[:, k, :], Ti[:, k, :], ALU.mult)
            V.tt(Zr[:, k, :], tmpa, Zi[:, k, :], ALU.subtract, g)
            V.tt(Zi[:, k, :], tmpb, sc4, ALU.add)
            if k == 0:
                V.copy(Zr[0:1, 0, :], small[0:1, 0:512])
                V.copy(Zi[0:1, 0, :], sc3[0:1, :])
            toks.append(V.last())
        return tok, toks

    def inverse(lhs, nt, t0, o, Zr, Zi, scl, tw, tz):
        bs = [bank() for _ in range(nt)]
        PE.need(tw, *[pf[b] for b in bs])
        for k in range(nt):
            PE.need(tz[k])
            for t in range(nt):
                nc.tensor.matmul(PS[:, bs[t], :], lhs(0, k, t), Zr[:, k, :], start=(k == 0), stop=False)
                m = nc.tensor.matmul(PS[:, bs[t], :], lhs(1, k, t), Zi[:, k, :], start=False, stop=(k == nt - 1))
        tok = PE.done(m)
        for t in range(nt):
            b = bs[t]
            z = UC[:, t0 + t, 0:512]
            ta_, tb_ = ((tmpa, tmpb), (sc3, sc4))[t % 2]
            g = G.tt(tb_, z, dsk, ALU.mult, tok, V.last() if t < 2 else zt_[t - 2])
            if t == 0:
                zt_ = []
            pf[b] = V.tt(ta_, PS[:, b, :], scl, ALU.mult, tok)
            V.tt(ta_, ta_, tb_, ALU.add, g)
            V.tt(z, ta_, UC[:, t0 + t, (o + 1) * 512:(o + 2) * 512], ALU.mult)
            zt_.append(V.last())
        return tok

    for o in range(2):
        f = barrier()
        tds = MQ.go(dsk, bcast(D["hy_skip"][o], 0, 128), *f)
        G.need(tds)
        w, tw = weight()
        spectrum(w, tw, o, 4, 1, ZR, ZI, TR, TI, sc1, 0, D["decay1"])
        spectrum(w, tw, o, 2, 2, zr, zi, tr, ti, sc2, 512, D["decay2"])
        barrier()
        t, tz = forward(w, tw, 4, 1, 0, ZR, ZI, TR, TI)
        t, tz2 = forward(w, tw, 2, 2, 4, zr, zi, tr, ti)
        used(t)
        w, tw = weight()
        inverse(lambda part, k, t, w=w: w[:, part * 4 + k, t * 128:t * 128 + 128], 4, 0, o, ZR, ZI, sc1, tw, tz)

        def lhs2(part, k, t, w=w):
            if part == 0:
                return w[:, k, t * 256:t * 256 + 256:2]
            if k == 0:
                return g2i[:, 0, t * 128:t * 128 + 128]
            return w[:, 4 + k, t * 256:t * 256 + 256:2]
        used(inverse(lhs2, 2, 4, o, zr, zi, sc2, tw, tz2))
    f = barrier()
    tx = load_x(*f)
    for j in range(4):
        for c0, nt, t0 in ((0, 4, 0), (512, 2, 4)):
            b = bank()
            PE.need(pf[b])
            for t in range(nt):
                m = nc.tensor.transpose(PS[:, b, t * 128:t * 128 + 128], UC[:, t0 + t, j * 128:j * 128 + 128],
                                        ident[:, :])
            y = yT[:, 4 + j, c0:c0 + nt * 128]
            pf[b] = V.stt(y, PS[:, b, 0:nt * 128], 0.5, y, ALU.mult, ALU.mult, PE.done(m))
    GB = [sb(BIG, 1024), sb(BIG + 1024, 1024)]
    tmp = grid(BIG + 2048, 2, 512)
    gates(GB, 2, None)
    V.need(*tx)
    G.need(*tx)
    out_proj(yT, 6, GB, [V.last(), A.last()], tmp)
    f = barrier()

    t_mod = modulation(1)
    hT = sb(BIG, 8, 768)
    yT = sb(BIG + 6144, 8, 512)
    QKw = sb(BIG + 10240, 6, 640)
    Vw = sb(BIG + 14080, 6, 128)
    QKn = sb(BIG + 14848, 6, 1024)
    Vn = sb(BIG + 20992, 6, 512)
    qTw = sb(BIG + 24064, 4, 512)
    kTw = sb(BIG + 26112, 768)
    kS = sb(BIG + 26880, 768)
    tmp16 = sb(BIG + 27648, 1280)
    g10 = sb(BIG + 28928, 640)
    g16 = sb(BIG + 29568, 1024)
    gtmp = sb(BIG + 24064, 512)
    tg = [MQ.go(g10, bcast(D["g10_1"], 0, 128), *f), MQ.go(g16, bcast(D["g16"], 0, 128), *f)]
    normed(hT, sb(BIG + 14848, 6, 1024), sb(BIG + 10240, 1024), None, t_mod)
    f = barrier()
    w, tw = weight()
    used(project(w, tw, 8, 0, 512, hT, range(4), lambda t: QKw[:, t, 0:512]))
    w, tw = weight()

    def ev_kv1(t, ps, tok):
        V.copy(QKw[:, t, 512:640], ps[:, 0:128], tok)
        return V.copy(Vw[:, t, :], ps[:, 128:256])
    used(project(w, tw, 8, 0, 256, hT, range(6), lambda t: t, ev_kv1))
    V.need(A.last())
    head_norm(lambda t: QKw[:, t, :], range(4), 10, g10, tg, tmp16, 8)
    head_norm(lambda t: QKw[:, t, 512:640], range(4, 6), 2, g10[:, 512:640], tg, tmp16, 0)
    rope_pairs(lambda t: QKw[:, t, :], range(4), 10, tmp16)
    w, tw = weight()
    used(project(w, tw, 8, 0, 512, hT, range(4), lambda t: QKn[:, t, 0:512]))
    w, tw = weight()
    used(project(w, tw, 8, 0, 512, hT, range(6), lambda t: QKn[:, t, 512:1024]))
    V.need(A.last())
    head_norm(lambda t: QKn[:, t, :], range(4), 16, g16, tg, tmp16, 8)
    head_norm(lambda t: QKn[:, t, 512:1024], range(4, 6), 8, g16[:, 512:1024], tg, tmp16, 0)
    t_n = V.last()
    w, tw = weight()
    used(project(w, tw, 8, 0, 512, hT, range(6), lambda t: Vn[:, t, :]))
    for n in range(2):
        w, tw = weight()
        for j in range(4):
            tok = project_T(w, tw, 8, j * 128, 128, hT, [(0, 512)], silu2_T(yT[:, 4 * n + j, :], gtmp))
        used(tok)
    f = barrier()
    qTn = sb(BIG, 4, 512)
    kTn = sb(BIG + 2048, 4, 768)
    head_transposes(QKw, lambda j: kTw, 4, (4,), [])
    t_s = swap(kS, kTw, V.last(), A.last())
    for j in range(4):
        b = bank()
        PE.need(pf[b])
        for t in range(4):
            m = nc.tensor.transpose(PS[:, b, t * 128:t * 128 + 128], QKw[:, t, j * 128:j * 128 + 128], ident[:, :])
        pf[b] = evac(qTw[:, j, :], PS[:, b, :], PE.done(m))
    for j in range(4):
        b = bank()
        PE.need(pf[b])
        for t in range(4):
            m = nc.tensor.transpose(PS[:, b, t * 128:t * 128 + 128], QKn[:, t, j * 128:j * 128 + 128], ident[:, :])
        pf[b] = evac(qTn[:, j, :], PS[:, b, :], PE.done(m))
    head_transposes(QKn, lambda j: kTn[:, j - 4, :], 4, (4, 5, 6, 7), [])
    P, PT = P_buffers(BIG + 14848), grid(BIG + 10240, 3, 512)
    wm = sb(BIG + 11776, 384)
    sink = sb(BIG + 12160, 8)
    cm = sb(BIG + 12168, 64)
    rp = grid(BIG + 27648, 3, 15, 64)
    f = barrier()
    t_c = [MQ.go(wm, D["wmask"], *f), MQ.go(sink, bcast(D["win_sink"], 0, 128), *f), MQ.go(cm, D["cmask"], *f)]
    V.need(*t_c)
    A.need(*t_c)
    G.need(*t_c)
    rtok = {}

    def load_rpb(h):
        t = MQ.go(rp[h % 3], D["rpx"][h], V.last())
        rtok[h] = G.tt(rp[h % 3], rp[h % 3], bcast(cm, 1, 15), ALU.add, t)
    jobs = []
    for pair in range(4):
        for half in range(2):
            h = pair * 2 + half
            g = h // 4
            ksrc = kTw if g == half else kS
            lo = half * 64

            def span(q):
                return max(0, q - 1), min(4, q + 2)

            def sc(q, pair=pair, lo=lo, ksrc=ksrc):
                l = qTw[lo:lo + 64, pair, q * 128:q * 128 + 128]
                a, b = span(q)
                return [(0, (b - a) * 128, l, ksrc[lo:lo + 64, a * 128:b * 128]),
                        (512, 256, l, ksrc[lo:lo + 64, 512:768])]

            def segs(q):
                a, b = span(q)
                m0 = (a - q + 1) * 128
                return (512, 768), (0, (b - a) * 128, wm[:, m0:m0 + (b - a) * 128])
            ob = 6 + pair % 2
            keys = [(lambda q, c=kt * 128: c, 128, 0, 4, Vw[:, kt, g * 64:g * 64 + 64]) for kt in (4, 5)]
            keys += [(lambda q, kt=kt: (kt - max(0, q - 1)) * 128, 128, max(0, kt - 1), min(4, kt + 2),
                      Vw[:, kt, g * 64:g * 64 + 64]) for kt in range(4)]
            jobs.append(dict(nq=4, scores=sc, segs=segs, out=(ob, half), first=True, last=True,
                             after=t_s if g != half else [],
                             sink=sink[:, h:h + 1], keys=keys, final=yfinal(pair, 0, 512, ob) if half else None))
    for pair in range(4):
        for half in range(2):
            h = pair * 2 + half
            lo = half * 64

            def sc(q, pair=pair, lo=lo, h=h):
                if q == 0:
                    if h == 0:
                        load_rpb(0)
                    if h < 7:
                        load_rpb(h + 1)
                l = qTn[lo:lo + 64, pair, q * 128:q * 128 + 128]
                return [(0, 512, l, kTn[lo:lo + 64, pair, 0:512]), (512, 256, l, kTn[lo:lo + 64, pair, 512:768])]

            def segs(q, h=h):
                V.need(rtok[h])
                s = 7 - 2 * q
                return (512, 768), (0, 512, rp[h % 3][:, s:s + 8, :].rearrange("p a b -> p (a b)"))
            ob = 6 + pair % 2
            jobs.append(dict(nq=4, scores=sc, segs=segs, out=(ob, half), first=True, last=True,
                             keys=[(lambda q, c=kt * 128: c, 128, 0, 4, Vn[:, kt, h * 64:h * 64 + 64])
                                   for kt in range(6)],
                             final=yfinal(4 + pair, 0, 512, ob) if half else None))
    attention(jobs, P, PT)
    f = barrier()
    T5B = BIG + 10240
    tab = sb(T5B, 8)
    oh = sb(T5B + 8, 640)
    tabb = grid(T5B + 700, 2, 128)
    ut = grid(T5B + 1000, 2, 640)
    T5 = sb(END - 4096, 8, 512)
    V.zero(tab[0:64, :], NEG)
    t4 = MQ.go(tab[0:32, :], D["t5"], V.last())
    t5_ = MQ.go(oh[0:33, :], D["onehot"], *f)
    scr = nc.dram_tensor("t5_rows", [8, 128 * 640], F32)
    tbs = []
    t5s = []
    for h in range(8):
        V.copy(tabb[h % 2][0:33, :], tab[0:33, h:h + 1].to_broadcast([33, 128]), t4, PE.last())
        tk = V.last()
        for c0, n in ((0, 512), (512, 128)):
            b = bank()
            tok = group(PS[:, b, 0:n], [(tabb[h % 2][0:33, :], oh[0:33, c0:c0 + n])], pf[b], tk, t5_)
            pf[b] = V.copy(ut[h % 2][:, c0:c0 + n], PS[:, b, 0:n], tok, tbs[-2] if len(tbs) > 1 else None)
        sv = bass.AP(scr, h * 81920, [[640, 128], [1, 640]])
        tw_ = MQ.go(sv, ut[h % 2], V.last())
        tbs.append(tw_)
        t6 = MQ.go(T5[:, h, :], bass.AP(scr, h * 81920 + 127, [[639, 128], [1, 512]]), tw_)
        t5s.append(t6)

    GB = [sb(BIG, 1024)]
    tmp = grid(BIG + 2048, 2, 512)
    gates(GB, 1, None)
    out_proj(yT, 4, GB, [V.last(), A.last()], tmp)
    f = barrier()

    xT = sb(BIG, 8, 512)
    oT = sb(BIG + 4096, 8, 512)
    B2 = BIG + 8192
    GBL = END - 6144
    XT = XR + 4096
    maskT = sb(XT, 512)
    tri = sb(XT + 512, 512)
    vmask = sb(XT + 1024, 8)
    t1 = MQ.go(maskT, D["cmask2"], *f)
    t2 = MQ.go(tri, D["tri"], *f)
    t3 = MQ.go(vmask, D["vmask"], *f)
    for e in (PE, V, A, G):
        e.need(t1, t2, t3, t5s)

    gb = [sb(GBL, 1024), sb(GBL + 1024, 1024)]

    def load_gb(n, *after):
        l, i = n // 3, n % 3
        return [MQ.go(gb[0], bcast(D["ln_g_2"][l, i], 0, 128), *after),
                MQ.go(gb[1], bcast(D["ln_b_2"][l, i], 0, 128), *after)]

    def norm_tile(t, gtok):
        mv = small[:, t * 32:t * 32 + 32]
        for h in range(2):
            V.begin(())
            V.done(nc.vector.bn_stats(mv[:, h * 6:h * 6 + 6], X[:, t, h * 512:h * 512 + 512]))
        V.begin(())
        V.done(nc.vector.bn_aggr(mv[:, 12:14], mv[:, 0:12]))
        V.ts1(mv[:, 14:15], mv[:, 13:14], LN_EPS, ALU.add)
        rsqrt(mv[:, 15:16], mv[:, 14:15], mv[:, 16:17], V.last())
        x = X[:, t, :]
        V.ts(x, x, mv[:, 12:13], ALU.subtract, mv[:, 15:16], ALU.mult)
        V.tt(x, x, gb[0], ALU.mult, gtok)
        return V.tt(x, x, gb[1], ALU.add)

    def tile_T(t, tok):
        for h in range(2):
            b = bank()
            PE.need(pf[b], tok)
            for i in range(4):
                k = h * 4 + i
                m = nc.tensor.transpose(PS[:, b, i * 128:i * 128 + 128], X[:, t, k * 128:k * 128 + 128], ident[:, :])
            dst = xT[:, h * 4:h * 4 + 4, t * 128:t * 128 + 128]
            src = PS[:, b, :].rearrange("p (k c) -> p k c", k=4)
            pf[b] = A.act(dst, src, ACT.Copy, PE.done(m))

    def residual(products, n, more=True):
        prev = None
        for t in range(4):
            for h in range(2):
                b, tok = products(t, h)
                x = X[:, t, h * 512:h * 512 + 512]
                pf[b] = V.stt(x, x, ALPHA, PS[:, b, :], ALU.mult, ALU.add, tok)
            tn = norm_tile(t, gbt[0])
            if more and prev is not None:
                tile_T(*prev)
            prev = (t, tn)
        if more:
            tile_T(*prev)
            gbt[0] = load_gb(n + 1, V.last())
        PE.need(V.last(), A.last())
        return V.last()

    def from_chunks(lhs_of, kt, parts, ready):
        def products(t, h):
            w, tw = parts[h]
            b = bank()
            return b, group(PS[:, b, :], [(lhs_of(k, t), w[:, k, :]) for k in range(kt)], pf[b], tw, *ready)
        return products

    gbt = [load_gb(0, *f)]

    def plain_final(dst, ob):
        return lambda tok: evac(dst, PS[:, ob, :], tok)

    for t in range(4):
        tile_T(t, V.last())
    for l in range(2):
        nqT = sb(B2, 4, 512)
        kkT = sb(B2 + 2048, 4, 512)
        kss = sb(B2 + 4096, 2, 512)
        vv = sb(B2 + 5120, 4, 2, 128)
        gt = sb(B2 + 6144, 4, 24)
        CC = sb(B2 + 6240, 2, 512)
        pe = sb(B2 + 7264, 2, 16)
        w2 = sb(B2 + 7328, 2, 64)
        hid = sb(B2 + 7456, 3, 128)
        hidT = sb(B2 + 7840, 64)
        kc2 = sb(B2 + 7904, 32)
        kcs = sb(B2 + 7936, 32)
        vc2 = sb(B2 + 7968, 2, 64)
        pcb = sb(B2 + 8096, 2, 4, 32)
        cs_ = sb(B2 + 8352, 2, 512)
        PB = B2 + 8352
        f = barrier()
        tpe = MQ.go(pe, D["peT"][l], *f)
        tw2 = MQ.go(w2, D["cmpw2"][l], *f)
        G.zero(vc2, 0.0)
        G.zero(pcb, 0.0)
        w, tw = weight()
        for j in range(4):
            tok = project_T(w, tw, 8, j * 128, 128, xT, [(0, 512)],
                            lambda t0, n, ps, tok, j=j: evac(nqT[:, j, :], ps, tok, scale=0.125),
                            V.last(), A.last())
        used(tok)
        w, tw = weight()
        for j in range(3):
            tok = project_T(w, tw, 8, j * 128, 128, xT, [(0, 512)],
                            lambda t0, n, ps, tok, j=j: evac(kkT[:, j, :], ps, tok))
        used(project(w, tw, 8, 384, 128, xT, range(4), lambda t: vv[:, t, 0, :]))
        w, tw = weight()
        tok = project_T(w, tw, 8, 0, 128, xT, [(0, 512)], lambda t0, n, ps, tok: evac(kkT[:, 3, :], ps, tok))

        def ev_vg(dst, ps, tok):
            V.copy(dst[0], ps[:, 0:128], tok)
            return V.copy(dst[1], ps[:, 128:152])
        used(project(w, tw, 8, 128, 152, xT, range(4), lambda t: (vv[:, t, 1, :], gt[:, t, :]), ev_vg))
        t = A.act(gt, gt, ACT.Tanh, V.last(), scale=0.5)
        V.ts(gt, gt, 0.5, ALU.mult, 0.5, ALU.add, t)
        t_s = swap(kss[:, 0, :], kkT[:, 2, :], V.last(), A.last()) + swap(kss[:, 1, :], kkT[:, 3, :], V.last(), A.last())
        t_cs = [swap(cs_[:, kv, :], kkT[:, kv, :], V.last(), A.last()) for kv in range(2)]
        for kv in range(2):
            V.need(tpe, t_cs[kv])
            V.zero(CC[64:128, :, 496:512], 0.0, PE.last())
            for g in range(2):
                for a in range(2):
                    src = (kkT if g == a else cs_)[a * 64:a * 64 + 64, kv, 16 * a:512]
                    n = 32 - a
                    V.tt(CC[a * 64:a * 64 + 64, g, 0:16 * n].rearrange("p (n l) -> p n l", l=16),
                         src.rearrange("p (n l) -> p n l", l=16), bcast(pe[a * 64:a * 64 + 64, kv, :], 1, n), ALU.add)
            w, tw = weight()
            b = bank()
            cf = CC.rearrange("p g t -> p (g t)")
            tok = group(PS[0:64, b, 0:128], [(cf[:, i:i + 16 * 63 + 1:16], w[:, i, :]) for i in range(16)],
                        pf[b], tw, V.last())
            used(tok)
            hx, hy, gx = hid[0:64, 0, :], hid[0:64, 1, :], hid[0:64, 2, :]
            pf[b] = V.copy(hx, PS[0:64, b, 0:128], tok)
            V.tt(hy, hx, hx, ALU.mult)
            V.ts(hy, hy, 0.044715, ALU.mult, 1.0, ALU.add)
            V.tt(hy, hy, hx, ALU.mult)
            t = A.act(hy, hy, ACT.Tanh, V.last(), scale=math.sqrt(2.0 / math.pi))
            V.stt(gx, hy, 1.0, hx, ALU.add, ALU.mult, t)
            V.ts1(gx, gx, 0.5, ALU.mult)
            b = bank()
            PE.need(pf[b], V.last())
            m = nc.tensor.transpose(PS[:, b, 0:64], gx, ident[0:64, 0:64])
            pf[b] = V.copy(hidT, PS[:, b, 0:64], PE.done(m))
            b = bank()
            if kv == 0:
                for g in range(2):
                    tok = group(PS[g * 64:g * 64 + 64, b, 0:31], [(w2[:, 0, :], hidT[:, g * 32:g * 32 + 31])],
                                pf[b], V.last(), tw2)
                pf[b] = V.copy(kc2[:, 0:31], PS[:, b, 0:31], tok)
                t_s += swap(kcs[:, 0:31], kc2[:, 0:31], V.last())
            else:
                for g in range(2):
                    tok = group(PS[0:31, b, g * 64:g * 64 + 64], [(hidT[:, g * 32:g * 32 + 31], w2[:, 1, :])],
                                pf[b], V.last(), tw2)
                pf[b] = V.copy(vc2[0:31, :, :], PS[0:31, b, 0:128].rearrange("p (g c) -> p g c", g=2), tok, G.last())
        f = barrier()
        P, PT = P_narrow(PB), grid(PB + 4096, 3, 512)
        gview = gt.rearrange("p t (h b) -> p t h b", b=3)
        jobs = []
        for pair in range(4):
            for half in range(2):
                h = pair * 2 + half
                g = h // 4
                lo = half * 64
                ob = 6 + pair % 2

                def gate(br, h=h):
                    return lambda q: gview[:, q, h, br:br + 1]

                for br in (1, 2, 0):
                    if br:
                        ksrc = kkT[:, 1 + br, :] if g == half else kss[:, br - 1, :]

                        def sc(q, pair=pair, lo=lo, ksrc=ksrc):
                            l = nqT[lo:lo + 64, pair, q * 128:q * 128 + 128]
                            return [(0, (q + 1) * 128, l, ksrc[lo:lo + 64, 0:(q + 1) * 128])]

                        def segs(q, h=h):
                            return None, (0, (q + 1) * 128, T5[:, h, 384 - 128 * q:512])
                        keys = [(lambda q, c=kt * 128: c, 128, kt, 4, vv[:, kt, br - 1, g * 64:g * 64 + 64])
                                for kt in range(4)]
                        jobs.append(dict(nq=4, scores=sc, segs=segs, out=(ob, half), first=br == 1, last=False,
                                         after=t_s, gate=gate(br), keys=keys))
                    else:
                        ksrc = kc2 if g == half else kcs

                        def sc(q, pair=pair, lo=lo, ksrc=ksrc):
                            l = nqT[lo:lo + 64, pair, q * 128:q * 128 + 128]
                            n = min(31, 8 * q + 7)
                            return [(0, n, l, ksrc[lo:lo + 64, 0:n])]

                        def segs(q, h=h):
                            n = min(31, 8 * q + 7)
                            c = 415 - 128 * q
                            return None, (0, n, T5[:, h, c:c + 16 * (n - 1) + 1:16])
                        jobs.append(dict(nq=4, scores=sc, segs=segs, out=(ob, half), first=False, last=True,
                                         gate=gate(0), P=[pcb[:, half, q, :] for q in range(4)],
                                         valid=lambda q: vmask[:, 0:7] if q == 0 else None,
                                         keys=[(lambda q: 0, 32, 0, 4, vc2[0:32, g, :])],
                                         final=plain_final(oT[:, pair, :], ob) if half else None))
        attention(jobs, P, PT, wide=False)
        f = barrier()

        cq = sb(B2, 4, 544)
        km = sb(B2 + 2176, 4, 384)
        vm = sb(B2 + 3712, 4, 256)
        qmT = sb(B2 + 4736, 4, 512)
        kmT = sb(B2 + 6784, 4, 512)
        PB = B2 + 8832
        qm = sb(PB, 4, 384)
        cT_ = sb(PB + 1536, 4, 512)
        gq = sb(PB + 3584, 512)
        tmpm = sb(PB + 4096, 512)
        tg = MQ.go(gq, bcast(D["mlag"][l], 0, 128), *f)
        w, tw = weight()
        for t in range(4):
            for c0, n in ((0, 384), (384, 160)):
                b = bank()
                tok = group(PS[:, b, 0:n], [(xT[:, k, t * 128:t * 128 + 128], w[:, k, c0:c0 + n]) for k in range(8)],
                            pf[b], tw)
                pf[b] = evac(cq[:, t, c0:c0 + n], PS[:, b, 0:n], tok)
        used(tok)
        V.need(A.last())
        for t in range(4):
            V.tt(tmpm[:, 0:512], cq[:, t, 0:512], cq[:, t, 0:512], ALU.mult)
            V.red(small[:, t:t + 1], tmpm[:, 0:384], ALU.add)
            V.red(small[:, 4 + t:5 + t], tmpm[:, 384:512], ALU.add)
        V.ts(small[:, 0:4], small[:, 0:4], 1.0 / 384, ALU.mult, EPS, ALU.add)
        V.ts(small[:, 4:8], small[:, 4:8], 1.0 / 128, ALU.mult, EPS, ALU.add)
        rsqrt(small[:, 8:16], small[:, 0:8], small[:, 16:24], V.last())
        for t in range(4):
            V.stt(cq[:, t, 0:384], cq[:, t, 0:384], small[:, 8 + t:9 + t], gq[:, 0:384], ALU.mult, ALU.mult, tg)
            V.stt(cq[:, t, 384:512], cq[:, t, 384:512], small[:, 12 + t:13 + t], gq[:, 384:512], ALU.mult, ALU.mult)
        flip(lambda k: cT_[:, k, :], lambda k, t: cq[:, t, k * 128:k * 128 + 128], range(4), range(4),
             after=[V.last()])
        w, tw = weight()
        V.need(A.last())
        used(project(w, tw, 3, 0, 384, cT_, range(4), lambda t: qm[:, t, :],
                     lambda d, s, tok: evac(d, s, tok, scale=96 ** -0.5), V.last(), A.last()))
        w, tw = weight()

        def ev_kv(t, ps, tok):
            v4 = ps.rearrange("p (h c) -> p h c", h=4)
            V.copy(km[:, t, :].rearrange("p (h c) -> p h c", h=4)[:, :, 0:64], v4[:, :, 0:64], tok)
            return V.copy(vm[:, t, :].rearrange("p (h c) -> p h c", h=4), v4[:, :, 64:128])
        used(project(w, tw, 1, 0, 512, cT_[:, 3:4, :], range(4), lambda t: t, ev_kv))
        V.need(A.last())
        for t in range(4):
            kr = cq[:, t, 512:544]
            q4 = qm[:, t, :].rearrange("p (h c) -> p h c", h=4)
            k4 = km[:, t, :].rearrange("p (h c) -> p h c", h=4)
            c, s = cos2[:, t, :], sin2[:, t, :]
            c4, s4 = bcast(c, 1, 4), bcast(s, 1, 4)
            u = [tmpm[:, i * 64:(i + 1) * 64].rearrange("p (h d) -> p h d", h=4) for i in range(4)]
            a, b_ = q4[:, :, 64:80], q4[:, :, 80:96]
            V.tt(u[0], a, c4, ALU.mult)
            V.tt(u[1], b_, s4, ALU.mult)
            V.tt(u[2], a, s4, ALU.mult)
            V.tt(u[3], b_, c4, ALU.mult)
            V.tt(a, u[0], u[1], ALU.subtract)
            V.tt(b_, u[2], u[3], ALU.add)
            r = [tmpm[:, 256 + i * 16:272 + i * 16] for i in range(6)]
            V.tt(r[0], kr[:, 0:16], c, ALU.mult)
            V.tt(r[1], kr[:, 16:32], s, ALU.mult)
            V.tt(r[2], kr[:, 0:16], s, ALU.mult)
            V.tt(r[3], kr[:, 16:32], c, ALU.mult)
            V.tt(r[4], r[0], r[1], ALU.subtract)
            V.tt(r[5], r[2], r[3], ALU.add)
            V.copy(k4[:, :, 64:96], bcast(tmpm[:, 320:352], 1, 4))
        flip(lambda h: qmT[0:96, h, :], lambda h, t: qm[:, t, h * 96:h * 96 + 96], range(4), range(4), m=96,
             after=[V.last()])
        flip(lambda h: kmT[0:96, h, :], lambda h, t: km[:, t, h * 96:h * 96 + 96], range(4), range(4), m=96)
        barrier()
        P, PT = P_narrow(PB), grid(PB + 4096, 3, 512)
        jobs = []
        for h in range(4):
            half, ob = h % 2, 6 + h // 2

            def sc(q, h=h):
                return [(0, (q + 1) * 128, qmT[0:96, h, q * 128:q * 128 + 128], kmT[0:96, h, 0:(q + 1) * 128])]
            jobs.append(dict(nq=4, scores=sc,
                             segs=lambda q: (None, (0, (q + 1) * 128, maskT[:, 384 - 128 * q:512])),
                             out=(ob, half), first=True, last=True,
                             keys=[(lambda q, c=kt * 128: c, 128, kt, 4, vm[:, kt, h * 64:h * 64 + 64])
                                   for kt in range(4)],
                             final=plain_final(oT[:, 4 + h // 2, :], ob) if half else None))
        attention(jobs, P, PT, wide=False)
        f = barrier()

        fqT = sb(B2, 4, 512)
        fv = sb(B2 + 2048, 4, 256)
        ff = sb(B2 + 3072, 4, 4)
        lsn = sb(B2 + 3088, 4, 4)
        cum = sb(B2 + 3104, 4, 4)
        ft = sb(B2 + 3120, 16)
        bf = sb(B2 + 3140, 4)
        Bk = sb(B2 + 3200, 4, 512)
        PB = B2 + 5248
        tbf = MQ.go(bf, bcast(D["fox_b_f_2"][l], 0, 128), *f)
        w, tw = weight()
        for j in range(4):
            tok = project_T(w, tw, 8, j * 128, 128, xT, [(0, 512)],
                            lambda t0, n, ps, tok, j=j: evac(fqT[:, j, :], ps, tok, scale=0.125 if j < 2 else None))
        used(tok)
        w, tw = weight()

        def ev_fv(t, ps, tok):
            V.copy(fv[:, t, :], ps[:, 0:256], tok)
            return V.tt(ff[:, t, :], ps[:, 256:260], bf, ALU.add, tbf)
        used(project(w, tw, 8, 0, 260, xT, range(4), lambda t: t, ev_fv))
        fl = ff.rearrange("p a b -> p (a b)")
        ll = lsn.rearrange("p a b -> p (a b)")
        V.stt(ft, fl, -1.0, fl, ALU.mult, ALU.max)
        t = A.act(ft, ft, ACT.Exp, V.last(), scale=-1.0)
        t = A.act(ft, ft, ACT.Ln, bias=ones[:, 0:1])
        V.stt(ll, fl, 0.0, ft, ALU.min, ALU.subtract, t)
        for i in range(4):
            b = bank()
            tok = group(PS[:, b, 0:4], [(tri[:, (i - j) * 128:(i - j) * 128 + 128], lsn[:, j, :])
                                        for j in range(i + 1)], pf[b], V.last())
            pf[b] = V.copy(cum[:, i, :], PS[:, b, 0:4], tok)
        V.ts1(ll, ll, -1.0, ALU.mult, PE.last())
        for h in range(4):
            b = bank()
            PE.need(pf[b], V.last())
            for j in range(4):
                m = nc.tensor.matmul(PS[:, b, 128 * j:512], lsn[:, j, h:h + 1].to_broadcast([128, 128]),
                                     tri[:, 0:512 - 128 * j], start=(j == 0), stop=(j == 3))
            pf[b] = evac(Bk[:, h, :], PS[:, b, :], PE.done(m))
        f = barrier()
        P, PT = P_narrow(PB), grid(PB + 4096, 3, 512)
        jobs = []
        for h in range(4):
            half, ob, lo = h % 2, 6 + h // 2, (h % 2) * 64

            def sc(q, h=h, lo=lo):
                return [(0, (q + 1) * 128, fqT[lo:lo + 64, h // 2, q * 128:q * 128 + 128],
                         fqT[lo:lo + 64, 2 + h // 2, 0:(q + 1) * 128])]
            jobs.append(dict(nq=4, scores=sc,
                             segs=lambda q: (None, (0, (q + 1) * 128, maskT[:, 384 - 128 * q:512])),
                             pre=lambda q, h=h: (cum[:, q, h:h + 1], Bk[:, h, 0:(q + 1) * 128]),
                             out=(ob, half), first=True, last=True,
                             keys=[(lambda q, c=kt * 128: c, 128, kt, 4, fv[:, kt, h * 64:h * 64 + 64])
                                   for kt in range(4)],
                             final=plain_final(oT[:, 6 + h // 2, :], ob) if half else None))
        attention(jobs, P, PT, wide=False)
        f = barrier()

        mg = sb(B2, 8, 512)
        brv = sb(B2 + 4096, 8, 512)
        gm = grid(B2 + 8192, 2, 512)
        for br, k0, kt in ((0, 0, 4), (1, 4, 2), (2, 6, 2)):
            w, tw = weight()
            for m_ in range(8):
                tok = project_T(w, tw, kt, m_ * 128, 128, oT[:, k0:k0 + kt, :], [(0, 512)],
                                lambda t0, n, ps, tok, m_=m_: evac(brv[:, m_, :], ps, tok, V.last(), G.last()))
            used(tok)
            for n in range(2):
                w, tw = weight()
                for s in range(4):
                    m_ = n * 4 + s
                    gmb = gm[m_ % 2]

                    def ev(t0, nn, ps, tok, m_=m_, gmb=gmb, br=br):
                        a = A.act(gmb, ps, ACT.Tanh, tok, V.last(), G.last(), scale=0.5)
                        V.need(A.last())
                        if br == 0:
                            V.stt(mg[:, m_, :], gmb, 1.0, brv[:, m_, :], ALU.add, ALU.mult, a)
                        else:
                            V.stt(gmb, gmb, 1.0, brv[:, m_, :], ALU.add, ALU.mult, a)
                            G.tt(mg[:, m_, :], mg[:, m_, :], gmb, ALU.add, V.last())
                        return a
                    tok = project_T(w, tw, 8, s * 128, 128, xT, [(0, 512)], ev)
                used(tok)
        V.need(G.last())
        V.ts1(mg, mg, 0.5, ALU.mult)
        ws = [weight(), weight()]
        tn = residual(from_chunks(lambda k, t: mg[:, k, t * 128:t * 128 + 128], 8, ws, [V.last()]), 3 * l)
        used(PE.last())
        used(PE.last())
        f = barrier()
        mem = sb(B2, 2, 1024)
        memT = sb(B2 + 2048, 8, 256)
        qa = sb(B2 + 4096, 2, 512)
        ka = sb(B2 + 5120, 2, 256)
        va = sb(B2 + 5632, 2, 256)
        PB = B2 + 6144
        tm = MQ.go(mem, D["mem_2"].rearrange("(t p) d -> p t d", p=128), *f)
        for k in range(8):
            b = bank()
            PE.need(pf[b], tm)
            for t in range(2):
                m = nc.tensor.transpose(PS[:, b, t * 128:t * 128 + 128], mem[:, t, k * 128:k * 128 + 128], ident[:, :])
            pf[b] = evac(memT[:, k, :], PS[:, b, 0:256], PE.done(m))
        w, tw = weight()
        for j in range(2):
            tok = project_T(w, tw, 8, j * 128, 128, xT, [(0, 512)],
                            lambda t0, n, ps, tok, j=j: evac(qa[:, j, :], ps, tok, scale=0.125), V.last(), A.last())
        used(tok)
        w, tw = weight()
        for j in range(2):
            tok = project_T(w, tw, 8, j * 128, 128, memT, [(0, 256)],
                            lambda t0, n, ps, tok, j=j: evac(ka[:, j, :], ps, tok))
        used(project(w, tw, 8, 256, 256, memT, range(2), lambda t: va[:, t, :]))
        barrier()
        P, PT = P_narrow(PB), grid(B2, 3, 512)
        jobs = []
        for h in range(4):
            half, ob, lo = h % 2, 6 + h // 2, (h % 2) * 64

            def sc(q, h=h, lo=lo):
                return [(0, 256, qa[lo:lo + 64, h // 2, q * 128:q * 128 + 128], ka[lo:lo + 64, h // 2, :])]
            jobs.append(dict(nq=4, scores=sc, segs=lambda q: ((0, 256), None), out=(ob, half), first=True,
                             last=True,
                             keys=[(lambda q, c=kt * 128: c, 128, 0, 4, va[:, kt, h * 64:h * 64 + 64])
                                   for kt in range(2)],
                             final=plain_final(oT[:, h // 2, :], ob) if half else None))
        attention(jobs, P, PT, wide=False)
        barrier()
        w, tw = weight()
        ws = [(w[:, :, 0:512], tw), (w[:, :, 512:1024], tw)]
        residual(from_chunks(lambda k, t: oT[:, k, t * 128:t * 128 + 128], 2, ws, [V.last()]), 3 * l + 1)
        used(PE.last())
        f = barrier()
        hd = sb(BIG + 4096, 32, 512)
        rl = grid(BIG + 4096 + 16384, 2, 512)
        for n in range(8):
            w, tw = weight()
            for s in range(4):
                j = n * 4 + s

                def ev(t0, nn, ps, tok, j=j):
                    a = A.act(rl[j % 2], ps, ACT.Relu, tok, V.last())
                    V.tt(hd[:, j, :], rl[j % 2], rl[j % 2], ALU.mult, a)
                    return a
                tok = project_T(w, tw, 8, s * 128, 128, xT, [(0, 512)], ev)
            used(tok)
        PE.need(V.last())
        bs = {(t, h): (t * 2 + h) for t in range(4) for h in range(2)}
        for b in range(8):
            PE.need(pf[b])

        def down(t, h, r, w, tw):
            PE.need(tw)
            for k in range(8):
                m = nc.tensor.matmul(PS[:, bs[t, h], :], hd[:, r * 8 + k, t * 128:t * 128 + 128], w[:, k, :],
                                     start=(r == 0 and k == 0), stop=(r == 3 and k == 7))
            return PE.done(m)
        for r in range(3):
            for h in range(2):
                w, tw = weight()
                for t in range(4):
                    tok = down(t, h, r, w, tw)
                used(tok)
        ws = [weight(), weight()]
        rot["b"] = 7
        t = residual(lambda t, h: (bs[t, h], down(t, h, 3, *ws[h])), 3 * l + 2, more=l == 0)
        used(PE.last())
        used(PE.last())
    t = MQ.go(out.rearrange("(t p) d -> p t d", p=128), X[:, 0:4, :], t)
    barrier()
    for s, v in zip(MQ.sems, MQ.vals):
        G.need((s, v))
    for s, v in zip(WQ.sems, WQ.vals):
        WQ.w.need((s, v))


def constants():
    f = np.float32
    c = {"ident": np.eye(128, dtype=f)}
    t = np.arange(512)
    inv = (f(10000.0) ** (-np.arange(16, dtype=f) / f(16))).astype(f)
    ang = np.concatenate([(t // 64).astype(f)[:, None] * inv, (t % 64).astype(f)[:, None] * inv], -1)
    c["cos1"], c["sin1"] = np.cos(ang).astype(f), np.sin(ang).astype(f)
    ang = t.astype(f)[:, None] * inv[None, :]
    c["cos2"], c["sin2"] = np.cos(ang).astype(f), np.sin(ang).astype(f)
    k = np.arange(512)
    tk = (t[:, None] * k[None, :]) % 1024
    cs, sn = np.cos(2 * np.pi * tk / 1024), np.sin(2 * np.pi * tk / 1024)
    alt = np.where(t % 2 == 0, 1.0, -1.0)
    fi = -sn.copy()
    fi[:, 0] = alt
    c["dftf"] = np.concatenate([cs, fi], 1).astype(f)
    gr = 2 * cs.T / 1024
    gr[0] = 1 / 1024
    gi = -2 * sn.T / 1024
    gi[0] = alt / 1024
    c["dftg"] = np.concatenate([gr, gi], 0).astype(f)
    t2 = np.arange(256)
    tk = (t2[:, None] * t2[None, :]) % 512
    gi2 = -2 * np.sin(2 * np.pi * tk / 512) / 1024
    gi2[0] = np.where(t2 % 2 == 0, 1.0, -1.0) / 1024
    c["g2i"] = gi2.astype(f)
    z = []
    for n in (512, 256):
        tt = np.linspace(0.0, 1.0, n, dtype=f)[:, None]
        w = (2.0 * np.pi * np.arange(n, dtype=f)[:, None] / f(n)).astype(f)
        fb = np.linspace(1e-4, 15, 16, dtype=f)[None, :]
        z.append(np.concatenate([tt, np.cos((fb * w).astype(f)), -np.sin((fb * w).astype(f))], -1).astype(f))
        d = np.linspace(math.log(1e-2) / 1.5, math.log(1e-2) / 0.3, 512, dtype=f)
        c["decay1" if n == 512 else "decay2"] = np.exp(-tt * np.abs(d)).astype(f)
    c["hyz"] = np.ascontiguousarray(np.concatenate(z, 0).T)
    p, j = np.arange(128)[:, None], np.arange(384)[None, :]
    c["wmask"] = np.where(np.abs(j - 128 - p) <= 128, 0.0, NEG).astype(f)
    col, kc = np.arange(128)[:, None] % 64, np.arange(64)[None, :]
    c0 = np.clip(col - 8, 0, 48)
    c["cmask"] = np.where((kc >= c0) & (kc < c0 + 16), 0.0, NEG).astype(f)
    j = np.arange(512)[None, :]
    c["cmask2"] = np.where(p - j + 384 >= 0, 0.0, NEG).astype(f)
    c["tri"] = (p <= j).astype(f)
    cc = np.arange(8)[None, :]
    c["vmask"] = (p - 16 * cc - 31 >= 0).astype(f)
    dist = 511 - np.arange(640)
    n = np.maximum(dist, 0)
    nf = np.maximum(n, 1).astype(f)
    large = 16 + (np.log(nf / f(16)) / f(math.log(128 / 16)) * f(16)).astype(np.int32)
    bucket = np.where(n < 16, n, np.minimum(large, 31))
    oh = np.zeros((33, 640), f)
    for i in range(639):
        oh[bucket[i] if dist[i] >= 0 else 32, i] = 1.0
    c["onehot"] = oh
    return c


def layouts(I):
    f = np.float32
    L = {}
    L["cT"] = np.stack([I["c"][0].reshape(8, 128).T, I["c_ctx"].reshape(8, 128).T], -1)
    L["b_adaT"] = I["b_ada"].reshape(2, 24, 128).transpose(0, 2, 1)
    L["norm_gT"] = I["norm_g"].reshape(2, 8, 128).transpose(0, 2, 1)
    L["g10_0"] = np.concatenate([np.tile(I["glob_q_norm"][0], 8), np.tile(I["glob_k_norm"][0], 2)])
    L["g10_1"] = np.concatenate([np.tile(I["win_q_norm"][0], 8), np.tile(I["win_k_norm"][0], 2)])
    L["g16"] = np.concatenate([np.tile(I["nat_q_norm"][0], 8), np.tile(I["nat_k_norm"][0], 8)])
    L["convT"] = np.concatenate([I["hy_conv_w"][0], I["hy_conv_b"]], 0).reshape(4, 12, 128).transpose(2, 1, 0)
    L["hyb"] = np.stack([I["hy_freq"][0], I["hy_b1"][0], I["hy_b2"][0]], 1)
    rp = np.zeros((8, 15, 127), f)
    rp[:, :, 48:79] = I["nat_rpb"][0]
    at = np.arange(64)[None, :] - np.arange(64)[:, None] + 63
    lo = rp[:, :, at].transpose(0, 2, 1, 3)
    x = np.zeros((8, 128, 15, 64), f)
    x[:, 0:64] = lo
    x[:, 64:128, 1:15] = lo[:, :, 0:14]
    L["rpx"] = x
    pe = I["cmp_pe_2"].reshape(2, 2, 2, 16, 64)
    L["peT"] = pe.transpose(0, 2, 4, 1, 3).reshape(2, 128, 2, 16)
    L["cmpw2"] = I["cmp_w2_2"].transpose(0, 2, 1, 3)
    L["mlag"] = np.concatenate([I["mla_q_norm_2"], I["mla_kv_norm_2"]], 1)
    L["t5"] = I["t5_table_2"]
    L["x"], L["ctx"], L["mem_2"] = I["x"][0], I["ctx"][0], I["mem_2"][0]
    L["hy_w1"], L["hy_w2"], L["hy_w3"], L["hy_skip"] = I["hy_w1"][0], I["hy_w2"][0], I["hy_w3"][0], I["hy_skip"][0]
    L["win_sink"] = I["win_sink"][0]
    for n in ("w_ada", "w_in", "w_out", "w_in_2", "cmp_w1_2", "mla_w_uq_2", "mla_w_ukv_2", "fox_b_f_2", "w_gate_2",
              "w_br_nsa_2", "w_br_mla_2", "w_br_fox_2", "w_mix_out_2", "xa_w_q_2", "xa_w_kv_2", "xa_w_o_2",
              "mlp_w_up_2", "mlp_w_down_2", "ln_g_2", "ln_b_2"):
        L[n] = I[n]
    return L


def kernel(**inputs):
    import concourse.bacc as bacc
    from concourse.bass_utils import run_bass_kernel_spmd

    I = {k: np.asarray(v) for k, v in inputs.items()}
    nc = bacc.Bacc("TRN2", target_bir_lowering=False, num_devices=1)
    arrays, D = {}, {}
    for name, a in {**layouts(I), **constants()}.items():
        a = np.ascontiguousarray(a)
        arrays["in_" + name] = a
        D[name] = nc.dram_tensor("in_" + name, a.shape, F32, kind="ExternalInput").ap()
    out = nc.dram_tensor("out_x", (512, 1024), F32, kind="ExternalOutput").ap()
    program(nc, D, out)
    r = run_bass_kernel_spmd(nc, [arrays], core_ids=[0])
    return r.results[0]["out_x"].reshape(1, 512, 1024)
```

```python
import math
from contextlib import ExitStack

import numpy as np
import concourse.bass as bass
from concourse import mybir
from concourse.alu_op_type import AluOpType as ALU

F32 = mybir.dt.float32
F32R = mybir.dt.float32r
ACT = mybir.ActivationFunctionType
AX = mybir.AxisListType
FAR = 1e30
HIGH = 3e38
EPS = 1e-6
LN_EPS = 1e-5
ALPHA = 4 ** 0.25

CONST = 0
XR = 3200
RING = XR + 6144
SLOT = 4352
NSLOT = 3
BIG = RING + SLOT * NSLOT
END = 53100
T5_AT = RING
GB_AT = T5_AT + 4096
RAW = GB_AT + 2048
HL = RAW + 4096
XT_HL = HL + 8192
AREA = XT_HL + 8192
AREA_END = 53096


class Engine:

    def __init__(self, nc, eng, name, serial=True):
        self.e, self.sem, self.n, self.seen, self.serial = eng, nc.alloc_semaphore(name), 0, {}, serial

    def need(self, *toks):
        for t in toks:
            if t is None:
                continue
            if isinstance(t, list):
                self.need(*t)
                continue
            sem, v = t
            if self.seen.get(id(sem), 0) < v:
                self.e.wait_ge(sem, v)
                self.seen[id(sem)] = v

    def begin(self, toks):
        self.need(*toks)
        if self.serial and self.n:
            self.need(self.last())

    def done(self, ins):
        self.n += 1
        ins.then_inc(self.sem, 1)
        return (self.sem, self.n)

    def last(self):
        return (self.sem, self.n)

    def tt(self, out, a, b, op, *after):
        self.begin(after)
        return self.done(self.e.tensor_tensor(out, a, b, op))

    def ts(self, out, a, s1, op0, s2, op1, *after):
        self.begin(after)
        return self.done(self.e.tensor_scalar(out, a, s1, s2, op0, op1))

    def ts1(self, out, a, s1, op0, *after):
        self.begin(after)
        return self.done(self.e.tensor_scalar(out, a, s1, None, op0))

    def stt(self, out, a, s, b, op0, op1, *after):
        self.begin(after)
        return self.done(self.e.scalar_tensor_tensor(out, a, s, b, op0, op1))

    def addmin(self, out, a, b, init, acc, *after):
        self.begin(after)
        return self.done(self.e.tensor_tensor_reduce(out=out, in0=a, in1=b, scale=1.0, scalar=init,
                                                     op0=ALU.add, op1=ALU.min, accum_out=acc))

    def red(self, out, a, op, *after):
        self.begin(after)
        return self.done(self.e.tensor_reduce(out, a, AX.X, op))

    def copy(self, out, a, *after):
        self.begin(after)
        return self.done(self.e.tensor_copy(out, a))

    def zero(self, out, v, *after):
        self.begin(after)
        return self.done(self.e.memset(out, v))

    def recip(self, out, a, *after):
        self.begin(after)
        return self.done(self.e.reciprocal(out, a))

    def act(self, out, a, f, *after, bias=0.0, scale=1.0, acc=None):
        self.begin(after)
        if acc is None:
            return self.done(self.e.activation(out, a, f, bias=bias, scale=scale))
        return self.done(self.e.activation(out, a, f, bias=bias, scale=scale, accum_out=acc))


class Dmas:

    def __init__(self, nc, eng, name, n, owner=None):
        self.sems = [nc.alloc_semaphore(f"{name}{i}") for i in range(n)]
        self.vals = [0] * n
        self.k = 0
        self.w = owner or Engine(nc, eng, name + "w")
        self.eng = eng

    def go(self, out, in_, *after):
        i = self.k % len(self.sems)
        self.k += 1
        self.w.need(*after)
        if self.vals[i]:
            self.w.need((self.sems[i], self.vals[i]))
        self.eng.dma_start(out, in_).then_inc(self.sems[i], 16)
        self.vals[i] += 16
        return (self.sems[i], self.vals[i])


def bcast(ap, at, n):
    dims = [list(d) for d in ap.ap]
    dims.insert(at, [0, n])
    return bass.AP(ap.tensor, ap.offset, dims)


def rows(w, r0, kt, c0, c1):
    return w[r0:r0 + 128 * kt, c0:c1].rearrange("(k p) n -> p k n", p=128)


def program(nc, D, out):
    S = nc.alloc_sbuf_tensor("S", [128, RING], F32)
    first = ExitStack()
    regions = [(0, S), (RING, first.enter_context(nc.sbuf_tensor("S1", [128, END - RING], F32)))]
    PS = nc.alloc_psum_tensor("PS", [128, 8, 512], F32)
    PE = Engine(nc, nc.tensor, "s_pe", serial=False)
    V = Engine(nc, nc.vector, "s_dve")
    A = Engine(nc, nc.scalar, "s_act")
    G = Engine(nc, nc.gpsimd, "s_pool")
    WQ = Dmas(nc, nc.sync, "s_w", 8)
    MQ = Dmas(nc, nc.gpsimd, "s_m", 12, owner=G)
    pf = [None] * 8

    def sb(off, *dims):
        n = 1
        for d in dims:
            n *= d
        o, t = [r for r in regions if r[0] <= off][-1]
        v = t[:, off - o:off - o + n]
        if len(dims) == 2:
            v = v.rearrange("p (a b) -> p a b", a=dims[0])
        if len(dims) == 3:
            v = v.rearrange("p (a b c) -> p a b c", a=dims[0], b=dims[1])
        return v

    def barrier():
        toks = [PE.last(), V.last(), A.last(), G.last()]
        toks = [t for t in toks if t[1]]
        for e in (PE, V, A, G):
            e.need(*toks)
        return toks

    plan = []

    def want(src, *dims):
        n = 1
        for d in dims:
            n *= d
        plan.append((src, dims))

    w_ada, w_in, w_out = D["w_ada"], D["w_in"], D["w_out"]
    E_IN = [(0, 512), (512, 768), (2304, 2816), (768, 1280), (1280, 1792), (1792, 2304), (2816, 3328)]
    for n in range(6):
        want(rows(w_ada[0], 0, 8, n * 512, n * 512 + 512), 8, 512)
    for a, b in E_IN:
        want(rows(w_in[0], 0, 8, a, b), 8, b - a)
    for o in range(2):
        want(D["dftf"].rearrange("(k p) n -> p k n", p=128), 4, 1024)
        want(D["dftg"].rearrange("(k p) n -> p k n", p=128), 8, 512)
    for n in range(2):
        want(rows(w_out[0], 0, 8, n * 512, n * 512 + 512), 8, 512)
    for n in range(6):
        want(rows(w_ada[1], 0, 8, n * 512, n * 512 + 512), 8, 512)
    for a, b in [(0, 512), (512, 768), (768, 1280), (1280, 1792), (1792, 2304), (2304, 2816), (2816, 3328)]:
        want(rows(w_in[1], 0, 8, a, b), 8, b - a)
    for n in range(2):
        want(rows(w_out[1], 0, 8, n * 512, n * 512 + 512), 8, 512)
    loaded = []
    state = {"next": 0}

    def load_weight(*after):
        i = len(loaded)
        if i >= len(plan):
            return
        src, dims = plan[i]
        v = sb(RING + (i % NSLOT) * SLOT, *dims)
        if isinstance(src, tuple):
            _, l, kv = src
            w = D["cmp_w1_2"][l, kv].rearrange("(a l d) n -> a d l n", a=2, d=64)
            t = [WQ.go(v[0:64], w[0], *after), WQ.go(v[64:128], w[1], *after)]
        else:
            t = WQ.go(v, src, *after)
        loaded.append((v, t))

    for _ in range(NSLOT):
        load_weight()

    def weight():
        i = state["next"]
        state["next"] += 1
        return loaded[i]

    def used(tok):
        load_weight(tok)

    def group(dst, pairs, *after):
        PE.need(*after)
        n = len(pairs)
        for i, (l, r) in enumerate(pairs):
            m = nc.tensor.matmul(dst, l, r, start=(i == 0), stop=(i == n - 1))
        return PE.done(m)

    rot = {"b": 0, "e": 0}

    def bank():
        rot["b"] = (rot["b"] + 1) % 8
        return rot["b"]

    def evac(dst, src, tok, *after, scale=None):
        rot["e"] ^= 1
        if rot["e"]:
            if scale is None:
                return V.copy(dst, src, tok, *after)
            return V.ts1(dst, src, scale, ALU.mult, tok, *after)
        return A.act(dst, src, ACT.Copy, tok, *after, scale=1.0 if scale is None else scale)

    def flip(dst_of, src_of, ins, outs, npart=128, m=128, evacuate=evac, after=()):
        toks = []
        for o in outs:
            b = bank()
            PE.need(pf[b], *after)
            for n, i in enumerate(ins):
                x = nc.tensor.transpose(PS[0:m, b, n * npart:(n + 1) * npart], src_of(o, i), ident[0:npart, 0:npart])
            tok = PE.done(x)
            pf[b] = evacuate(dst_of(o), PS[0:m, b, 0:len(ins) * npart], tok)
            toks.append(pf[b])
        return toks

    c_at = {"o": CONST}

    def cst(*dims):
        n = 1
        for d in dims:
            n *= d
        o = c_at["o"]
        c_at["o"] += n
        assert c_at["o"] <= RING
        return sb(o, *dims)

    ident = cst(128)
    cT, ctmp = cst(8, 2), cst(8, 2)
    cc = MQ.go(cT, D["cT"])
    t_id = MQ.go(ident, D["ident"])
    t = A.act(ctmp, cT, ACT.Tanh, cc, scale=0.5)
    V.stt(ctmp, ctmp, 1.0, cT, ALU.add, ALU.mult, t, cc)
    V.ts1(ctmp, ctmp, 0.5, ALU.mult)
    ones = cst(128)
    V.zero(ones, 1.0)
    small = cst(512)
    stats = cst(80)
    g2i = cst(2, 256)
    MQ.go(g2i, D["g2i"].rearrange("(k p) n -> p k n", p=128))
    cos1, sin1 = cst(4, 32), cst(4, 32)
    cos2, sin2 = cst(4, 16), cst(4, 16)
    for v, name in ((cos1, "cos1"), (sin1, "sin1"), (cos2, "cos2"), (sin2, "sin2")):
        MQ.go(v, D[name].rearrange("(k p) n -> p k n", p=128))
    aff = cst(8, 2, 2)
    ada = cst(24, 2)
    bada = cst(24)
    ng = cst(8)
    vmask = cst(32)
    sc_ = cst(2, 32)
    rest = cst(4, 36)
    ka = cst(4, 256)
    const_toks = [(s, v) for s, v in zip(MQ.sems, MQ.vals) if v]
    for e in (PE, V, A, G):
        e.need(*const_toks)
    barrier()

    def rsqrt(r, x, t1, *after):
        a = A.act(t1, x, ACT.Sqrt, *after)
        a = V.recip(r, t1, a)
        V.tt(t1, r, r, ALU.mult, a)
        V.tt(t1, t1, x, ALU.mult)
        V.ts(t1, t1, -0.5, ALU.mult, 1.5, ALU.add)
        return V.tt(r, r, t1, ALU.mult)

    X = sb(XR, 6, 1024)

    def attention(jobs, P, PT, wide=True, extra=()):
        norm_act, evac_v, lag = (9, 2, 1.5) if wide else (2, 3, 2.5)
        free_P = [None] * len(P)
        free_PT = [None] * len(PT)
        cnt = {"u": 0, "t": 0, "j": 0}
        pending = []
        late = []
        extra = list(extra)

        def order_evac(dst, src, tok, *after):
            cnt["e"] = cnt.get("e", 0) + 1
            if cnt["e"] % evac_v == 0:
                return V.copy(dst, src, tok, *after)
            return A.act(dst, src, ACT.Copy, tok, *after)

        def scores(j, st, q):
            if wide:
                b0 = 2 * (cnt["u"] % 2)
                bs = [b0, b0 + 1]
                ps = PS[:, b0:b0 + 2, :].rearrange("p a b -> p (a b)")
            else:
                b0 = cnt["u"] % 4
                bs = [b0]
                ps = PS[:, b0, :]
            PE.need([pf[b] for b in bs], *j.get("after", ()))
            for c0, nn, l, r in j["scores"](q):
                m = nc.tensor.matmul(ps[:, c0:c0 + nn], l, r, start=True, stop=True)
            tok = PE.done(m)
            slot = cnt["u"] % len(P)
            cnt["u"] += 1
            j["slots"].append(slot)
            rel = softmax(j, q, ps, P[slot], st, tok, free_P[slot])
            for b in bs:
                pf[b] = rel
            while late:
                late.pop(0)()
            for _ in range(2):
                if extra:
                    extra.pop(0)()
            if q == j["nq"] - 1:
                ta = A.last()
                late.append(lambda: normalize(j, st, ta))

        def softmax(j, q, ps, Pq, st, tok, free):
            plain, biased = j["segs"](q)
            m = None
            rel = []
            if plain:
                c0, c1 = plain
                t = V.red(st[:, 0, q:q + 1], ps[:, c0:c1], ALU.min, tok)
                m = st[:, 0, q:q + 1]
                if j.get("sink") is not None:
                    t = V.tt(m, m, j["sink"], ALU.min)
                rel.append(t)
            if biased:
                c0, c1, bias = biased
                src = ps[:, c0:c1]
                if j.get("pre") is not None:
                    cumq, Bk = j["pre"](q)
                    t = V.stt(Pq[:, c0:c1], src, cumq, Bk, ALU.add, ALU.add, tok, free)
                    rel.append(t)
                    src = Pq[:, c0:c1]
                t = V.addmin(Pq[:, c0:c1], src, bias, HIGH if m is None else m, st[:, 1, q:q + 1], tok, free)
                m = st[:, 1, q:q + 1]
                rel.append(t)
            k = 0
            if plain:
                c0, c1 = plain
                ta = A.act(Pq[:, c0:c1], ps[:, c0:c1], ACT.Exp, t, free, bias=m, scale=-1.0,
                           acc=st[:, 2 + k, q:q + 1])
                k += 1
                rel.append(ta)
            if biased:
                c0, c1, _ = biased
                A.act(Pq[:, c0:c1], Pq[:, c0:c1], ACT.Exp, t, bias=m, scale=-1.0, acc=st[:, 2 + k, q:q + 1])
                k += 1
            if j.get("sink") is not None:
                A.act(st[:, 2 + k, q:q + 1], j["sink"], ACT.Exp, t, bias=m, scale=-1.0)
                k += 1
            j["k"] = k
            return rel

        def normalize(j, st, ta):
            nq = j["nq"]
            r = st[:, 2, 0:nq]
            V.need(ta)
            for i in range(1, j["k"]):
                V.tt(r, r, st[:, 2 + i, 0:nq], ALU.add)
            V.recip(r, r)
            if j.get("gate") is not None:
                V.tt(r, r, j["gate"], ALU.mult)
            rv = V.last()
            for q in range(nq):
                plain, biased = j["segs"](q)
                if plain and biased:
                    c0, c1 = biased[0], plain[1]
                else:
                    c0, c1 = (plain or biased)[0:2]
                x = P[j["slots"][q]][:, c0:c1]
                if q % norm_act == norm_act - 1:
                    ta = A.act(x, x, ACT.Copy, rv, scale=st[:, 2, q:q + 1])
                else:
                    tv = V.ts1(x, x, st[:, 2, q:q + 1], ALU.mult)
            j["ready"] = [ta, tv]

        def transposes(j, kt):
            pcol, nk, q0, q1, v = j["keys"][kt]
            b = 4 + cnt["t"] % 2
            slot = cnt["t"] % len(PT)
            pt = PT[slot]
            cnt["t"] += 1
            if "ready" not in j:
                while late:
                    late.pop(0)()
            if j.get("P") is not None:
                while extra:
                    extra.pop(0)()
                j["ready"] = j["ptok"][0]
            PE.need(pf[b], j["ready"])
            for q in range(q0, q1):
                Pq = j["P"][q] if j.get("P") is not None else P[j["slots"][q]]
                m = nc.tensor.transpose(PS[0:nk, b, q * 128:q * 128 + 128], Pq[:, pcol(q):pcol(q) + nk], ident[:, :])
            tok = PE.done(m)
            pf[b] = order_evac(pt[0:nk, q0 * 128:q1 * 128], PS[0:nk, b, q0 * 128:q1 * 128], tok, free_PT[slot])
            return (j, kt, pt, slot, pf[b])

        def values(x):
            j, kt, pt, slot, ready = x
            pcol, nk, q0, q1, v = j["keys"][kt]
            ob, half = j["out"]
            last = kt == len(j["keys"]) - 1
            PE.need(ready)
            if kt == 0 and j["first"]:
                PE.need(pf[ob])
            m = nc.tensor.matmul(PS[half * 64:half * 64 + 64, ob, q0 * 128:q1 * 128], v,
                                 pt[0:nk, q0 * 128:q1 * 128], start=(kt == 0 and j["first"]),
                                 stop=(last and j["last"]))
            tok = PE.done(m)
            free_PT[slot] = tok
            if last and j.get("final"):
                pf[ob] = j["final"](tok)

        steps = []
        end = 0
        for n, j in enumerate(jobs):
            j["slots"] = []
            for q in range(j["nq"]):
                steps.append((end + q, n, 0, q))
            end += j["nq"]
            nk = len(j["keys"])
            after = [x["nq"] for x in jobs[n + 1:] if x["nq"]]
            span = after[0] if after else 1
            for kt in range(nk):
                steps.append((end + lag + span * (kt / nk if j["nq"] else 0.99), n, 1, kt))
        for _, n, stage, i in sorted(steps):
            j = jobs[n]
            if stage == 0:
                if i == 0:
                    st = stats[:, (cnt["j"] % 4) * 20:(cnt["j"] % 4) * 20 + 20].rearrange("p (k q) -> p k q", q=4)
                    cnt["j"] += 1
                scores(j, st, i)
                continue
            pending.append(transposes(j, i))
            if i == len(j["keys"]) - 1:
                for slot in j["slots"]:
                    free_P[slot] = PE.last()
            if len(pending) > 1:
                values(pending.pop(0))
        while pending:
            values(pending.pop(0))

    def grid(base, n, *dims):
        s = 1
        for d in dims:
            s *= d
        return [sb(base + i * s, *dims) for i in range(n)]

    def split_heads(lo, hi):
        def ev(t0, n, ps, tok):
            return [evac(lo[0:64, t0:t0 + n], ps[0:64], tok), evac(hi[64:128, t0:t0 + n], ps[64:128], tok)]
        return ev

    def modulation(l, rowbuf):
        b1 = MQ.go(bada, D["b_adaT"][l])
        b2 = MQ.go(ng, D["norm_gT"][l])
        bt = bank()
        row = rowbuf[0:2, :]
        tr = None
        for n in range(6):
            w, tw = weight()
            b = bank()
            if b == bt:
                b = bank()
            t = group(PS[0:2, b, :], [(ctmp[:, k, :], w[:, k, :]) for k in range(8)], tw, pf[b])
            used(t)
            pf[b] = V.copy(row, PS[0:2, b, :], t, tr)
            PE.need(pf[b], pf[bt])
            for i in range(4):
                c = (n * 4 + i) * 2
                m = nc.tensor.transpose(PS[:, bt, c:c + 2], row[:, i * 128:i * 128 + 128], ident[0:2, 0:2])
            tr = PE.done(m)
        ps = PS[:, bt, 0:48].rearrange("p (a b) -> p a b", a=24)
        pf[bt] = V.tt(ada, ps, bcast(bada, 2, 2), ALU.add, tr, b1)
        V.ts1(aff[:, :, :, 0], ada[:, 8:16, :], 1.0, ALU.add)
        V.tt(aff[:, :, :, 0], aff[:, :, :, 0], bcast(ng, 2, 2), ALU.mult, b2)
        return V.copy(aff[:, :, :, 1], ada[:, 0:8, :])

    def gates(dst, nv, t_mod):
        for v in range(nv):
            for h in range(2):
                b = bank()
                PE.need(pf[b], t_mod)
                for k in range(4):
                    m = nc.tensor.matmul(PS[:, b, k * 128:k * 128 + 128],
                                         ada[:, 16 + h * 4 + k, v:v + 1].to_broadcast([128, 128]), ident[:, :],
                                         start=True, stop=True)
                pf[b] = t = evac(dst[v][:, h * 512:h * 512 + 512], PS[:, b, :], PE.done(m))
        return t

    def normed(xn, junk, tx):
        for t in range(6):
            a = A.act(junk, X[:, t, :], ACT.Square, tx, acc=small[:, t:t + 1])
        V.ts(small[:, 0:6], small[:, 0:6], 1.0 / 1024, ALU.mult, EPS, ALU.add, a)
        rsqrt(small[:, 8:14], small[:, 0:6], small[:, 16:22], V.last())
        for t in range(6):
            tn = V.ts1(xn[:, t, :], X[:, t, :], small[:, 8 + t:9 + t], ALU.mult)
        return tn

    def modulated(hT, xn, tn, t_mod):
        toks = []
        for k in range(8):
            for v, ts_ in ((0, range(4)), (1, range(4, 6))):
                b = bank()
                PE.need(pf[b], tn, t_mod)
                for n, t in enumerate(ts_):
                    m = nc.tensor.transpose(PS[:, b, n * 128:n * 128 + 128], xn[:, t, k * 128:k * 128 + 128],
                                            ident[:, :])
                tok = PE.done(m)
                n = len(ts_) * 128
                rot["e"] ^= 1
                if rot["e"]:
                    pf[b] = V.ts(hT[:, k, v * 512:v * 512 + n], PS[:, b, 0:n], aff[:, k, v, 0:1], ALU.mult,
                                 aff[:, k, v, 1:2], ALU.add, tok)
                else:
                    pf[b] = A.act(hT[:, k, v * 512:v * 512 + n], PS[:, b, 0:n], ACT.Identity, tok, t_mod,
                                  scale=aff[:, k, v, 0:1], bias=aff[:, k, v, 1:2])
                toks.append(pf[b])
        return [V.last(), A.last()]

    def project(w, tw, kt, c0, n, hT, tiles, dst_of, evacuate=evac, *after):
        for t in tiles:
            b = bank()
            tok = group(PS[:, b, 0:n], [(hT[:, k, t * 128:t * 128 + 128], w[:, k, c0:c0 + n]) for k in range(kt)],
                        pf[b], tw, *after)
            pf[b] = evacuate(dst_of(t), PS[:, b, 0:n], tok)
        return tok

    def project_T(w, tw, kt, c0, m, hT, spans, evacuate, *after):
        for t0, n in spans:
            b = bank()
            tok = group(PS[0:m, b, 0:n], [(w[:, k, c0:c0 + m], hT[:, k, t0:t0 + n]) for k in range(kt)],
                        pf[b], tw, *after)
            pf[b] = evacuate(t0, n, PS[0:m, b, 0:n], tok)
        return tok

    def silu2_T(dst, tmp):
        def ev(t0, n, ps, tok):
            a = A.act(tmp[:, 0:n], ps, ACT.Tanh, tok, V.last(), scale=0.5)
            return V.stt(dst[:, t0:t0 + n], tmp[:, 0:n], 1.0, ps, ALU.add, ALU.mult, a)
        return ev

    def head_norm(Q, tiles, nh, g, tg, tmp, qscale_heads, *after):
        ss, rr, t1 = small[:, 0:6 * nh], small[:, 128:128 + 6 * nh], small[:, 256:256 + 6 * nh]
        V.need(*after)
        for t in tiles:
            q = Q(t)
            V.tt(tmp[:, 0:nh * 64], q, q, ALU.mult)
            V.red(ss[:, t * nh:t * nh + nh], tmp[:, 0:nh * 64].rearrange("p (h d) -> p h d", d=64), ALU.add)
        a, b = tiles[0] * nh, (tiles[-1] + 1) * nh
        V.ts(ss[:, a:b], ss[:, a:b], 1.0 / 64, ALU.mult, EPS, ALU.add)
        rsqrt(rr[:, a:b], ss[:, a:b], t1[:, a:b], V.last())
        if qscale_heads:
            r3 = rr[:, a:b].rearrange("p (t h) -> p t h", h=nh)[:, :, 0:qscale_heads]
            V.ts1(r3, r3, -0.125, ALU.mult)
        for t in tiles:
            q = Q(t).rearrange("p (h d) -> p h d", d=64)
            V.tt(q, q, bcast(rr[:, t * nh:t * nh + nh], 2, 64), ALU.mult)
            V.tt(Q(t), Q(t), g, ALU.mult, tg)
        return V.last()

    def rope_pairs(Q, tiles, nh, tmp):
        for t in tiles:
            q = Q(t).rearrange("p (h d two) -> p h d two", d=32, two=2)
            x0, x1 = q[:, :, :, 0], q[:, :, :, 1]
            c, s = bcast(cos1[:, t, :], 1, nh), bcast(sin1[:, t, :], 1, nh)
            u = [tmp[:, i * nh * 32:(i + 1) * nh * 32].rearrange("p (h d) -> p h d", d=32) for i in range(4)]
            V.tt(u[0], x0, c, ALU.mult)
            V.tt(u[1], x1, s, ALU.mult)
            V.tt(u[2], x0, s, ALU.mult)
            V.tt(u[3], x1, c, ALU.mult)
            V.tt(x0, u[0], u[1], ALU.subtract)
            V.tt(x1, u[2], u[3], ALU.add)
        return V.last()

    def swap(dst, src, *after):
        return [MQ.go(dst[0:64], src[64:128], *after), MQ.go(dst[64:128], src[0:64], *after)]

    def out_proj(yT, nt, GB, t_ready, tmp):
        for n in range(2):
            w, tw = weight()
            for t in range(nt):
                b = bank()
                tok = group(PS[:, b, :], [(yT[:, k, t * 128:t * 128 + 128], w[:, k, :]) for k in range(8)],
                            pf[b], tw, *t_ready)
                x = X[:, t, n * 512:n * 512 + 512]
                u = tmp[t % 2]
                pf[b] = V.tt(u, PS[:, b, :], GB[0 if t < 4 else 1][:, n * 512:n * 512 + 512], ALU.mult, tok,
                             G.last() if G.n else None)
                G.tt(x, x, u, ALU.add, pf[b])
            used(tok)

    x_d, ctx_d = D["x"], D["ctx"]

    def load_x(*after):
        return [MQ.go(X[:, 0:4, :], x_d.rearrange("(t p) d -> p t d", p=128), *after),
                MQ.go(X[:, 4:6, :], ctx_d.rearrange("(t p) d -> p t d", p=128), *after)]

    def head_transposes(QK, qT, ntile, blocks, after):
        for j in blocks:
            for c0, t0, nt in ((0, 0, ntile), (512, 4, 2)):
                if nt:
                    b = bank()
                    PE.need(pf[b], *after)
                    for t in range(nt):
                        m = nc.tensor.transpose(PS[:, b, t * 128:t * 128 + 128],
                                                QK[:, t0 + t, j * 128:j * 128 + 128], ident[:, :])
                    pf[b] = evac(qT(j)[:, c0:c0 + nt * 128], PS[:, b, 0:nt * 128], PE.done(m))

    def kv_pads(kp, K):
        G.zero(kp[64:128, 0, :], 0.0)
        G.zero(kp[0:64, 3, :], 0.0)
        G.zero(kp[0:64, 1, :], 0.0)
        tz = G.zero(kp[64:128, 2, :], 0.0)
        for c0, t0, nt in ((0, 0, 4), (512, 4, 2)):
            b = bank()
            PE.need(pf[b])
            for t in range(nt):
                m = nc.tensor.transpose(PS[:, b, t * 128:t * 128 + 128], K(t0 + t), ident[:, :])
            tok = PE.done(m)
            n = nt * 128
            pf[b] = [evac(kp[0:64, 0, c0:c0 + n], PS[0:64, b, 0:n], tok),
                     evac(kp[64:128, 3, c0:c0 + n], PS[64:128, b, 0:n], tok)]
        t = [V.last(), A.last()]
        return [tz, MQ.go(kp[64:128, 1, :], kp[0:64, 0, :], *t), MQ.go(kp[0:64, 2, :], kp[64:128, 3, :], *t)]

    tx = load_x()
    tn = normed(sb(BIG + 12288, 6, 1024), sb(BIG + 6144, 1024), tx)
    t_mod = modulation(0, sb(BIG + 21504, 512))
    hT = sb(BIG, 8, 768)
    yT = sb(BIG + 6144, 8, 768)
    UC = sb(BIG + 12288, 6, 1536)
    QK = sb(BIG + 21504, 6, 640)
    VV = sb(BIG + 25344, 6, 128)
    g10 = sb(BIG + 26112, 640)
    tmp10 = sb(BIG + 26752, 1280)
    uct = grid(BIG + 28032, 2, 768)
    gtmp = sb(BIG + 29568, 512)
    cw = sb(BIG + 30080, 12, 4)
    tg = MQ.go(g10, bcast(D["g10_0"], 0, 128))
    tcw = MQ.go(cw, D["convT"])
    modulated(hT, sb(BIG + 12288, 6, 1024), tn, t_mod)
    barrier()
    w, tw = weight()
    used(project(w, tw, 8, 0, 512, hT, range(6), lambda t: QK[:, t, 0:512]))
    w, tw = weight()

    def ev_kv0(t, ps, tok):
        V.copy(QK[:, t, 512:640], ps[:, 0:128], tok)
        return V.copy(VV[:, t, :], ps[:, 128:256])
    used(project(w, tw, 8, 0, 256, hT, range(6), lambda t: t, ev_kv0))
    head_norm(lambda t: QK[:, t, :], range(6), 10, g10, tg, tmp10, 8, A.last(), V.last())
    t_q = rope_pairs(lambda t: QK[:, t, :], range(4), 10, tmp10)
    w, tw = weight()
    for j in range(4):
        tok = project_T(w, tw, 8, j * 128, 128, hT, [(0, 512), (512, 256)], silu2_T(yT[:, j, :], gtmp))
    used(tok)

    V.need(tcw)
    A.need(tcw)
    free_u = [None, None]

    def to_tokens(ct, u, after):
        for t0, nt in ((0, 4), (4, 2)):
            b = bank()
            PE.need(pf[b], after)
            for t in range(nt):
                m = nc.tensor.transpose(PS[:, b, t * 128:t * 128 + 128], u[:, (t0 + t) * 128:(t0 + t + 1) * 128],
                                        ident[:, :])
            tok = PE.done(m)
            pf[b] = evac(UC[:, t0:t0 + nt, ct * 128:ct * 128 + 128],
                         PS[:, b, 0:nt * 128].rearrange("p (t c) -> p t c", t=nt), tok)
        free_u[ct % 2] = tok
    conv_prev = None
    for n in range(3):
        w, tw = weight()
        for s in range(4):
            ct = n * 4 + s
            u = uct[ct % 2]
            for t0, nn in ((0, 512), (512, 256)):
                b = bank()
                tok = group(PS[:, b, 0:nn], [(w[:, k, s * 128:s * 128 + 128], hT[:, k, t0:t0 + nn]) for k in range(8)],
                            pf[b], tw)
                a = A.act(u[:, t0:t0 + nn], PS[:, b, 0:nn], ACT.Identity, tok, free_u[ct % 2],
                          scale=cw[:, ct, 1:2], bias=cw[:, ct, 3:4])
                V.stt(u[:, t0 + 1:t0 + nn], PS[:, b, 0:nn - 1], cw[:, ct, 0:1], u[:, t0 + 1:t0 + nn],
                      ALU.mult, ALU.add, a)
                pf[b] = V.stt(u[:, t0:t0 + nn - 1], PS[:, b, 1:nn], cw[:, ct, 2:3], u[:, t0:t0 + nn - 1],
                              ALU.mult, ALU.add)
            if s == 3:
                used(tok)
            if conv_prev:
                to_tokens(*conv_prev)
            conv_prev = (ct, u, V.last())
    w, tw = weight()
    for j in range(4):
        tok = project_T(w, tw, 8, j * 128, 128, hT, [(0, 512), (512, 256)], silu2_T(yT[:, 4 + j, :], gtmp))
        if j == 0:
            to_tokens(*conv_prev)
    used(tok)
    f = barrier()
    qT = sb(BIG, 4, 768)
    kp = sb(BIG + 3072, 4, 768)
    t_s = kv_pads(kp, lambda t: QK[:, t, 512:640])
    head_transposes(QK, lambda j: qT[:, j, :], 4, (0, 1, 2, 3), [])
    V.need(PE.last())
    A.need(PE.last())
    P, PT = grid(XR, 8, 768) + grid(BIG + 21504, 4, 768), grid(BIG + 28032, 3, 512)

    def yfinal(pair, c0, n, ob):
        def final(tok):
            return V.stt(yT[:, pair, c0:c0 + n], PS[:, ob, 0:n], 0.5, yT[:, pair, c0:c0 + n], ALU.mult, ALU.mult, tok)
        return final

    jobs = []
    for nq, q00, kts in ((4, 0, range(6)), (2, 4, (4, 5))):
        for pair in range(4):
            for half in range(2):
                h = pair * 2 + half
                g = h // 4
                ksrc = kp[:, g * 2 + half, :]

                def sc(q, pair=pair, ksrc=ksrc, nq=nq, q00=q00):
                    l = qT[:, pair, (q00 + q) * 128:(q00 + q) * 128 + 128]
                    a = [(0, 512, l, ksrc[:, 0:512])] if nq == 4 else []
                    return a + [(512, 256, l, ksrc[:, 512:768])]
                ob = 6 + pair % 2
                jobs.append(dict(nq=nq, scores=sc, segs=lambda q, nq=nq: ((0 if nq == 4 else 512, 768), None),
                                 out=(ob, half), first=True, last=True, after=[V.last(), A.last()] + t_s,
                                 keys=[(lambda q, c=kt * 128: c, 128, 0, nq, VV[:, kt, g * 64:g * 64 + 64])
                                       for kt in kts],
                                 final=yfinal(pair, q00 * 128, nq * 128, ob) if half else None))
    attention(jobs, P, PT)
    f = barrier()

    TR, TI = sb(BIG, 4, 512), sb(BIG + 2048, 4, 512)
    tr, ti = sb(BIG + 4096, 2, 512), sb(BIG + 5120, 2, 512)
    ZR, ZI = sb(BIG + 21504, 4, 512), sb(BIG + 23552, 4, 512)
    zr, zi = sb(BIG + 25600, 2, 512), sb(BIG + 26624, 2, 512)
    tmpa, tmpb = sb(BIG + 27648, 512), sb(BIG + 28160, 512)
    w3 = sb(XR, 2048)
    h2 = sb(XR + 2048, 768)
    zt = sb(XR + 2816, 768)
    hw = sb(XR + 3584, 192)
    dec = grid(XR + 3776, 2, 512)
    dsk = sb(XR + 4800, 512)
    sc1, sc2 = sb(XR + 5312, 512), sb(BIG + 28672, 512)
    t1 = MQ.go(w3[0:64], D["hy_w3"], *f)
    V.zero(w3[64:128], 0.0)
    PE.need(V.zero(h2[64:128], 0.0))
    t2 = MQ.go(zt[0:33], D["hyz"], *f)
    t3 = MQ.go(hw[0:33, 0:64], D["hy_w1"], *f)
    t4 = MQ.go(hw[0:64, 64:128], D["hy_w2"], *f)
    t5 = MQ.go(hw[0:64, 128:131], D["hyb"], *f)
    for e in (PE, V, A):
        e.need(t1, t2, t3, t4, t5)

    def wrapped_sin(dst, src, bcol, tok, n):
        x, k = tmpa[0:64, 0:n], tmpb[0:64, 0:n]
        rel = V.ts(x, src, bcol, ALU.add, hw[0:64, 128:129], ALU.mult, tok)
        V.ts(k, x, 1.0 / (2 * math.pi), ALU.mult, 12582912.0, ALU.add)
        V.ts1(k, k, 12582912.0, ALU.subtract)
        V.stt(x, k, -6.28125, x, ALU.mult, ALU.add)
        V.stt(x, k, -(2 * math.pi - 6.28125), x, ALU.mult, ALU.add)
        V.ts(x, x, 3.1415925, ALU.min, -3.1415925, ALU.max)
        return rel, A.act(dst, x, ACT.Sin, V.last())

    for a0, n in ((0, 512), (512, 256)):
        b = bank()
        tok = group(PS[0:64, b, 0:n], [(hw[0:33, 0:64], zt[0:33, a0:a0 + n])], pf[b])
        pf[b], t = wrapped_sin(h2[0:64, a0:a0 + n], PS[0:64, b, 0:n], hw[0:64, 129:130], tok, n)
        b = bank()
        tok = group(PS[0:64, b, 0:n], [(hw[0:64, 64:128], h2[0:64, a0:a0 + n])], pf[b], t)
        pf[b], t = wrapped_sin(h2[0:64, a0:a0 + n], PS[0:64, b, 0:n], hw[0:64, 130:131], tok, n)
        V.need(t)

    def spectrum(w, tw, o, nt, st, s_, d_, Tr, Ti, scl, a0, decay):
        PE.need(A.last())
        td = [MQ.go(dec[t], decay[t * 128:t * 128 + 128, :], V.last()) for t in range(2)]
        for t in range(nt):
            pair = []
            for side in range(2):
                b = bank()
                c = (o * 2 + side) * 512
                tok = group(PS[:, b, :], [(h2[:, a0 + t * 128:a0 + t * 128 + 128], w3[:, c:c + 512])], pf[b])
                pair.append((b, tok))
            for side in range(2):
                b, tok = pair[side]
                pf[b] = V.tt((tmpa, tmpb)[side], PS[:, b, :], dec[t % 2], ALU.mult, tok, td[t])
            if t + 2 < nt:
                td.append(MQ.go(dec[t % 2], decay[(t + 2) * 128:(t + 3) * 128, :], V.last()))
            if t == 0:
                V.zero(tmpb[0:1, :], 0.0)
            V.tt(s_[:, t, :], tmpa, tmpb, ALU.add)
            V.tt(d_[:, t, :], tmpa, tmpb, ALU.subtract)
        ready = V.last()

        def transform():
            PE.need(ready)
            bn = bank()
            sums = []
            for k in range(nt):
                for src, dst, half in ((s_, Tr, 0), (d_, Ti, 512)):
                    b = bank()
                    if b == bn:
                        b = bank()
                    tok = group(PS[:, b, :], [(w[:, t, half + k * 128 * st:half + (k + 1) * 128 * st:st], src[:, t, :])
                                              for t in range(nt)], pf[b], tw)
                    pf[b] = A.act(dst[:, k, :], PS[:, b, :], ACT.Copy, tok)
                u = (tmpa, tmpb)[k % 2]
                V.tt(u, s_[:, k, :], s_[:, k, :], ALU.mult, sums[k - 2] if k > 1 else None)
                V.tt(sc4, d_[:, k, :], d_[:, k, :], ALU.mult)
                x = V.tt(u, u, sc4, ALU.add)
                PE.need(x, pf[bn] if k == 0 else None)
                sums.append(PE.done(nc.tensor.matmul(PS[:, bn, :], ones[:, :], u, start=(k == 0), stop=(k == nt - 1))))
            b = bank()
            if b == bn:
                b = bank()
            tok = group(PS[0:1, b, :], [(w[:, t, 512:513], s_[:, t, :]) for t in range(nt)], pf[b])
            V.ts(tmpa, PS[:, bn, :], 0.5, ALU.mult, EPS, ALU.add, sums[-1])
            pf[bn] = V.last()
            rsqrt(scl, tmpa, tmpb, V.last())
            if nt == 2:
                V.ts1(scl, scl, 2.0, ALU.mult)
            pf[b] = V.copy(Ti[0:1, 0, :], PS[0:1, b, :], tok, A.last())
            return tok
        return transform

    sc3, sc4 = sb(BIG + 29184, 512), sb(BIG + 29696, 512)

    def forward(w, tw, nt, st, t0, Zr, Zi, Tr, Ti):
        toks = []
        A.need(V.last(), G.last(), PE.last())
        V.need(A.last())
        for k in range(nt):
            ev = []
            for dst, half in ((Zr, 0), (Zi, 512)):
                b = bank()
                tok = group(PS[:, b, :], [(w[:, t, half + k * 128 * st:half + (k + 1) * 128 * st:st],
                                           UC[:, t0 + t, 0:512]) for t in range(nt)], pf[b], tw)
                pf[b] = A.act(dst[:, k, :], PS[:, b, :], ACT.Copy, tok)
                ev.append(pf[b])
            if k == 0:
                V.tt(small[0:1, 0:512], Zr[0:1, 0, :], Tr[0:1, 0, :], ALU.mult, *ev)
                V.tt(sc3[0:1, :], Zi[0:1, 0, :], Ti[0:1, 0, :], ALU.mult)
            g = G.tt(tmpb, Zr[:, k, :], Ti[:, k, :], ALU.mult, V.last(), *ev)
            V.tt(tmpa, Zr[:, k, :], Tr[:, k, :], ALU.mult, *ev)
            V.tt(sc4, Zi[:, k, :], Tr[:, k, :], ALU.mult)
            V.tt(Zi[:, k, :], Zi[:, k, :], Ti[:, k, :], ALU.mult)
            V.tt(Zr[:, k, :], tmpa, Zi[:, k, :], ALU.subtract, g)
            V.tt(Zi[:, k, :], tmpb, sc4, ALU.add)
            if k == 0:
                V.copy(Zr[0:1, 0, :], small[0:1, 0:512])
                V.copy(Zi[0:1, 0, :], sc3[0:1, :])
            toks.append(V.last())
        return tok, toks

    def inverse(lhs, nt, t0, o, Zr, Zi, scl, tw, tz):
        bs = [bank() for _ in range(nt)]
        PE.need(tw, *[pf[b] for b in bs])
        for k in range(nt):
            PE.need(tz[k])
            for t in range(nt):
                nc.tensor.matmul(PS[:, bs[t], :], lhs(0, k, t), Zr[:, k, :], start=(k == 0), stop=False)
                m = nc.tensor.matmul(PS[:, bs[t], :], lhs(1, k, t), Zi[:, k, :], start=False, stop=(k == nt - 1))
        tok = PE.done(m)
        for t in range(nt):
            b = bs[t]
            z = UC[:, t0 + t, 0:512]
            ta_, tb_ = ((tmpa, tmpb), (sc3, sc4))[t % 2]
            g = G.tt(tb_, z, dsk, ALU.mult, tok, V.last() if t < 2 else zt_[t - 2])
            if t == 0:
                zt_ = []
            pf[b] = V.tt(ta_, PS[:, b, :], scl, ALU.mult, tok)
            V.tt(ta_, ta_, tb_, ALU.add, g)
            V.tt(z, ta_, UC[:, t0 + t, (o + 1) * 512:(o + 2) * 512], ALU.mult)
            zt_.append(V.last())
        return tok

    for o in range(2):
        f = barrier()
        tds = MQ.go(dsk, bcast(D["hy_skip"][o], 0, 128), *f)
        G.need(tds)
        w, tw = weight()
        parts = [spectrum(w, tw, o, 4, 1, ZR, ZI, TR, TI, sc1, 0, D["decay1"]),
                 spectrum(w, tw, o, 2, 2, zr, zi, tr, ti, sc2, 512, D["decay2"])]
        for transform in parts:
            transform()
        t, tz = forward(w, tw, 4, 1, 0, ZR, ZI, TR, TI)
        t, tz2 = forward(w, tw, 2, 2, 4, zr, zi, tr, ti)
        used(t)
        w, tw = weight()
        inverse(lambda part, k, t, w=w: w[:, part * 4 + k, t * 128:t * 128 + 128], 4, 0, o, ZR, ZI, sc1, tw, tz)

        def lhs2(part, k, t, w=w):
            if part == 0:
                return w[:, k, t * 256:t * 256 + 256:2]
            if k == 0:
                return g2i[:, 0, t * 128:t * 128 + 128]
            return w[:, 4 + k, t * 256:t * 256 + 256:2]
        used(inverse(lhs2, 2, 4, o, zr, zi, sc2, tw, tz2))
    f = barrier()
    tx = load_x(*f)
    for j in range(4):
        for c0, nt, t0 in ((0, 4, 0), (512, 2, 4)):
            b = bank()
            PE.need(pf[b])
            for t in range(nt):
                m = nc.tensor.transpose(PS[:, b, t * 128:t * 128 + 128], UC[:, t0 + t, j * 128:j * 128 + 128],
                                        ident[:, :])
            y = yT[:, 4 + j, c0:c0 + nt * 128]
            pf[b] = V.stt(y, PS[:, b, 0:nt * 128], 0.5, y, ALU.mult, ALU.mult, PE.done(m))
    GB = [sb(BIG, 1024), sb(BIG + 1024, 1024)]
    tmp = grid(BIG + 2048, 2, 512)
    gates(GB, 2, None)
    V.need(*tx)
    G.need(*tx)
    out_proj(yT, 6, GB, [V.last(), A.last()], tmp)
    f = barrier()

    tn = normed(sb(BIG + 14848, 6, 1024), sb(BIG + 12288, 1024), None)
    t_mod = modulation(1, sb(BIG + 21504, 512))
    hT = sb(BIG, 8, 768)
    yT = sb(BIG + 6144, 8, 512)
    QKw = sb(BIG + 10240, 6, 640)
    Vw = sb(BIG + 14080, 6, 128)
    QKn = sb(BIG + 14848, 6, 1024)
    Vn = sb(BIG + 20992, 6, 512)
    kp = sb(BIG + 24064, 4, 768)
    tmp16 = sb(BIG + 27648, 1280)
    g10 = sb(BIG + 28928, 640)
    g16 = sb(BIG + 29568, 1024)
    gtmp = sb(BIG + 24064, 512)
    tg = [MQ.go(g10, bcast(D["g10_1"], 0, 128), *f), MQ.go(g16, bcast(D["g16"], 0, 128), *f)]
    modulated(hT, sb(BIG + 14848, 6, 1024), tn, t_mod)
    f = barrier()
    w, tw = weight()
    used(project(w, tw, 8, 0, 512, hT, range(4), lambda t: QKw[:, t, 0:512]))
    w, tw = weight()

    def ev_kv1(t, ps, tok):
        V.copy(QKw[:, t, 512:640], ps[:, 0:128], tok)
        return V.copy(Vw[:, t, :], ps[:, 128:256])
    used(project(w, tw, 8, 0, 256, hT, range(6), lambda t: t, ev_kv1))
    V.need(A.last())
    head_norm(lambda t: QKw[:, t, :], range(4), 10, g10, tg, tmp16, 8)
    head_norm(lambda t: QKw[:, t, 512:640], range(4, 6), 2, g10[:, 512:640], tg, tmp16, 0)
    rope_pairs(lambda t: QKw[:, t, :], range(4), 10, tmp16)
    w, tw = weight()
    used(project(w, tw, 8, 0, 512, hT, range(4), lambda t: QKn[:, t, 0:512]))
    w, tw = weight()
    used(project(w, tw, 8, 0, 512, hT, range(6), lambda t: QKn[:, t, 512:1024]))
    V.need(A.last())
    head_norm(lambda t: QKn[:, t, :], range(4), 16, g16, tg, tmp16, 8)
    head_norm(lambda t: QKn[:, t, 512:1024], range(4, 6), 8, g16[:, 512:1024], tg, tmp16, 0)
    t_n = V.last()
    w, tw = weight()
    used(project(w, tw, 8, 0, 512, hT, range(6), lambda t: Vn[:, t, :]))
    for n in range(2):
        w, tw = weight()
        for j in range(4):
            tok = project_T(w, tw, 8, j * 128, 128, hT, [(0, 512)], silu2_T(yT[:, 4 * n + j, :], gtmp))
        used(tok)
    f = barrier()
    qTn = sb(BIG, 8, 512)
    qTw = sb(BIG + 4096, 4, 512)
    kTn = grid(BIG + 12240, 2, 768) + grid(XR + 4096, 2, 768)
    t_s = kv_pads(kp, lambda t: QKw[:, t, 512:640])
    q4 = qTn.rearrange("p (j two) n -> p j two n", two=2)
    G.zero(q4[64:128, :, 0, :], 0.0)
    tz = G.zero(q4[0:64, :, 1, :], 0.0)
    for Q, j0, dst in ((QKw, 0, qTw), (QKn, 0, None)):
        for j in range(4):
            b = bank()
            PE.need(pf[b])
            for t in range(4):
                m = nc.tensor.transpose(PS[:, b, t * 128:t * 128 + 128], Q[:, t, j * 128:j * 128 + 128], ident[:, :])
            tok = PE.done(m)
            if dst is None:
                pf[b] = split_heads(qTn[:, 2 * j, :], qTn[:, 2 * j + 1, :])(0, 512, PS[:, b, :], tok)
            else:
                pf[b] = evac(dst[:, j, :], PS[:, b, :], tok)
    V.need(PE.last(), *t_s)
    A.need(PE.last(), *t_s)
    head_transposes(QKn, lambda j: kTn[j - 4], 4, (4, 5, 6, 7), [])
    P, PT = grid(BIG + 14848, 8, 768) + grid(BIG + 29056, 2, 768), grid(BIG + 10240, 3, 512)
    wm = sb(BIG + 11776, 384)
    sink = sb(BIG + 12160, 8)
    cm = sb(BIG + 12168, 64)
    rp = grid(BIG + 27136, 2, 15, 64)
    f = barrier()
    t_c = [MQ.go(wm, D["wmask"], *f), MQ.go(sink, bcast(D["win_sink"], 0, 128), *f), MQ.go(cm, D["cmask"], *f)]
    V.need(*t_c)
    A.need(*t_c)
    G.need(*t_c)
    A.need(V.ts1(sink, sink, -1.0, ALU.mult))
    rtok = {}

    def load_rpb(h):
        t = MQ.go(rp[h % 2], D["rpx"][h], V.last())
        rtok[h] = G.tt(rp[h % 2], bcast(cm, 1, 15), rp[h % 2], ALU.subtract, t)
    jobs = []
    for pair in range(4):
        for half in range(2):
            h = pair * 2 + half
            g = h // 4
            ksrc = kp[:, g * 2 + half, :]

            def span(q):
                return max(0, q - 1), min(4, q + 2)

            def sc(q, pair=pair, ksrc=ksrc):
                l = qTw[:, pair, q * 128:q * 128 + 128]
                a, b = span(q)
                return [(512 - (b - a) * 128, (b - a) * 128, l, ksrc[:, a * 128:b * 128]),
                        (512, 256, l, ksrc[:, 512:768])]

            def segs(q):
                a, b = span(q)
                m0 = (a - q + 1) * 128
                return (512, 768), (512 - (b - a) * 128, 512, wm[:, m0:m0 + (b - a) * 128])
            ob = 6 + pair % 2
            keys = [(lambda q, c=kt * 128: c, 128, 0, 4, Vw[:, kt, g * 64:g * 64 + 64]) for kt in (4, 5)]
            keys += [(lambda q, kt=kt: 512 + (kt - min(4, q + 2)) * 128, 128, max(0, kt - 1), min(4, kt + 2),
                      Vw[:, kt, g * 64:g * 64 + 64]) for kt in range(4)]
            jobs.append(dict(nq=4, scores=sc, segs=segs, out=(ob, half), first=True, last=True,
                             after=t_s, sink=sink[:, h:h + 1], keys=keys, final=yfinal(pair, 0, 512, ob) if half else None))
    for pair in range(4):
        for half in range(2):
            h = pair * 2 + half

            def sc(q, pair=pair, h=h):
                if q == 0:
                    if h == 0:
                        load_rpb(0)
                    if h < 7:
                        load_rpb(h + 1)
                l = qTn[:, h, q * 128:q * 128 + 128]
                return [(0, 512, l, kTn[pair][:, 0:512]), (512, 256, l, kTn[pair][:, 512:768])]

            def segs(q, h=h):
                V.need(rtok[h])
                s = 7 - 2 * q
                return (512, 768), (0, 512, rp[h % 2][:, s:s + 8, :].rearrange("p a b -> p (a b)"))
            ob = 6 + pair % 2
            jobs.append(dict(nq=4, scores=sc, segs=segs, out=(ob, half), first=True, last=True, after=[tz],
                             keys=[(lambda q, c=kt * 128: c, 128, 0, 4, Vn[:, kt, h * 64:h * 64 + 64])
                                   for kt in range(6)],
                             final=yfinal(4 + pair, 0, 512, ob) if half else None))
    attention(jobs, P, PT)
    f = barrier()
    T5B = BIG + 10240
    tab = sb(T5B, 8)
    oh = sb(T5B + 8, 640)
    ut = sb(T5B + 704, 640)
    V.zero(tab[0:64, :], FAR)
    t4 = MQ.go(tab[0:32, :], D["t5"], V.last())
    t5_ = MQ.go(oh[0:33, :], D["onehot"], *f)
    t4 = V.ts1(tab[0:32, :], tab[0:32, :], -1.0, ALU.mult, t4)
    scr = nc.dram_tensor("t5_rows", [8, 128 * 640], F32)
    for c0, n in ((0, 512), (512, 128)):
        b = bank()
        tok = group(PS[0:8, b, 0:n], [(tab[0:33, :], oh[0:33, c0:c0 + n])], pf[b], t4, t5_)
        pf[b] = V.copy(ut[0:8, c0:c0 + n], PS[0:8, b, 0:n], tok)
    tbs = [MQ.go(bass.AP(scr, 0, [[81920, 8], [640, 128], [1, 640]]), bcast(ut[0:8, :], 1, 128), V.last())]

    GB = [sb(BIG, 1024)]
    tmp = grid(BIG + 2048, 2, 512)
    gates(GB, 1, None)
    out_proj(yT, 4, GB, [V.last(), A.last()], tmp)
    f = barrier()

    first.close()
    second = ExitStack()
    regions[1:] = [(RING, second.enter_context(nc.sbuf_tensor("S2", [128, HL - RING], F32)))]
    HLt = second.enter_context(nc.sbuf_tensor("HL", [128, 4, 2048], F32R))
    xTt = second.enter_context(nc.sbuf_tensor("XT", [128, 2, 8, 512], F32R))
    xT = (xTt[:, 0], xTt[:, 1])
    T5 = sb(T5_AT, 8, 512)
    WQ.w.need(*f)

    plan2 = []
    for l in range(2):
        w2 = D["w_in_2"][l]
        parts = [[(0, 256)], [(256, 512)], [(1280, 1304), (1816, 1848), (2616, 2620)],
                 [(512, 640), (640, 768)], [(768, 896), (1024, 1152)], [(896, 1024), (1152, 1280)]]
        for i, p in enumerate(parts):
            plan2.append(([rows(w2, 0, 8, a, b) for a, b in p], (8, sum(b - a for a, b in p)), True))
            if i > 3:
                plan2.append((("cmpw", l, i - 4), (16, 128), False))
        for a, b in [(1304, 1560), (1560, 1816)]:
            plan2.append((rows(w2, 0, 8, a, b), (8, b - a), True))
        plan2.append((rows(D["mla_w_uq_2"][l], 0, 3, 0, 384), (3, 384), False))
        plan2.append((rows(D["mla_w_ukv_2"][l], 0, 1, 0, 512), (1, 512), False))
        for a, b in [(1848, 2104), (2104, 2360), (2360, 2616)]:
            plan2.append((rows(w2, 0, 8, a, b), (8, b - a), True))
        for br, name, kt in ((0, "w_br_nsa_2", 4), (1, "w_br_mla_2", 2), (2, "w_br_fox_2", 2)):
            for n in range(4):
                plan2.append((rows(D[name][l], 0, kt, n * 256, n * 256 + 256), (kt, 256), False))
                c = br * 1024 + n * 256
                plan2.append((rows(D["w_gate_2"][l], 0, 8, c, c + 256), (8, 256), True))
        for c in (0, 256):
            plan2.append((rows(D["xa_w_kv_2"][l], 0, 8, c, c + 256), (8, 256), False))
        plan2.append((rows(D["xa_w_q_2"][l], 0, 8, 0, 256), (8, 256), True))
        plan2.append((rows(D["xa_w_o_2"][l], 0, 2, 0, 1024), (2, 1024), False))
        for half in range(2):
            for n in range(8):
                c = half * 2048 + n * 256
                plan2.append((rows(D["mlp_w_up_2"][l], 0, 8, c, c + 256), (8, 256), True))
            for r in range(2):
                for n in range(4):
                    plan2.append((rows(D["mlp_w_down_2"][l], half * 2048 + r * 1024, 8, n * 256, n * 256 + 256),
                                  (8, 256), True))
    raw_tok, views, out_queue = {}, {}, []
    hl_free = [None, None]
    st2 = {"next": 0, "loaded": 0, "prep": 0, "split": 0}

    freed = {}

    def load2():
        i = st2["loaded"]
        if i >= len(plan2) or (i > 1 and i - 2 not in freed):
            return
        st2["loaded"] += 1
        after = freed.get(i - 2, ())
        src, dims, _ = plan2[i]
        v = sb(RAW + (i % 2) * 2048, *dims)
        if isinstance(src, tuple):
            _, l, kv = src
            w = D["cmp_w1_2"][l, kv].rearrange("(a l d) n -> a d l n", a=2, d=64)
            t = [WQ.go(v[0:64], w[0], *after), WQ.go(v[64:128], w[1], *after)]
        elif isinstance(src, list):
            t, c = [], 0
            for x in src:
                n = x.shape[2]
                t.append(WQ.go(v[:, :, c:c + n], x, *after))
                c += n
        else:
            t = WQ.go(v, src, *after)
        raw_tok[i] = (v, t)

    def prepare(i):
        if i < st2["prep"] or i >= len(plan2):
            return True
        v, t = raw_tok[i]
        _, dims, split = plan2[i]
        if split:
            slot = st2["split"] % 2
            if hl_free[slot] == "busy":
                return False
            n = dims[0] * dims[1]
            hi = HLt[:, slot * 2, 0:n].rearrange("p (k c) -> p k c", k=dims[0])
            lo = HLt[:, slot * 2 + 1, 0:n].rearrange("p (k c) -> p k c", k=dims[0])
            a = A.act(hi, v, ACT.Copy, t, hl_free[slot])
            b = V.tt(lo, v, hi.bitcast(F32), ALU.subtract, a, t)
            hl_free[slot] = "busy"
            st2["split"] += 1
            views[i] = ((hi, lo), b, slot)
            freed[i] = (a, b)
            load2()
            load2()
        else:
            views[i] = (v, t, None)
        st2["prep"] = i + 1
        return True

    def weight2():
        i = st2["next"]
        st2["next"] += 1
        assert prepare(i)
        w, t, slot = views[i]
        out_queue.append((i, slot))
        j = i + 1
        while j < i + 3 and j < st2["loaded"] and j < len(plan2):
            if not prepare(j) or plan2[j][2]:
                break
            j += 1
        return w, t

    def used2(tok):
        i, slot = out_queue.pop(0)
        if slot is None:
            freed[i] = (tok,)
            load2()
            load2()
        else:
            hl_free[slot] = tok

    def split_of(dst, src, tok):
        a = A.act(dst[0], src, ACT.Copy, tok)
        return [a, V.tt(dst[1], src, dst[0].bitcast(F32), ALU.subtract, a, tok)]

    def group3(dst, pairs, *after):
        PE.need(*after)
        n = len(pairs)
        for i, (l, r) in enumerate(pairs):
            for j, (x, y) in enumerate(((0, 0), (0, 1), (1, 0))):
                m = nc.tensor.matmul(dst, l[x], r[y], start=(i == 0 and j == 0), stop=(i == n - 1 and j == 2))
        return PE.done(m)

    def cols3(x, k, c0, n):
        return (x[0][:, k, c0:c0 + n], x[1][:, k, c0:c0 + n])

    def project3(w, tw, c0, n, dst_of, evacuate=evac, *after):
        for t in range(4):
            b = bank()
            tok = group3(PS[:, b, 0:n], [(cols3(xT, k, t * 128, 128), cols3(w, k, c0, n)) for k in range(8)],
                         pf[b], tw, *after)
            pf[b] = evacuate(dst_of(t), PS[:, b, 0:n], tok)
        return tok

    def project3_T(w, tw, c0, evacuate, *after):
        b = bank()
        tok = group3(PS[:, b, :], [(cols3(w, k, c0, 128), cols3(xT, k, 0, 512)) for k in range(8)], pf[b], tw, *after)
        pf[b] = evacuate(0, 512, PS[:, b, :], tok)
        return tok

    load2()
    load2()
    GBL = GB_AT
    XT = XR + 4096
    maskT = sb(XT, 512)
    tri = sb(XT + 512, 512)
    T5C = sb(XT + 1024, 8, 4, 32)
    t1 = MQ.go(maskT, D["cmask2"], *f)
    t2 = MQ.go(tri, D["tri"], *f)
    t3 = MQ.go(vmask, D["vmask"], *f)
    t5s = [MQ.go(T5, bass.AP(scr, 127, [[639, 128], [81920, 8], [1, 512]]), tbs, *f)]
    gb = [sb(GBL, 1024), sb(GBL + 1024, 1024)]

    def load_gb(n, *after):
        l, i = n // 3, n % 3
        return [MQ.go(gb[0], bcast(D["ln_g_2"][l, i], 0, 128), *after),
                MQ.go(gb[1], bcast(D["ln_b_2"][l, i], 0, 128), *after)]

    def norm_stats(t):
        mv = small[:, t * 32:t * 32 + 32]
        for h in range(2):
            V.begin(())
            V.done(nc.vector.bn_stats(mv[:, h * 6:h * 6 + 6], X[:, t, h * 512:h * 512 + 512]))
        V.begin(())
        V.done(nc.vector.bn_aggr(mv[:, 12:14], mv[:, 0:12]))
        V.ts1(mv[:, 14:15], mv[:, 13:14], LN_EPS, ALU.add)
        return A.act(mv[:, 16:17], mv[:, 14:15], ACT.Sqrt, V.last())

    def norm_apply(t, ta, gtok):
        mv = small[:, t * 32:t * 32 + 32]
        r, x1 = mv[:, 15:16], mv[:, 17:18]
        V.recip(r, mv[:, 16:17], ta)
        V.tt(x1, r, r, ALU.mult)
        V.tt(x1, x1, mv[:, 14:15], ALU.mult)
        V.ts(x1, x1, -0.5, ALU.mult, 1.5, ALU.add)
        V.tt(r, r, x1, ALU.mult)
        tb = V.stt(mv[:, 18:19], mv[:, 12:13], -1.0, r, ALU.mult, ALU.mult)
        a = A.act(X[:, t, :], X[:, t, :], ACT.Identity, tb, scale=r, bias=mv[:, 18:19])
        for e, c in ((G, 640), (V, 0)):
            x = X[:, t, c:c + 384 if c else 640]
            n = 384 if c else 640
            e.tt(x, x, gb[0][:, c:c + n], ALU.mult, a, gtok)
            e.tt(x, x, gb[1][:, c:c + n], ALU.add)
        return [V.last(), G.last()]

    def tile_T(t, tok):
        for h in range(2):
            b = bank()
            PE.need(pf[b], tok)
            for i in range(4):
                k = h * 4 + i
                m = nc.tensor.transpose(PS[:, b, i * 128:i * 128 + 128], X[:, t, k * 128:k * 128 + 128], ident[:, :])
            dst = [x[:, h * 4:h * 4 + 4, t * 128:t * 128 + 128] for x in xT]
            src = PS[:, b, :].rearrange("p (k c) -> p k c", k=4)
            pf[b] = split_of(dst, src, PE.done(m))

    def residual(products, n, more=True, scale=ALPHA, fill=None):
        st, done = {}, {}
        for t in range(4):
            for h in range(2):
                b, tok = products(t, h)
                x = X[:, t, h * 512:h * 512 + 512]
                pf[b] = V.stt(x, x, scale, PS[:, b, :], ALU.mult, ALU.add, tok)
            st[t] = norm_stats(t)
            if t:
                done[t - 1] = norm_apply(t - 1, st[t - 1], gbt[0])
            if more and t > 1:
                tile_T(t - 2, done[t - 2])
        done[3] = norm_apply(3, st[3], gbt[0])
        if fill:
            fill()
        if more:
            tile_T(2, done[2])
            tile_T(3, done[3])
            gbt[0] = load_gb(n + 1, V.last(), G.last())
        PE.need(V.last(), A.last())
        return [V.last(), G.last()]

    def from_chunks(lhs_of, kt, parts, ready):
        def products(t, h):
            w, tw = parts[h]
            b = bank()
            return b, group(PS[:, b, :], [(lhs_of(k, t), w[:, k, :]) for k in range(kt)], pf[b], tw, *ready)
        return products

    gbt = [load_gb(0, *f)]

    def plain_final(dst, ob):
        return lambda tok: evac(dst, PS[:, ob, :], tok)

    for e in (V, A):
        e.need(tbs)
    for t in range(4):
        tile_T(t, V.last())
    PE.need(V.last(), A.last())
    for e in (PE, V, A, G):
        e.need(t1, t2, t3, t5s)
    G.zero(T5C, FAR)
    for q in range(4):
        n = min(31, 8 * q + 7)
        c = 415 - 128 * q
        G.copy(T5C[:, :, q, 0:n], T5[:, :, c:c + 16 * (n - 1) + 1:16])
    for l in range(2):
        area = ExitStack()
        regions[2:] = [(AREA, area.enter_context(nc.sbuf_tensor(f"area{l}", [128, AREA_END - AREA], F32)))]
        oT = sb(AREA, 8, 512)
        B2 = AREA + 4096
        nqT = sb(B2, 4, 512)
        kp = sb(B2 + 2048, 2, 4, 512)
        vv = sb(B2 + 6144, 4, 2, 128)
        gt = sb(B2 + 7168, 4, 24)
        Pc = sb(B2 + 7264, 8, 4, 32)
        kcp = sb(B2 + 8288, 4, 32)
        vc2 = sb(B2 + 8416, 2, 64)
        PB = B2 + 8544
        kkT = sb(PB, 2, 512)
        CC = sb(PB + 1024, 2, 512)
        cs_ = sb(PB + 2048, 2, 512)
        pe = sb(PB + 3072, 2, 16)
        w2 = sb(PB + 3136, 2, 64)
        hid = sb(PB + 3264, 2, 3, 128)
        hidT_ = sb(PB + 4032, 2, 64)
        f = barrier()
        tpe = MQ.go(pe, D["peT"][l], *f)
        tw2 = MQ.go(w2, D["cmpw2"][l], *f)
        G.zero(vc2, 0.0)
        G.zero(kcp, 0.0)
        for i in range(2):
            G.zero(kp[64:128, i, 0, :], 0.0)
            G.zero(kp[0:64, i, 3, :], 0.0)
            G.zero(kp[0:64, i, 1, :], 0.0)
            G.zero(kp[64:128, i, 2, :], 0.0)
        for n in range(2):
            w, tw = weight2()
            for j in range(2):
                tok = project3_T(w, tw, j * 128,
                                 lambda t0, n, ps, tok, j=2 * n + j: evac(nqT[:, j, :], ps, tok, scale=-0.125))
            used2(tok)
        w, tw = weight2()
        b = bank()
        tok = group3(PS[0:60, b, :], [(cols3(w, k, 0, 60), cols3(xT, k, 0, 512)) for k in range(8)], pf[b], tw)
        used2(tok)
        narrow = sb(B2 + 7264, 512)
        pf[b] = tok = evac(narrow[0:60, :], PS[0:60, b, :], tok)
        b = bank()
        PE.need(pf[b], tok)
        for t in range(4):
            m = nc.tensor.transpose(PS[:, b, t * 60:t * 60 + 60], narrow[0:60, t * 128:t * 128 + 128],
                                    ident[0:60, 0:60])
        tok = PE.done(m)
        src = PS[:, b, 0:240].rearrange("p (t c) -> p t c", t=4)
        V.copy(gt, src[:, :, 0:24], tok)
        pf[b] = V.copy(rest, src[:, :, 24:60])
        w, tw = weight2()
        for j in range(2):
            tok = project3_T(w, tw, j * 128, lambda t0, n, ps, tok, j=j: evac(kkT[:, j, :], ps, tok))
        used2(tok)
        t_cs = [swap(cs_[:, kv, :], kkT[:, kv, :], V.last(), A.last()) for kv in range(2)]
        w, tw = weight2()
        for i in range(2):
            tok = project3_T(w, tw, i * 128, split_heads(kp[:, i, 0, :], kp[:, i, 3, :]))
        used2(tok)
        ctok = [None]

        def hidden(kv):
            V.need(tpe, t_cs[kv])
            V.zero(CC[64:128, :, 496:512], 0.0, ctok[0])
            for g in range(2):
                for a in range(2):
                    src = (kkT if g == a else cs_)[a * 64:a * 64 + 64, kv, 16 * a:512]
                    n = 32 - a
                    V.tt(CC[a * 64:a * 64 + 64, g, 0:16 * n].rearrange("p (n l) -> p n l", l=16),
                         src.rearrange("p (n l) -> p n l", l=16), bcast(pe[a * 64:a * 64 + 64, kv, :], 1, n), ALU.add)
            w, tw = weight2()
            b = bank()
            cf = CC.rearrange("p g t -> p (g t)")
            tok = group(PS[0:64, b, 0:128], [(cf[:, i:i + 16 * 63 + 1:16], w[:, i, :]) for i in range(16)],
                        pf[b], tw, V.last())
            used2(tok)
            ctok[0] = tok
            hx, hy, gx = hid[0:64, kv, 0, :], hid[0:64, kv, 1, :], hid[0:64, kv, 2, :]
            pf[b] = V.copy(hx, PS[0:64, b, 0:128], tok)
            V.tt(hy, hx, hx, ALU.mult)
            V.ts(hy, hy, 0.044715, ALU.mult, 1.0, ALU.add)
            V.tt(hy, hy, hx, ALU.mult)
            t = A.act(hy, hy, ACT.Tanh, V.last(), scale=math.sqrt(2.0 / math.pi))
            V.stt(gx, hy, 1.0, hx, ALU.add, ALU.mult, t)
            return gx, V.ts1(gx, gx, 0.5, ALU.mult)

        def compressed(kv, gx, tg_):
            hidT = hidT_[:, kv, :]
            b = bank()
            PE.need(pf[b], tg_)
            m = nc.tensor.transpose(PS[:, b, 0:64], gx, ident[0:64, 0:64])
            pf[b] = V.copy(hidT, PS[:, b, 0:64], PE.done(m))
            b = bank()
            if kv == 0:
                for g in range(2):
                    tok = group(PS[g * 64:g * 64 + 64, b, 0:31], [(w2[:, 0, :], hidT[:, g * 32:g * 32 + 31])],
                                pf[b], V.last(), tw2)
                V.copy(kcp[0:64, 0, 0:31], PS[0:64, b, 0:31], tok, G.last())
                pf[b] = V.copy(kcp[64:128, 3, 0:31], PS[64:128, b, 0:31])
                t_s.extend([MQ.go(kcp[64:128, 1, :], kcp[0:64, 0, :], pf[b]),
                        MQ.go(kcp[0:64, 2, :], kcp[64:128, 3, :], pf[b])])
            else:
                for g in range(2):
                    tok = group(PS[0:31, b, g * 64:g * 64 + 64], [(hidT[:, g * 32:g * 32 + 31], w2[:, 1, :])],
                                pf[b], V.last(), tw2)
                pf[b] = V.copy(vc2[0:31, :, :], PS[0:31, b, 0:128].rearrange("p (g c) -> p g c", g=2), tok, G.last())

        g0 = hidden(0)
        w, tw = weight2()
        used2(project3(w, tw, 0, 256, lambda t: vv[:, t, :, :].rearrange("p b c -> p (b c)")))
        t = A.act(gt, gt, ACT.Tanh, V.last(), scale=0.5)
        V.ts(gt, gt, 0.5, ALU.mult, 0.5, ALU.add, t)
        t = [V.last(), A.last()]
        t_s = [MQ.go(kp[64:128, :, 1, :], kp[0:64, :, 0, :], *t), MQ.go(kp[0:64, :, 2, :], kp[64:128, :, 3, :], *t)]
        g1 = hidden(1)
        compressed(0, *g0)
        compressed(1, *g1)
        f = barrier()
        P, PT = grid(PB, 6, 512) + grid(AREA + 2048, 4, 512), grid(PB + 3072, 2, 512)
        gview = gt.rearrange("p t (h b) -> p t h b", b=3)
        PE.need(t_s)
        ctok = []
        for half in range(2):
            b = 6 + half
            PE.need(pf[b])
            for i in range(4):
                h = half * 4 + i
                for q in range(4):
                    m = nc.tensor.matmul(PS[:, b, (i * 4 + q) * 32:(i * 4 + q) * 32 + 32],
                                         nqT[:, h // 2, q * 128:q * 128 + 128], kcp[:, half * 2 + h % 2, :],
                                         start=True, stop=True)
            ctok.append(PE.done(m))
        Pg = Pc.rearrange("p h q c -> p (h q) c")
        mn, sm = sc_[:, 0, :], sc_[:, 1, :]
        for half in range(2):
            hs = slice(half * 4, half * 4 + 4)
            pf[6 + half] = V.tt(Pc[:, hs, :, :].rearrange("p h q c -> p (h q c)"), PS[:, 6 + half, :],
                                T5C[:, hs, :, :].rearrange("p h q c -> p (h q c)"), ALU.add, ctok[half])
        ptok = []

        def gated():
            V.recip(sm, sm)
            for q in range(4):
                V.tt(sm.rearrange("p (h q) -> p h q", q=4)[:, :, q], sm.rearrange("p (h q) -> p h q", q=4)[:, :, q],
                     gview[:, q, :, 0], ALU.mult)
        extra = [
            lambda: V.red(mn, Pg, ALU.min),
            lambda: V.tt(Pg, Pg, bcast(mn, 2, 32), ALU.subtract),
            lambda: A.act(Pg, Pg, ACT.Exp, V.last(), scale=-1.0),
            lambda: None,
            lambda: V.red(sm, Pg, ALU.add, A.last()),
            gated,
            lambda: V.tt(Pg, Pg, bcast(sm, 2, 32), ALU.mult),
            lambda: ptok.append(V.tt(Pc[:, :, 0, :], Pc[:, :, 0, :], bcast(vmask, 1, 8), ALU.mult)),
        ]
        jobs = []
        for pair in range(4):
            for half in range(2):
                h = pair * 2 + half
                g = h // 4
                ob = 6 + pair % 2
                for br in (1, 2):
                    ksrc = kp[:, br - 1, g * 2 + half, :]

                    def sc(q, pair=pair, ksrc=ksrc):
                        return [(0, (q + 1) * 128, nqT[:, pair, q * 128:q * 128 + 128], ksrc[:, 0:(q + 1) * 128])]

                    def segs(q, h=h):
                        return None, (0, (q + 1) * 128, T5[:, h, 384 - 128 * q:512])
                    keys = [(lambda q, c=kt * 128: c, 128, kt, 4, vv[:, kt, br - 1, g * 64:g * 64 + 64])
                            for kt in range(4)]
                    jobs.append(dict(nq=4, scores=sc, segs=segs, out=(ob, half), first=br == 1, last=False,
                                     gate=gview[:, :, h, br], keys=keys))
                jobs.append(dict(nq=0, out=(ob, half), first=False, last=True, P=[Pc[:, h, q, :] for q in range(4)],
                                 ptok=ptok, keys=[(lambda q: 0, 32, 0, 4, vc2[0:32, g, :])],
                                 final=plain_final(oT[:, pair, :], ob) if half else None))
        attention(jobs, P, PT, wide=False, extra=extra)
        f = barrier()

        cq = sb(B2, 4, 544)
        km = sb(B2 + 2176, 4, 384)
        vm = sb(B2 + 3712, 4, 256)
        qmT = sb(B2 + 4736, 4, 512)
        kmT = sb(B2 + 6784, 4, 512)
        PB = B2 + 8832
        qm = sb(PB, 4, 384)
        cT_ = sb(PB + 1536, 4, 512)
        gq = sb(AREA + 3072, 512)
        tmpm = sb(AREA + 3584, 512)
        tg = MQ.go(gq, bcast(D["mlag"][l], 0, 128), *f)
        for c0, n in ((0, 256), (256, 256)):
            w, tw = weight2()
            used2(project3(w, tw, 0, n, lambda t: cq[:, t, c0:c0 + n]))
        A.need(V.last())
        for t in range(4):
            A.act(tmpm[:, 0:384], cq[:, t, 0:384], ACT.Square, acc=small[:, t:t + 1])
            A.act(tmpm[:, 384:512], cq[:, t, 384:512], ACT.Square, acc=small[:, 4 + t:5 + t])
        V.need(A.last())
        V.ts(small[:, 0:4], small[:, 0:4], 1.0 / 384, ALU.mult, EPS, ALU.add)
        V.ts(small[:, 4:8], small[:, 4:8], 1.0 / 128, ALU.mult, EPS, ALU.add)
        rsqrt(small[:, 8:16], small[:, 0:8], small[:, 16:24], V.last())
        for t in range(4):
            V.stt(cq[:, t, 0:384], cq[:, t, 0:384], small[:, 8 + t:9 + t], gq[:, 0:384], ALU.mult, ALU.mult, tg)
            V.stt(cq[:, t, 384:512], cq[:, t, 384:512], small[:, 12 + t:13 + t], gq[:, 384:512], ALU.mult, ALU.mult)
        flip(lambda k: cT_[:, k, :], lambda k, t: cq[:, t, k * 128:k * 128 + 128], range(4), range(4),
             after=[V.last()])
        w, tw = weight2()
        V.need(A.last())
        used2(project(w, tw, 3, 0, 384, cT_, range(4), lambda t: qm[:, t, :],
                     lambda d, s, tok: evac(d, s, tok, scale=-(96 ** -0.5)), V.last(), A.last()))
        w, tw = weight2()

        def ev_kv(t, ps, tok):
            v4 = ps.rearrange("p (h c) -> p h c", h=4)
            V.copy(km[:, t, :].rearrange("p (h c) -> p h c", h=4)[:, :, 0:64], v4[:, :, 0:64], tok)
            return V.copy(vm[:, t, :].rearrange("p (h c) -> p h c", h=4), v4[:, :, 64:128])
        used2(project(w, tw, 1, 0, 512, cT_[:, 3:4, :], range(4), lambda t: t, ev_kv))
        V.need(A.last())
        V.need(PE.last())
        u = [sb(PB + 1536 + i * 256, 4, 4, 16) for i in range(4)]
        r = [sb(PB + 2560 + i * 64, 4, 16) for i in range(4)]
        rk = sb(PB + 2816, 4, 32)
        q4 = qm.rearrange("p t (h c) -> p t h c", h=4)
        k4 = km.rearrange("p t (h c) -> p t h c", h=4)
        c4, s4 = bcast(cos2, 2, 4), bcast(sin2, 2, 4)
        kr = rest
        V.tt(r[0], kr[:, :, 0:16], cos2, ALU.mult)
        V.tt(r[1], kr[:, :, 16:32], sin2, ALU.mult)
        V.tt(r[2], kr[:, :, 0:16], sin2, ALU.mult)
        V.tt(r[3], kr[:, :, 16:32], cos2, ALU.mult)
        V.tt(rk[:, :, 0:16], r[0], r[1], ALU.subtract)
        V.tt(rk[:, :, 16:32], r[2], r[3], ALU.add)
        V.copy(k4[:, :, :, 64:96], bcast(rk, 2, 4))
        flip(lambda h: kmT[0:96, h, :], lambda h, t: km[:, t, h * 96:h * 96 + 96], range(4), range(4), m=96,
             after=[V.last()], evacuate=lambda d, s_, tok: A.act(d, s_, ACT.Copy, tok))
        a, b_ = q4[:, :, :, 64:80], q4[:, :, :, 80:96]
        V.tt(u[0], a, c4, ALU.mult)
        V.tt(u[1], b_, s4, ALU.mult)
        V.tt(u[2], a, s4, ALU.mult)
        V.tt(u[3], b_, c4, ALU.mult)
        V.tt(a, u[0], u[1], ALU.subtract)
        V.tt(b_, u[2], u[3], ALU.add)
        flip(lambda h: qmT[0:96, h, :], lambda h, t: qm[:, t, h * 96:h * 96 + 96], range(4), range(4), m=96,
             after=[V.last()])
        barrier()
        P, PT = grid(PB, 8, 512) + grid(B2, 4, 512), grid(B2 + 2176, 3, 512)
        jobs = []
        for h in range(4):
            half, ob = h % 2, 6 + h // 2

            def sc(q, h=h):
                return [(0, (q + 1) * 128, qmT[0:96, h, q * 128:q * 128 + 128], kmT[0:96, h, 0:(q + 1) * 128])]
            jobs.append(dict(nq=4, scores=sc,
                             segs=lambda q: (None, (0, (q + 1) * 128, maskT[:, 384 - 128 * q:512])),
                             out=(ob, half), first=True, last=True,
                             keys=[(lambda q, c=kt * 128: c, 128, kt, 4, vm[:, kt, h * 64:h * 64 + 64])
                                   for kt in range(4)],
                             final=plain_final(oT[:, 4 + h // 2, :], ob) if half else None))
        attention(jobs, P, PT, wide=False)
        f = barrier()

        fq = sb(B2, 2, 512)
        fk = sb(B2 + 1024, 4, 512)
        fv = sb(B2 + 3072, 4, 256)
        ff = sb(B2 + 4096, 4, 4)
        lsn = sb(B2 + 4112, 4, 4)
        cum = sb(B2 + 4128, 4, 4)
        ft = sb(B2 + 4144, 16)
        bf = sb(B2 + 4160, 4)
        Bk = sb(B2 + 4224, 4, 512)
        PB = B2 + 6272
        for h in range(4):
            G.zero(fk[64 - 64 * (h % 2):128 - 64 * (h % 2), h, :], 0.0)
        tbf = MQ.go(bf, bcast(D["fox_b_f_2"][l], 0, 128), *f)
        V.tt(ff, rest[:, :, 32:36], bcast(bf, 1, 4), ALU.add, tbf)
        fl = ff.rearrange("p a b -> p (a b)")
        ll = lsn.rearrange("p a b -> p (a b)")
        V.stt(ft, fl, -1.0, fl, ALU.mult, ALU.max)
        t = A.act(ft, ft, ACT.Exp, V.last(), scale=-1.0)
        t = A.act(ft, ft, ACT.Ln, bias=ones[:, 0:1])
        V.stt(ll, fl, 0.0, ft, ALU.min, ALU.subtract, t)
        V.ts1(ll, ll, -1.0, ALU.mult)
        for n in range(2):
            w, tw = weight2()
            for j in range(2):
                tok = project3_T(w, tw, j * 128, split_heads(fk[:, 2 * j, :], fk[:, 2 * j + 1, :]) if n else
                                 (lambda t0, n, ps, tok, j=j: evac(fq[:, j, :], ps, tok, scale=-0.125)))
            used2(tok)
        w, tw = weight2()
        used2(project3(w, tw, 0, 256, lambda t: fv[:, t, :]))
        for i in range(4):
            b = bank()
            tok = group(PS[:, b, 0:4], [(tri[:, (i - j) * 128:(i - j) * 128 + 128], lsn[:, j, :])
                                        for j in range(i + 1)], pf[b], V.last())
            pf[b] = V.copy(cum[:, i, :], PS[:, b, 0:4], tok)
        V.ts1(ll, ll, -1.0, ALU.mult, PE.last())
        for h in range(4):
            b = bank()
            PE.need(pf[b], V.last())
            for j in range(4):
                m = nc.tensor.matmul(PS[:, b, 128 * j:512], lsn[:, j, h:h + 1].to_broadcast([128, 128]),
                                     tri[:, 0:512 - 128 * j], start=(j == 0), stop=(j == 3))
            pf[b] = evac(Bk[:, h, :], PS[:, b, :], PE.done(m))
        f = barrier()
        P, PT = grid(PB, 10, 512), grid(PB + 5120, 3, 512)
        jobs = []
        for h in range(4):
            half, ob = h % 2, 6 + h // 2

            def sc(q, h=h):
                return [(0, (q + 1) * 128, fq[:, h // 2, q * 128:q * 128 + 128], fk[:, h, 0:(q + 1) * 128])]
            jobs.append(dict(nq=4, scores=sc,
                             segs=lambda q: (None, (0, (q + 1) * 128, maskT[:, 384 - 128 * q:512])),
                             pre=lambda q, h=h: (cum[:, q, h:h + 1], Bk[:, h, 0:(q + 1) * 128]),
                             out=(ob, half), first=True, last=True,
                             keys=[(lambda q, c=kt * 128: c, 128, kt, 4, fv[:, kt, h * 64:h * 64 + 64])
                                   for kt in range(4)],
                             final=plain_final(oT[:, 6 + h // 2, :], ob) if half else None))
        attention(jobs, P, PT, wide=False)
        f = barrier()

        mg = sb(B2, 8, 512)
        brv = grid(B2 + 4096, 2, 512)
        gm = grid(B2 + 5120, 2, 512)
        wm = [sb(B2 + 6144, 8, 512), oT]
        mem, memT = sb(B2 + 10240, 2, 1024), sb(B2 + 4096, 8, 256)
        va = sb(B2 + 12288, 2, 256)
        tm = MQ.go(mem, D["mem_2"].rearrange("(t p) d -> p t d", p=128), *f)
        for h in range(4):
            G.zero(ka[64 - 64 * (h % 2):128 - 64 * (h % 2), h, :], 0.0)

        def memory_kv():
            def on_act(d, x, tok):
                return A.act(d, x, ACT.Copy, tok)

            def two(lo, hi):
                def ev(t0, n, ps, tok):
                    on_act(lo[0:64, t0:t0 + n], ps[0:64], tok)
                    return on_act(hi[64:128, t0:t0 + n], ps[64:128], tok)
                return ev
            A.need(brv_free)
            for k in range(8):
                b = bank()
                PE.need(pf[b], tm)
                for t in range(2):
                    m = nc.tensor.transpose(PS[:, b, t * 128:t * 128 + 128], mem[:, t, k * 128:k * 128 + 128],
                                            ident[:, :])
                pf[b] = on_act(memT[:, k, :], PS[:, b, 0:256], PE.done(m))
            w, tw = weight2()
            for j in range(2):
                tok = project_T(w, tw, 8, j * 128, 128, memT, [(0, 256)], two(ka[:, 2 * j, :], ka[:, 2 * j + 1, :]),
                                A.last())
            used2(tok)
            w, tw = weight2()
            used2(project(w, tw, 8, 0, 256, memT, range(2), lambda t: va[:, t, :], on_act))
        twm = [MQ.go(wm[0], rows(D["w_mix_out_2"][l], 0, 8, 0, 512), *f), None]
        for br, k0, kt in ((0, 0, 4), (1, 4, 2), (2, 6, 2)):
            for n in range(4):
                wb, twb = weight2()
                w, tw = weight2()
                toks = []
                for i in range(2):
                    m_ = n * 2 + i
                    v = brv[m_ % 2]
                    toks.append(project_T(wb, twb, kt, i * 128, 128, oT[:, k0:k0 + kt, :], [(0, 512)],
                                          lambda t0, nn, ps, tok, v=v: evac(v, ps, tok, V.last(), G.last())))
                used2(toks[-1])
                if br == 2 and n == 3:
                    twm[1] = MQ.go(wm[1], rows(D["w_mix_out_2"][l], 0, 8, 512, 1024), toks[-1])
                for i in range(2):
                    m_ = n * 2 + i
                    v, gmb = brv[m_ % 2], gm[m_ % 2]

                    def ev(t0, nn, ps, tok, m_=m_, gmb=gmb, v=v, br=br):
                        a = A.act(gmb, ps, ACT.Tanh, tok, V.last(), G.last(), scale=0.5)
                        V.need(A.last())
                        if br == 0:
                            V.stt(mg[:, m_, :], gmb, 1.0, v, ALU.add, ALU.mult, a)
                        else:
                            V.stt(gmb, gmb, 1.0, v, ALU.add, ALU.mult, a)
                            G.tt(mg[:, m_, :], mg[:, m_, :], gmb, ALU.add, V.last())
                        return a
                    tok = project3_T(w, tw, i * 128, ev)
                used2(tok)
        V.need(G.last())
        brv_free = [V.ts1(mg, mg, 0.5, ALU.mult), G.last()]
        tn = residual(from_chunks(lambda k, t: mg[:, k, t * 128:t * 128 + 128], 8,
                                  [(wm[0], twm[0]), (wm[1], twm[1])], [V.last()]), 3 * l,
                      fill=memory_kv)
        f = barrier()
        qa = sb(B2 + 4096, 2, 512)
        PB = B2 + 6656
        w, tw = weight2()
        for j in range(2):
            tok = project3_T(w, tw, j * 128, lambda t0, n, ps, tok, j=j: evac(qa[:, j, :], ps, tok, scale=-0.125))
        used2(tok)
        barrier()
        P, PT = grid(PB, 14, 256), grid(B2, 3, 512)
        jobs = []
        for h in range(4):
            half, ob = h % 2, 6 + h // 2

            def sc(q, h=h):
                return [(0, 256, qa[:, h // 2, q * 128:q * 128 + 128], ka[:, h, :])]
            jobs.append(dict(nq=4, scores=sc, segs=lambda q: ((0, 256), None), out=(ob, half), first=True,
                             last=True,
                             keys=[(lambda q, c=kt * 128: c, 128, 0, 4, va[:, kt, h * 64:h * 64 + 64])
                                   for kt in range(2)],
                             final=plain_final(oT[:, h // 2, :], ob) if half else None))
        attention(jobs, P, PT, wide=False)
        barrier()
        w, tw = weight2()
        ws = [(w[:, :, 0:512], tw), (w[:, :, 512:1024], tw)]
        residual(from_chunks(lambda k, t: oT[:, k, t * 128:t * 128 + 128], 2, ws, [V.last()]), 3 * l + 1)
        used2(PE.last())
        f = barrier()
        area.close()
        regions[2:] = []
        area = ExitStack()
        hdt = area.enter_context(nc.sbuf_tensor(f"hd{l}", [128, 2, 16, 512], F32R))
        sq = area.enter_context(nc.sbuf_tensor(f"sq{l}", [128, 512], F32))[:, 0:512]
        hd = (hdt[:, 0], hdt[:, 1])
        bs = {(t, h): (t * 2 + h) for t in range(4) for h in range(2)}
        for half in range(2):
            for n in range(8):
                w, tw = weight2()
                for i in range(2):
                    j = n * 2 + i

                    def ev(t0, nn, ps, tok, j=j):
                        rel = A.act(sq, ps, ACT.Relu, tok, V.last())
                        v = V.tt(sq, sq, sq, ALU.mult, rel)
                        split_of((hd[0][:, j, :], hd[1][:, j, :]), sq, v)
                        return rel
                    tok = project3_T(w, tw, i * 128, ev)
                used2(tok)
            PE.need(V.last(), A.last())
            for b in range(8):
                PE.need(pf[b])

            def down(t, n, r, w, tw):
                PE.need(tw)
                for k in range(8):
                    for q, (x, y) in enumerate(((0, 0), (0, 1), (1, 0))):
                        m = nc.tensor.matmul(PS[:, bs[t, n // 2], (n % 2) * 256:(n % 2) * 256 + 256],
                                             hd[x][:, r * 8 + k, t * 128:t * 128 + 128], w[y][:, k, :],
                                             start=(r == 0 and k == 0 and q == 0 and n % 2 == 0),
                                             stop=(r == 1 and k == 7 and q == 2 and n % 2 == 1))
                return PE.done(m)
            for r in range(2):
                for n in range(4):
                    w, tw = weight2()
                    if r == 1 and n == 3 and half == 1:
                        break
                    for t in range(4):
                        tok = down(t, n, r, w, tw)
                    used2(tok)
            if half == 0:
                for t in range(4):
                    for h in range(2):
                        x = X[:, t, h * 512:h * 512 + 512]
                        pf[bs[t, h]] = V.stt(x, x, ALPHA, PS[:, bs[t, h], :], ALU.mult, ALU.add, tok)
                rot["b"] = 7
        rot["b"] = 7
        t = residual(lambda t, h: (bs[t, h], down(t, 3, 1, w, tw) if h == 0 else PE.last()), 3 * l + 2,
                     more=l == 0, scale=1.0)
        used2(PE.last())
        f = barrier()
        area.close()
    t = MQ.go(out.rearrange("(t p) d -> p t d", p=128), X[:, 0:4, :], t)
    barrier()
    for s, v in zip(MQ.sems, MQ.vals):
        G.need((s, v))
    for s, v in zip(WQ.sems, WQ.vals):
        WQ.w.need((s, v))


def constants():
    f = np.float32
    c = {"ident": np.eye(128, dtype=f)}
    t = np.arange(512)
    inv = (f(10000.0) ** (-np.arange(16, dtype=f) / f(16))).astype(f)
    ang = np.concatenate([(t // 64).astype(f)[:, None] * inv, (t % 64).astype(f)[:, None] * inv], -1)
    c["cos1"], c["sin1"] = np.cos(ang).astype(f), np.sin(ang).astype(f)
    ang = t.astype(f)[:, None] * inv[None, :]
    c["cos2"], c["sin2"] = np.cos(ang).astype(f), np.sin(ang).astype(f)
    k = np.arange(512)
    tk = (t[:, None] * k[None, :]) % 1024
    cs, sn = np.cos(2 * np.pi * tk / 1024), np.sin(2 * np.pi * tk / 1024)
    alt = np.where(t % 2 == 0, 1.0, -1.0)
    fi = -sn.copy()
    fi[:, 0] = alt
    c["dftf"] = np.concatenate([cs, fi], 1).astype(f)
    gr = 2 * cs.T / 1024
    gr[0] = 1 / 1024
    gi = -2 * sn.T / 1024
    gi[0] = alt / 1024
    c["dftg"] = np.concatenate([gr, gi], 0).astype(f)
    t2 = np.arange(256)
    tk = (t2[:, None] * t2[None, :]) % 512
    gi2 = -2 * np.sin(2 * np.pi * tk / 512) / 1024
    gi2[0] = np.where(t2 % 2 == 0, 1.0, -1.0) / 1024
    c["g2i"] = gi2.astype(f)
    z = []
    for n in (512, 256):
        tt = np.linspace(0.0, 1.0, n, dtype=f)[:, None]
        w = (2.0 * np.pi * np.arange(n, dtype=f)[:, None] / f(n)).astype(f)
        fb = np.linspace(1e-4, 15, 16, dtype=f)[None, :]
        z.append(np.concatenate([tt, np.cos((fb * w).astype(f)), -np.sin((fb * w).astype(f))], -1).astype(f))
        d = np.linspace(math.log(1e-2) / 1.5, math.log(1e-2) / 0.3, 512, dtype=f)
        c["decay1" if n == 512 else "decay2"] = np.exp(-tt * np.abs(d)).astype(f)
    c["hyz"] = np.ascontiguousarray(np.concatenate(z, 0).T)
    p, j = np.arange(128)[:, None], np.arange(384)[None, :]
    c["wmask"] = np.where(np.abs(j - 128 - p) <= 128, 0.0, FAR).astype(f)
    col, kc = np.arange(128)[:, None] % 64, np.arange(64)[None, :]
    c0 = np.clip(col - 8, 0, 48)
    c["cmask"] = np.where((kc >= c0) & (kc < c0 + 16), 0.0, FAR).astype(f)
    j = np.arange(512)[None, :]
    c["cmask2"] = np.where(p - j + 384 >= 0, 0.0, FAR).astype(f)
    c["tri"] = (p <= j).astype(f)
    cc = np.arange(32)[None, :]
    c["vmask"] = (p - 16 * cc - 31 >= 0).astype(f)
    dist = 511 - np.arange(640)
    n = np.maximum(dist, 0)
    nf = np.maximum(n, 1).astype(f)
    large = 16 + (np.log(nf / f(16)) / f(math.log(128 / 16)) * f(16)).astype(np.int32)
    bucket = np.where(n < 16, n, np.minimum(large, 31))
    oh = np.zeros((33, 640), f)
    for i in range(639):
        oh[bucket[i] if dist[i] >= 0 else 32, i] = 1.0
    c["onehot"] = oh
    return c


def layouts(I):
    f = np.float32
    L = {}
    L["cT"] = np.stack([I["c"][0].reshape(8, 128).T, I["c_ctx"].reshape(8, 128).T], -1)
    L["b_adaT"] = I["b_ada"].reshape(2, 24, 128).transpose(0, 2, 1)
    L["norm_gT"] = I["norm_g"].reshape(2, 8, 128).transpose(0, 2, 1)
    L["g10_0"] = np.concatenate([np.tile(I["glob_q_norm"][0], 8), np.tile(I["glob_k_norm"][0], 2)])
    L["g10_1"] = np.concatenate([np.tile(I["win_q_norm"][0], 8), np.tile(I["win_k_norm"][0], 2)])
    L["g16"] = np.concatenate([np.tile(I["nat_q_norm"][0], 8), np.tile(I["nat_k_norm"][0], 8)])
    L["convT"] = np.concatenate([I["hy_conv_w"][0], I["hy_conv_b"]], 0).reshape(4, 12, 128).transpose(2, 1, 0)
    L["hyb"] = np.stack([I["hy_freq"][0], I["hy_b1"][0], I["hy_b2"][0]], 1)
    rp = np.zeros((8, 15, 127), f)
    rp[:, :, 48:79] = I["nat_rpb"][0]
    at = np.arange(64)[None, :] - np.arange(64)[:, None] + 63
    lo = rp[:, :, at].transpose(0, 2, 1, 3)
    x = np.zeros((8, 128, 15, 64), f)
    x[:, 0:64] = lo
    x[:, 64:128, 1:15] = lo[:, :, 0:14]
    L["rpx"] = x
    pe = I["cmp_pe_2"].reshape(2, 2, 2, 16, 64)
    L["peT"] = pe.transpose(0, 2, 4, 1, 3).reshape(2, 128, 2, 16)
    L["cmpw2"] = I["cmp_w2_2"].transpose(0, 2, 1, 3)
    L["mlag"] = np.concatenate([I["mla_q_norm_2"], I["mla_kv_norm_2"]], 1)
    L["t5"] = I["t5_table_2"]
    L["x"], L["ctx"], L["mem_2"] = I["x"][0], I["ctx"][0], I["mem_2"][0]
    L["hy_w1"], L["hy_w2"], L["hy_w3"], L["hy_skip"] = I["hy_w1"][0], I["hy_w2"][0], I["hy_w3"][0], I["hy_skip"][0]
    L["win_sink"] = I["win_sink"][0]
    for n in ("w_ada", "w_in", "w_out", "w_in_2", "cmp_w1_2", "mla_w_uq_2", "mla_w_ukv_2", "fox_b_f_2", "w_gate_2",
              "w_br_nsa_2", "w_br_mla_2", "w_br_fox_2", "w_mix_out_2", "xa_w_q_2", "xa_w_kv_2", "xa_w_o_2",
              "mlp_w_up_2", "mlp_w_down_2", "ln_g_2", "ln_b_2"):
        L[n] = I[n]
    return L


def kernel(**inputs):
    import concourse.bacc as bacc
    from concourse.bass_utils import run_bass_kernel_spmd

    I = {k: np.asarray(v) for k, v in inputs.items()}
    nc = bacc.Bacc("TRN2", target_bir_lowering=False, num_devices=1)
    arrays, D = {}, {}
    for name, a in {**layouts(I), **constants()}.items():
        a = np.ascontiguousarray(a)
        arrays["in_" + name] = a
        D[name] = nc.dram_tensor("in_" + name, a.shape, F32, kind="ExternalInput").ap()
    out = nc.dram_tensor("out_x", (512, 1024), F32, kind="ExternalOutput").ap()
    program(nc, D, out)
    r = run_bass_kernel_spmd(nc, [arrays], core_ids=[0])
    return r.results[0]["out_x"].reshape(1, 512, 1024)
```
